# Optimizing a Trainium2 kernel written in Bass

```python
import jax
import jax.numpy as jnp
from jax import lax
import numpy as np

D_MODEL = 1024
BATCH = 1
SEQ = 512
DEPTH = 2
DEC_BATCH = 8
DEC_SEQ = 1
PAST_LEN = 256
PAGE_SIZE = 128

HEAD_DIM = 64
H_HGRN = 5
HGRN_DK = 64
HGRN_DV = 64
H_MLSTM = 5
MLSTM_DK = 64
MLSTM_DV = 64
SWA_PAIRS = ((128, 1), (512, 4), (2048, 16))
N_SWA_GROUPS = 3
SWA_HEADS_PER_GROUP = 2
H_SWA = N_SWA_GROUPS * SWA_HEADS_PER_GROUP
SWA_BLOCK = 128
CHUNK = 64
CONV_W = 4
W_HG_K = H_HGRN * HGRN_DK
W_HG_V = H_HGRN * HGRN_DV
W_ML = H_MLSTM * MLSTM_DV
W_SW = H_SWA * HEAD_DIM
MIX_WIDTH = W_HG_V + W_ML + W_SW
IN_SPLITS = (W_HG_K, W_HG_K, W_HG_V, W_HG_V, W_ML, W_ML, W_ML, H_MLSTM, H_MLSTM, W_SW, W_SW, W_SW)
N_IN = 2 * W_HG_K + 2 * W_HG_V + 3 * W_ML + 2 * H_MLSTM + 3 * W_SW
D_FF = 2816
N_EXPERTS = 8
TOP_K = 2
EXPERT_FF = 1408
N_DENSE = (DEPTH + 1) // 2
N_MOE = DEPTH // 2
EPS = 1e-6
F32 = jnp.float32

kernel_name = 'hybrid_hgrn2_mlstm_dilated_swa_decode_step'

def rmsnorm(x, g):
    xf = x.astype(F32)
    y = xf * lax.rsqrt(jnp.mean(xf * xf, axis=-1, keepdims=True) + EPS)
    return (y * g.astype(F32)).astype(x.dtype)

def head_rmsnorm(x, g):
    B, T, H, Dh = x.shape
    y = x * lax.rsqrt(jnp.mean(x * x, axis=-1, keepdims=True) + EPS)
    return y.reshape(B, T, H * Dh) * g.astype(F32)

def chunk_scan(fn, init, xs):
    B, T = xs[0].shape[:2]
    n = T // CHUNK
    xs_c = tuple(a.reshape((B, n, CHUNK) + a.shape[2:]).swapaxes(0, 1) for a in xs)
    final, ys = lax.scan(lambda c, a: fn(c, *a), init, xs_c)
    ys = ys.swapaxes(0, 1)
    return final, ys.reshape((B, T) + ys.shape[3:])

def hgrn_chunk(S, q, k, v, logf):
    S = S.astype(F32)
    L = q.shape[1]
    b = jnp.cumsum(logf, axis=1)
    causal = jnp.tril(jnp.ones((L, L), dtype=bool))[None, :, :, None, None]
    decay = jnp.exp(jnp.where(causal, b[:, :, None] - b[:, None, :], -jnp.inf))
    attn = jnp.sum(decay * q[:, :, None] * k[:, None, :], axis=-1)
    o = jnp.einsum('btsh,bshv->bthv', attn, v) + jnp.einsum('bthk,bhkv->bthv', q * jnp.exp(b), S)
    b_last = b[:, -1]
    S_new = jnp.exp(b_last)[..., None] * S + jnp.einsum('bshk,bshv->bhkv', k * jnp.exp(b_last[:, None] - b), v)
    return S_new, o

def mlstm_chunk(state, q, k, v, ig, lf):
    C, n, m = (a.astype(F32) for a in state)
    L = q.shape[1]
    F = jnp.cumsum(lf, axis=1)
    causal = jnp.tril(jnp.ones((L, L), dtype=bool))[None, :, :, None]
    logD = jnp.where(causal, F[:, :, None] - F[:, None, :] + ig[:, None, :], -jnp.inf)
    log_inter = F + m[:, None]
    m_t = jnp.maximum(log_inter, jnp.max(logD, axis=2))
    Dw = jnp.exp(logD - m_t[:, :, None])
    a_inter = jnp.exp(log_inter - m_t)
    qk = jnp.einsum('bthk,bshk->btsh', q, k) * Dw
    num = jnp.einsum('btsh,bshv->bthv', qk, v) + a_inter[..., None] * jnp.einsum('bthk,bhkv->bthv', q, C)
    nq = jnp.sum(qk, axis=2) + a_inter * jnp.einsum('bthk,bhk->bth', q, n)
    h = num / jnp.maximum(jnp.abs(nq), jnp.exp(-m_t))[..., None]
    m_new = m_t[:, -1]
    w = jnp.exp(F[:, -1:] - F + ig - m_new[:, None])
    a_c = jnp.exp(F[:, -1] + m - m_new)
    kw = k * w[..., None]
    C_new = a_c[..., None, None] * C + jnp.einsum('bshk,bshv->bhkv', kw, v)
    n_new = a_c[..., None] * n + jnp.sum(kw, axis=1)
    return (C_new, n_new, m_new), h

def causal_conv(u, buf, w, bias):
    T = u.shape[1]
    padded = jnp.concatenate([buf.astype(u.dtype), u], axis=1)
    y = bias.astype(F32)
    for j in range(CONV_W):
        y = y + w[j].astype(F32) * padded[:, j:j + T].astype(F32)
    return y, padded[:, T:]

def swa_prompt(q, k, v, window, dil):
    B, S, Hg, Dh = q.shape
    Ls = S // dil
    J = window // dil
    nblk = -(-Ls // SWA_BLOCK)
    pad = nblk * SWA_BLOCK - Ls

    def to_blocks(a):
        a = a.reshape(B, Ls, dil, Hg, Dh).transpose(0, 2, 1, 3, 4).astype(F32)
        a = jnp.pad(a, ((0, 0), (0, 0), (0, pad), (0, 0), (0, 0)))
        return a.reshape(B, dil, nblk, SWA_BLOCK, Hg, Dh)

    def with_prev(a):
        prev = jnp.pad(a, ((0, 0), (0, 0), (1, 0), (0, 0), (0, 0), (0, 0)))[:, :, :-1]
        return jnp.concatenate([prev, a], axis=3)

    def from_blocks(a):
        a = a.reshape((B, dil, nblk * SWA_BLOCK) + a.shape[4:])[:, :, :Ls]
        a = jnp.moveaxis(a, 1, 2)
        return a.reshape((B, S) + a.shape[3:])

    qb = to_blocks(q)
    kk = with_prev(to_blocks(k))
    vv = with_prev(to_blocks(v))
    s = jnp.einsum('brnqhd,brnkhd->brnhqk', qb, kk) * (Dh ** -0.5)
    qi = jnp.arange(SWA_BLOCK)[:, None]
    kj = jnp.arange(2 * SWA_BLOCK)[None, :]
    dist = qi + SWA_BLOCK - kj
    blk = jnp.arange(nblk)[:, None, None]
    mask = (dist >= 0) & (dist <= J) & (blk * SWA_BLOCK + kj - SWA_BLOCK >= 0)
    s = jnp.where(mask[None, None, :, None], s, -jnp.inf)
    mx = jnp.max(s, axis=-1, keepdims=True)
    p = jnp.exp(s - mx)
    den = jnp.sum(p, axis=-1)
    o = jnp.einsum('brnhqk,brnkhd->brnqhd', p, vv) / den.swapaxes(-1, -2)[..., None]
    lse = (mx[..., 0] + jnp.log(den)).swapaxes(-1, -2)
    return from_blocks(o), from_blocks(lse)

def swa_sample(q, k, v, buf, window, dil):
    N, T, Hg, Dh = q.shape
    Wb = buf.shape[1]
    J = window // dil
    kk = jnp.concatenate([buf[:, :, 0].astype(F32), k.astype(F32)], axis=1)
    vv = jnp.concatenate([buf[:, :, 1].astype(F32), v.astype(F32)], axis=1)
    idx = Wb + jnp.arange(T)[:, None] - dil * jnp.arange(J + 1)[None, :]
    valid = idx >= 0
    idx = jnp.maximum(idx, 0)
    kg = kk[:, idx]
    vg = vv[:, idx]
    s = jnp.einsum('nthd,ntjhd->nthj', q.astype(F32), kg) * (Dh ** -0.5)
    s = jnp.where(valid[None, :, None, :], s, -jnp.inf)
    mx = jnp.max(s, axis=-1, keepdims=True)
    p = jnp.exp(s - mx)
    den = jnp.sum(p, axis=-1)
    o = jnp.einsum('nthj,ntjhd->nthd', p, vg) / den[..., None]
    lse = mx[..., 0] + jnp.log(den)
    new_buf = jnp.concatenate([buf, jnp.stack([k, v], axis=2).astype(buf.dtype)], axis=1)[:, T:]
    return o, lse, new_buf

def mixer(h, lp, st):
    B, T, _ = h.shape
    proj = h @ lp['w_in']
    (hq, hf, hi, hg, mu, mv, mo, mig, mfg, sq, sk, sv) = jnp.split(
        proj, np.cumsum(IN_SPLITS)[:-1].tolist(), axis=-1)

    lb = lp['lb']
    z = hf.astype(F32)
    logf_h = jnp.logaddexp(jnp.log(lb), jnp.log1p(-lb) + jax.nn.log_sigmoid(z))
    k_h = (1.0 - lb) * jax.nn.sigmoid(-z)
    q_h = jax.nn.silu(hq.astype(F32))
    shp_k = (B, T, H_HGRN, HGRN_DK)
    args_h = (q_h.reshape(shp_k), k_h.reshape(shp_k),
              hi.astype(F32).reshape(B, T, H_HGRN, HGRN_DV), logf_h.reshape(shp_k))
    if st is None:
        S_h, o_h = chunk_scan(hgrn_chunk, jnp.zeros((B, H_HGRN, HGRN_DK, HGRN_DV), F32), args_h)
    else:
        S_h, o_h = hgrn_chunk(st['hgrn'], *args_h)
    out_h = head_rmsnorm(o_h, lp['hgrn_g']) * jax.nn.silu(hg.astype(F32))

    buf = jnp.zeros((B, CONV_W - 1, W_ML), mu.dtype) if st is None else st['conv']
    cu, conv_new = causal_conv(mu, buf, lp['conv_w'], lp['conv_b'])
    c = jax.nn.silu(cu).reshape(B, T, H_MLSTM, MLSTM_DV)
    q_m = jnp.einsum('bthc,hcd->bthd', c, lp['ml_wq'].astype(F32))
    k_m = jnp.einsum('bthc,hcd->bthd', c, lp['ml_wk'].astype(F32)) * (MLSTM_DK ** -0.5)
    v_m = mv.astype(F32).reshape(B, T, H_MLSTM, MLSTM_DV)
    ig = mig.astype(F32) + lp['ig_b'].astype(F32)
    lf = jax.nn.log_sigmoid(mfg.astype(F32) + lp['fg_b'].astype(F32))
    if st is None:
        init = (jnp.zeros((B, H_MLSTM, MLSTM_DK, MLSTM_DV), F32),
                jnp.zeros((B, H_MLSTM, MLSTM_DK), F32), jnp.zeros((B, H_MLSTM), F32))
        (C_m, n_m, m_m), o_m = chunk_scan(mlstm_chunk, init, (q_m, k_m, v_m, ig, lf))
    else:
        (C_m, n_m, m_m), o_m = mlstm_chunk((st['C'], st['n'], st['m']), q_m, k_m, v_m, ig, lf)
    out_m = head_rmsnorm(o_m, lp['ml_g']) * jax.nn.sigmoid(mo.astype(F32))

    q_s = sq.reshape(B, T, H_SWA, HEAD_DIM)
    k_s = sk.reshape(B, T, H_SWA, HEAD_DIM)
    v_s = sv.reshape(B, T, H_SWA, HEAD_DIM)
    outs, lses, bufs = [], [], []
    for g, (win, dil) in enumerate(SWA_PAIRS):
        hs = slice(g * SWA_HEADS_PER_GROUP, (g + 1) * SWA_HEADS_PER_GROUP)
        if st is None:
            o, lse = swa_prompt(q_s[:, :, hs], k_s[:, :, hs], v_s[:, :, hs], win, dil)
            keep = min(win, T)
            nb = jnp.stack([k_s[:, T - keep:, hs], v_s[:, T - keep:, hs]], axis=2)
        else:
            o, lse, nb = swa_sample(q_s[:, :, hs], k_s[:, :, hs], v_s[:, :, hs], st['swa'][g], win, dil)
        outs.append(o)
        lses.append(lse)
        bufs.append(nb)
    alpha = jax.nn.softmax(jnp.stack(lses, axis=2), axis=2)
    out_s = (jnp.stack(outs, axis=2) * alpha[..., None]).reshape(B, T, W_SW)

    mix = jnp.concatenate([out_h, out_m, out_s], axis=-1).astype(h.dtype)
    new_st = {'hgrn': S_h, 'C': C_m, 'n': n_m, 'm': m_m, 'conv': conv_new, 'swa': bufs}
    return mix, new_st

def swiglu(x, wg, wu, wd):
    return (jax.nn.silu(x @ wg) * (x @ wu)) @ wd

def moe_ffn(x, router_w, router_b, wg, wu, wd):
    B, T, D = x.shape
    xf = x.reshape(B * T, D)
    logits = (xf @ router_w).astype(F32) + router_b.astype(F32)
    top_v, top_i = lax.top_k(logits, TOP_K)
    w_k = jax.nn.softmax(top_v, axis=-1)
    gates = jnp.sum(jax.nn.one_hot(top_i, N_EXPERTS, dtype=F32) * w_k[..., None], axis=1)
    y = jnp.zeros((B * T, D), F32)
    for e in range(N_EXPERTS):
        y = y + gates[:, e:e + 1] * swiglu(xf, wg[e], wu[e], wd[e]).astype(F32)
    return y.astype(x.dtype).reshape(B, T, D)

def block(x, lp, st, ffn_fn, ffn_p):
    mix, new_st = mixer(rmsnorm(x, lp['n1']), lp, st)
    x = x + mix @ lp['w_out']
    x = x + ffn_fn(rmsnorm(x, lp['n2']), *ffn_p)
    return x, new_st

def setup_inputs(seed: int = 0) -> dict:
    key = jax.random.key(seed)
    keys = iter(jax.random.split(key, 48))

    def nrm(shape, scale):
        return scale * jax.random.normal(next(keys), shape, F32)

    win = [min(w, PAST_LEN) for w, _ in SWA_PAIRS]
    return {
        'x_prompt': nrm((BATCH, SEQ, D_MODEL), 1.0),
        'x_sample': nrm((DEC_BATCH, DEC_SEQ, D_MODEL), 1.0),
        'state_hgrn': nrm((DEPTH, DEC_BATCH, H_HGRN, HGRN_DK, HGRN_DV), 0.3),
        'state_mlstm_C': nrm((DEPTH, DEC_BATCH, H_MLSTM, MLSTM_DK, MLSTM_DV), 0.3),
        'state_mlstm_n': nrm((DEPTH, DEC_BATCH, H_MLSTM, MLSTM_DK), 0.3),
        'state_mlstm_m': nrm((DEPTH, DEC_BATCH, H_MLSTM), 1.0),
        'state_mlstm_conv': nrm((DEPTH, DEC_BATCH, CONV_W - 1, W_ML), 1.0),
        'cache_swa_w128': nrm((DEPTH, DEC_BATCH, win[0], 2, SWA_HEADS_PER_GROUP, HEAD_DIM), 1.0),
        'cache_swa_w512': nrm((DEPTH, DEC_BATCH, win[1], 2, SWA_HEADS_PER_GROUP, HEAD_DIM), 1.0),
        'cache_swa_w2048': nrm((DEPTH, DEC_BATCH, win[2], 2, SWA_HEADS_PER_GROUP, HEAD_DIM), 1.0),
        'norm1_g': 1.0 + nrm((DEPTH, D_MODEL), 0.1),
        'norm2_g': 1.0 + nrm((DEPTH, D_MODEL), 0.1),
        'final_norm_g': 1.0 + nrm((D_MODEL,), 0.1),
        'w_in': nrm((DEPTH, D_MODEL, N_IN), D_MODEL ** -0.5),
        'w_out': nrm((DEPTH, MIX_WIDTH, D_MODEL), MIX_WIDTH ** -0.5),
        'hgrn_lb_param': nrm((DEPTH, W_HG_K), 0.5),
        'hgrn_onorm_g': 1.0 + nrm((DEPTH, W_HG_V), 0.1),
        'mlstm_conv_w': nrm((DEPTH, CONV_W, W_ML), CONV_W ** -0.5),
        'mlstm_conv_b': nrm((DEPTH, W_ML), 0.01),
        'mlstm_wq': nrm((DEPTH, H_MLSTM, MLSTM_DV, MLSTM_DK), MLSTM_DV ** -0.5),
        'mlstm_wk': nrm((DEPTH, H_MLSTM, MLSTM_DV, MLSTM_DK), MLSTM_DV ** -0.5),
        'mlstm_ig_b': nrm((DEPTH, H_MLSTM), 0.1),
        'mlstm_fg_b': jnp.linspace(3.0, 6.0, H_MLSTM, dtype=F32)[None] + nrm((DEPTH, H_MLSTM), 0.1),
        'mlstm_onorm_g': 1.0 + nrm((DEPTH, W_ML), 0.1),
        'ffn_w_gate': nrm((N_DENSE, D_MODEL, D_FF), D_MODEL ** -0.5),
        'ffn_w_up': nrm((N_DENSE, D_MODEL, D_FF), D_MODEL ** -0.5),
        'ffn_w_down': nrm((N_DENSE, D_FF, D_MODEL), D_FF ** -0.5),
        'moe_router_w': nrm((N_MOE, D_MODEL, N_EXPERTS), D_MODEL ** -0.5),
        'moe_router_b': nrm((N_MOE, N_EXPERTS), 0.01),
        'moe_w_gate': nrm((N_MOE, N_EXPERTS, D_MODEL, EXPERT_FF), D_MODEL ** -0.5),
        'moe_w_up': nrm((N_MOE, N_EXPERTS, D_MODEL, EXPERT_FF), D_MODEL ** -0.5),
        'moe_w_down': nrm((N_MOE, N_EXPERTS, EXPERT_FF, D_MODEL), EXPERT_FF ** -0.5),
    }

def reference(x_prompt, x_sample, state_hgrn, state_mlstm_C, state_mlstm_n, state_mlstm_m,
              state_mlstm_conv, cache_swa_w128, cache_swa_w512, cache_swa_w2048,
              norm1_g, norm2_g, final_norm_g, w_in, w_out, hgrn_lb_param, hgrn_onorm_g,
              mlstm_conv_w, mlstm_conv_b, mlstm_wq, mlstm_wk, mlstm_ig_b, mlstm_fg_b, mlstm_onorm_g,
              ffn_w_gate, ffn_w_up, ffn_w_down, moe_router_w, moe_router_b,
              moe_w_gate, moe_w_up, moe_w_down):
    p_lb = jax.nn.softmax(hgrn_lb_param.astype(F32), axis=0)
    cs = jnp.cumsum(p_lb, axis=0)
    lb_all = cs - cs[0:1]

    xp, xs = x_prompt, x_sample
    sp_list, ss_list = [], []
    for li in range(DEPTH):
        lp = {'n1': norm1_g[li], 'n2': norm2_g[li], 'w_in': w_in[li], 'w_out': w_out[li],
              'lb': lb_all[li], 'hgrn_g': hgrn_onorm_g[li], 'conv_w': mlstm_conv_w[li],
              'conv_b': mlstm_conv_b[li], 'ml_wq': mlstm_wq[li], 'ml_wk': mlstm_wk[li],
              'ig_b': mlstm_ig_b[li], 'fg_b': mlstm_fg_b[li], 'ml_g': mlstm_onorm_g[li]}
        j = li // 2
        if li % 2 == 0:
            ffn_fn, ffn_p = swiglu, (ffn_w_gate[j], ffn_w_up[j], ffn_w_down[j])
        else:
            ffn_fn, ffn_p = moe_ffn, (moe_router_w[j], moe_router_b[j], moe_w_gate[j], moe_w_up[j], moe_w_down[j])
        st = {'hgrn': state_hgrn[li], 'C': state_mlstm_C[li], 'n': state_mlstm_n[li],
              'm': state_mlstm_m[li], 'conv': state_mlstm_conv[li],
              'swa': [cache_swa_w128[li], cache_swa_w512[li], cache_swa_w2048[li]]}
        xp, sp = block(xp, lp, None, ffn_fn, ffn_p)
        xs, ss = block(xs, lp, st, ffn_fn, ffn_p)
        sp_list.append(sp)
        ss_list.append(ss)

    y_prompt = rmsnorm(xp, final_norm_g)
    y_sample = rmsnorm(xs, final_norm_g)

    def stk(lst, name):
        return jnp.stack([s[name] for s in lst], axis=0)

    def stk_swa(lst, g):
        return jnp.stack([s['swa'][g] for s in lst], axis=0)

    return (y_prompt, y_sample,
            stk(sp_list, 'hgrn'), stk(ss_list, 'hgrn'),
            stk(sp_list, 'C'), stk(ss_list, 'C'),
            stk(sp_list, 'n'), stk(ss_list, 'n'),
            stk(sp_list, 'm'), stk(ss_list, 'm'),
            stk(sp_list, 'conv'), stk(ss_list, 'conv'),
            stk_swa(sp_list, 0), stk_swa(ss_list, 0),
            stk_swa(sp_list, 1), stk_swa(ss_list, 1),
            stk_swa(sp_list, 2), stk_swa(ss_list, 2))


_drawn_inputs = setup_inputs


def setup_inputs(seed=0):
    import zlib

    import numpy as np

    out = dict(_drawn_inputs(seed))
    spreads = {}
    factors = {}
    for name, (base, spread) in spreads.items():
        noise = np.random.default_rng([zlib.crc32(name.encode()), seed]).standard_normal(out[name].shape)
        drawn = base * np.exp(spread * noise) if base else spread * noise
        out[name] = jnp.asarray(drawn.astype(out[name].dtype))
    for name, factor in factors.items():
        out[name] = (out[name] * factor).astype(out[name].dtype)
    return out
```

```python
from contextlib import ExitStack

import concourse.bass as bass
from concourse import mybir

F32 = mybir.dt.float32
F32R = mybir.dt.float32r
I32 = mybir.dt.int32
ALU = mybir.AluOpType
ACT = mybir.ActivationFunctionType
AX = mybir.AxisListType.X

P = 128
SEQ = 512
NB = 8
T = SEQ + NB
H2 = T // 2
D = 1024
KD = D // P
CH = 128
NC = SEQ // CH
NT = 27
EFF = 1408
KF = EFF // P
UPE = 2 * KF + KD
RAW = 3
SPL = 2
NPS = 3
LVL = 7
CONV = 4
WB = (128, 256, 256)
TOP_K = 2
EPS = 1e-6
NEG = -1e30
TQ, TF, TI, TG, TU, TV, TSQ, TSK, TSV = 0, 3, 6, 8, 13, 16, 18, 21, 24
MIXT = [8, 9, 10, 11, 12, 18, 19, 20]
ROWS_G = (128, 64, 16)
C_ID, C_ONE, C_NEGC, C_NEG0, C_NEG1, C_NEGR, C_NEGT, C_HP, C_DM, C_S2, C_RST, C_LT, C_EPS, C_END = \
    0, 128, 256, 384, 640, 896, 1024, 1152, 1536, 1664, 1792, 2304, 2368, 2369
PR_G1, PR_G2, PR_ON, PR_CW, PR_CB, PR_LB, PR_IB, PR_FB, PR_RB, PR_GF, PR_END = 0, 8, 16, 21, 33, 36, 39, 40, 41, 42, 50


def mixer_jobs():
    jobs = [("tm", i) for i in range(3)] + [("vt", g) for g in range(3)]

    def sc(n):
        return [("sc", n, p) for p in range(2 if n < 2 else 1)]

    def pt(n):
        return [("pt", n, p) for p in range(2 if n < 2 else 1)]

    jobs += sc(0) + sc(1)
    for n in range(6):
        jobs += pt(n)
        if n + 2 < 6:
            jobs += sc(n + 2)
        jobs += [("pv", n)]
        if n % 2:
            jobs += [("st", n // 2)]
    jobs += [("lt", g) for g in range(3)] + [("al", g) for g in range(3)]
    jobs += [("qb", g, p) for g in range(3) for p in range(2)] + [("sct", g) for g in range(3)]
    jobs += [("ppt",), ("spv",)]
    jobs += [("hv", c) for c in range(NC)] + [("th", i) for i in range(2)]
    for c in range(NC):
        jobs += [("kh", c), ("su", c)]
    jobs += [("at", h, l) for l in range(LVL + 1) for h in range(5)]
    for h in range(5):
        jobs += [("ho", h)]
        if h in (1, 3):
            jobs += [("mt", h // 2)]
    jobs += [("mv", c) for c in range(NC)]
    jobs += [("mq", f, s) for f in range(3) for s in range(4)]
    jobs += [("rt",), ("ac",)]
    for c in range(NC):
        jobs += [("kt", c), ("cu", c)]
    for h in range(5):
        jobs += [("md", h), ("mqk", h), ("mi", h), ("mo", h)]
        if h in (0, 2, 4):
            jobs += [("mt", 2 + h // 2)]
    jobs += [("vb", f) for f in range(3)] + [("so", 0), ("so", 1)]
    jobs += [("rs",), ("aw",)] + [("vc", f) for f in range(3)] + [("co", 0), ("co", 1)] + [("fx",)]
    return jobs


def program(nc, a):
    jobs = mixer_jobs()
    NJ = len(jobs)
    JOB = {k: n for n, k in enumerate(jobs)}
    uses = [len(range(b, NJ, 8)) for b in range(8)]
    U_IN = [0, NT + KD + 2 * UPE]
    U_OUT = [u + NT for u in U_IN]
    U_FF = [u + KD for u in U_OUT]
    NEX = [2, 8]
    X_OUT = [KD, 4 * KD]
    X_FF = [3 * KD, 12 * KD]
    G_FF = [0, 2 * KF]
    with ExitStack() as ctx:
        def sem(name):
            return ctx.enter_context(nc.semaphore(name))

        top = [16512]
        END = 229344

        def at(name, shape, dt=F32, off=None):
            n = 4
            for s in shape[1:]:
                n *= s
            n = (n + 31) // 32 * 32
            if off is None:
                off = top[0]
                top[0] += n
            assert off + n <= END, (name, off + n - END)
            return nc.alloc_sbuf_tensor_at(name, shape, dt, offset=off), off + n

        xT, _ = at("xT", [P, KD, T])
        xn_off = top[0]
        xnh, _ = at("xnh", [P, KD, T], F32R)
        xnl, _ = at("xnl", [P, KD, T], F32R)
        xn_end = top[0]
        wraw = [at(f"wraw{n}", [P, KF * P])[0] for n in range(RAW)]
        whi = [at(f"whi{n}", [P, KF * P], F32R)[0] for n in range(SPL)]
        wlo = [at(f"wlo{n}", [P, KF * P], F32R)[0] for n in range(SPL)]
        cst, _ = at("cst", [P, C_END])
        lvm, _ = at("lvm", [P, LVL + 1, P], I32)
        prm, _ = at("prm", [P, 2, PR_END])
        bd, _ = at("bd", [P, 2, 2, 3, P])
        cbuf, _ = at("cbuf", [P, 2, 3, CONV - 1, NB])
        lbt, _ = at("lbt", [P, 4, 3])
        rstd, _ = at("rstd", [P, T])
        osw, _ = at("osw", [NB, 3 * P])
        proj_off = top[0]
        proj, _ = at("proj", [P, NT, T])
        scr_off = top[0]

        o = proj_off
        hh, o = at("hh", [P, KF, T], F32R, o)
        hl, o = at("hl", [P, KF, T], F32R, o)
        sg, o = at("sg", [P, 2, T], F32, o)
        h32, o = at("h32", [P, 2, T], F32, o)
        assert o <= scr_off
        o = scr_off
        sqb, o = at("sqb", [P, 2, T], F32, o)
        n32, o = at("n32", [P, 2, T], F32, o)
        ytmp, o = at("ytmp", [P, 2, T], F32, o)
        gb, o = at("gb", [P, 8, T], F32, o)
        rw, o = at("rw", [P, KD * 8], F32, o)
        rwh, o = at("rwh", [P, KD * 8], F32R, o)
        rwl, o = at("rwl", [P, KD * 8], F32R, o)
        lg, o = at("lg", [8, T], F32, o)
        rl, o = at("rl", [P, 5, 8], F32, o)
        re, o = at("re", [P, 5, 8], F32, o)
        rk, o = at("rk", [P, 40], F32, o)
        rm, o = at("rm", [P, 5], F32, o)
        c1, o = at("c1", [P, 40, 8], F32, o)
        c2, o = at("c2", [P, 40, 8], F32, o)
        gT, o = at("gT", [8, T], F32, o)
        yout = at("yout", [P, KD, T], F32, proj_off)[0]

        A = {}
        o = scr_off
        for name, shape in (("vt", [P, 3, 4, P]), ("pb", [P, 2, 1024]), ("ptb", [P, 2, 1024]), ("os", [P, 2, 4, P]),
                            ("mx", [P, 6, 4]), ("nm", [P, 6, 4]), ("den", [P, 6, 4]), ("rd", [P, 6, 4]),
                            ("lse", [P, 6, 4]), ("lr", [2, 3, SEQ]), ("lm", [2, SEQ]), ("tms", [NB, 9 * P]),
                            ("scr", [P, 3, 2, NB]), ("smx", [NB, 6]), ("sden", [NB, 6]), ("slse", [NB, 6]),
                            ("sm2", [NB, 2])):
            if name == "pb":
                probs_off = o
            A[name], o = at("a_" + name, shape, F32, o)
        o = probs_off
        for name, shape in (("ss", [NB, 6, 129]), ("sp", [NB, 6, 129]), ("pm", [P, 6, NB, NB])):
            A[name], o = at("a_" + name, shape, F32, o)
        o = xn_off
        for name, shape in (("ck", [P, 3, NB, 256]), ("dq", [NB, NB, P]), ("pr", [P, 512]), ("own", [NB, 6, 64])):
            A[name], o = at("a_" + name, shape, F32, o)
        assert o <= xn_end

        R = {}
        o = xn_off
        for name in ("kh", "bt", "ee", "w0", "w1"):
            R[name], o = at("r_" + name, [P, 3, T], F32, o)
        assert o <= xn_end
        o = scr_off
        R["dw"], _ = at("r_dw", [P, 2, SEQ], F32, o)
        R["qd"], _ = at("r_qd", [P, 2, SEQ], F32, o + 2 * SEQ * 4)
        o2 = o
        for name, shape in (("obs", [NB, 10, 64]), ("sq8", [NB, 10, 64]), ("n8", [NB, 5, 65])):
            R[name], o2 = at("r_" + name, shape, F32, o2)
        for name, shape in (("att", [P, 5, SEQ]), ("vh", [P, NC, 384]), ("kt", [P, 2, 384]),
                            ("sall", [P, NC + 1, 3, 64]), ("rows", [P, SEQ]), ("dl", [P, 3, NC]),
                            ("call", [P, NC + 1, 3, 65]),
                            ("num", [P, NC, 65]), ("t1", [P, NC, 65]), ("ec", [P, 3, NC, 5]), ("acb", [P, NC, 3]),
                            ("ob", [P, 2, NC, P]), ("sqo", [P, NC, P]), ("ss2", [P, 8]), ("rden", [P, NC]),
                            ("thm", [NB, 6 * P]), ("ff", [P, 3, NB]), ("k8", [P, 3, NB]), ("qm8", [P, 3, NB, NB]),
                            ("aw", [P, 3, 2 * NB]), ("sc8", [NB, 48]), ("s10", [NB, 10]),
                            ("e8", [NB, 5]), ("d8", [NB, 5]),
                            ("fx", [P, 5, NB])):
            if name == "vh":
                R["va"], _ = at("r_va", [P, NC, 5, 65], F32, o)
            if name == "kt":
                R["kw"], _ = at("r_kw", [P, 2, 6, 64], F32, o)
            R[name], o = at("r_" + name, shape, F32, o)

        psum = ctx.enter_context(nc.psum_tensor("psum", [P, 8, 512], F32))

        const_in, x_in = sem("const_in"), sem("x_in")
        raw_in = [sem(f"raw_in{n}") for n in range(RAW)]
        hi_made, lo_made, unit_done = sem("hi_made"), sem("lo_made"), sem("unit_done")
        proj_read, x_updated, gate_read, up_read = sem("proj_read"), sem("x_updated"), sem("gate_read"), sem("up_read")
        hh_made, hl_made, y_scaled = sem("hh_made"), sem("hl_made"), sem("y_scaled")
        sq_made, sq_used, rstd_made = sem("sq_made"), sem("sq_used"), sem("rstd_made")
        n32_made, nh_made, nl_made = sem("n32_made"), sem("nh_made"), sem("nl_made")
        job_done = sem("job_done")
        bank_read = [sem(f"bank_read{b}") for b in range(8)]
        mixh_made, mixl_made = sem("mixh_made"), sem("mixl_made")
        dve_step, act_step, pool_step = sem("dve_step"), sem("act_step"), sem("pool_step")
        cache_in, state_in, out_dma, shift_dma, window_dma = (
            sem(n) for n in ("cache_in", "state_in", "out_dma", "shift_dma", "window_dma"))
        rw_in, rw_hi, rw_lo, rt_done, rt_read, y_made = (
            sem(n) for n in ("rw_in", "rw_hi", "rw_lo", "rt_done", "rt_read", "y_made"))
        named = {}

        def S(name):
            if name not in named:
                named[name] = sem(name)
            return named[name]

        counts = {}

        def bump(ins, s, eng):
            counts[s.name] = counts.get(s.name, 0) + 1
            ins.then_inc(s, 1)
            eng.wait_ge(s, counts[s.name])

        def K(c0, n, rows=P, r0=0):
            return cst[r0:r0 + rows, c0:c0 + n]

        ident = K(C_ID, P)

        def par(li, c, n=1, rows=P, r0=0):
            return prm[r0:r0 + rows, li, c:c + n]

        def bc(ap, *shape):
            return ap.broadcast_to(list(shape))

        def flat(tile0, cols):
            return proj[:, tile0:tile0 + 3, :].rearrange("p f t -> p (f t)")[:, 0:cols]

        def perm(g, tile, i, r0=0, rows=P):
            v = proj[r0:r0 + rows, tile, 0:SEQ]
            if g == 0:
                return v[:, i * P:(i + 1) * P]
            return v.rearrange("p (j r) -> p r j", r=4)[:, i, :]

        def natural(g, ap):
            return ap if g == 0 else ap.rearrange("p (j r) -> p r j", r=4)

        def grouped(g, ap):
            return ap if g == 0 else ap.rearrange("p (r j) -> p r j", r=4)

        def bank(*key):
            return psum[:, JOB[key] % 8, :]

        def made(eng, li, *key):
            eng.wait_ge(job_done, li * NJ + JOB[key] + 1)

        def taken(eng, li, *key):
            j = JOB[key]
            eng.wait_ge(bank_read[j % 8], li * uses[j % 8] + j // 8 + 1)

        def release(eng, ins, li, *key):
            ins.then_inc(bank_read[JOB[key] % 8], 1)
            taken(eng, li, *key)

        def v_col(h):
            return h * 64 if h < 4 else 320

        def part(u):
            s = 2 * (u % NPS)
            return psum[:, s:s + 2, 0:H2]

        def halves(ap):
            return ap.rearrange("p (s t) -> p s t", s=2)

        block = ctx.enter_context(nc.Block())

        @block.sync
        def _(sp):
            def load(u, src, cols, when=None):
                if when is not None or u >= RAW:
                    sp.wait_ge(lo_made, (u if when is None else when) - RAW + 1)
                sp.dma_start(wraw[u % RAW][:, 0:cols], src).then_inc(raw_in[u % RAW], 16)

            sp.dma_start(xT[:], a["x"]).then_inc(x_in, 16)
            for name, dst in (("cst", cst), ("lvm", lvm), ("prm", prm), ("bd", bd), ("cbuf", cbuf)):
                sp.dma_start(dst[:], a[name]).then_inc(const_in, 16)
            for li in range(2):
                for n in range(RAW):
                    load(U_IN[li] + n, a["w_in"][li, n], KD * P)
                with sp.Fori(0, (NT - RAW) // RAW) as i:
                    for n in range(RAW):
                        u = U_IN[li] + RAW + n
                        src = a["w_in"][li, bass.ds(i * RAW + (RAW + n), 1)].rearrange("o p c -> (o p) c")
                        load(u, src, KD * P, i * RAW + u)
                for n in range(KD):
                    load(U_OUT[li] + n, a["w_out"][li, n], KD * P)
                gu, dn = ("ffn_gu", "ffn_dn") if li == 0 else ("moe_gu", "moe_dn")
                with sp.Fori(0, NEX[li]) as e:
                    for n in range(UPE):
                        u = U_FF[li] + n
                        if n < 2 * KF:
                            src, cols = a[gu][bass.ds(e, 1), n].rearrange("o p c -> (o p) c"), KD * P
                        else:
                            src, cols = a[dn][bass.ds(e, 1), n - 2 * KF].rearrange("o p c -> (o p) c"), KF * P
                        load(u, src, cols, e * UPE + u)
            sp.wait_ge(y_made, KD)
            sp.dma_start(a["y"], yout[:]).then_inc(out_dma, 16)
            sp.wait_ge(out_dma, 16)

        @block.gpsimd
        def _(pool):
            def lo(u, cols, when=None):
                pool.wait_ge(hi_made, (u if when is None else when) + 1)
                pool.tensor_tensor(wlo[u % SPL][:, 0:cols], wraw[u % RAW][:, 0:cols],
                                   whi[u % SPL][:, 0:cols].bitcast(F32), ALU.subtract).then_inc(lo_made, 1)

            def norm_lo(r):
                for k in range(KD):
                    pool.wait_ge(nh_made, KD * r + k + 1)
                    pool.tensor_tensor(xnl[:, k, :], n32[:, k % 2, :], xnh[:, k, :].bitcast(F32),
                                       ALU.subtract).then_inc(nl_made, 1)

            def step(ins):
                bump(ins, pool_step, pool)

            for li in range(2):
                norm_lo(2 * li)
                for n in range(3):
                    lo(U_IN[li] + n, KD * P)
                with pool.Fori(0, (NT - 3) // 6) as i:
                    for n in range(6):
                        lo(U_IN[li] + 3 + n, KD * P, i * 6 + (U_IN[li] + 3 + n))
                pool.wait_ge(S("window_end"), li + 1)
                step(pool.memset(R["att"][:], 0.0))
                step(pool.memset(R["rows"][:], 0.0))
                step(pool.memset(R["sall"][:, 0, :, :], 0.0))
                step(pool.memset(R["call"][:, 0, :, :], 0.0))
                bump(pool.memset(R["acb"][:], 0.0), S("scratch_clear"), pool)
                for m in range(KD):
                    pool.wait_ge(mixh_made, KD * li + m + 1)
                    pool.tensor_tensor(xnl[:, m, :], proj[:, MIXT[m], :], xnh[:, m, :].bitcast(F32),
                                       ALU.subtract).then_inc(mixl_made, 1)
                for n in range(KD):
                    lo(U_OUT[li] + n, KD * P)
                norm_lo(2 * li + 1)
                if li == 1:
                    pool.wait_ge(rw_hi, 1)
                    pool.tensor_tensor(rwl[:], rw[:], rwh[:].bitcast(F32), ALU.subtract).then_inc(rw_lo, 1)
                with pool.Fori(0, NEX[li]) as e:
                    for n in range(UPE):
                        lo(U_FF[li] + n, (KD if n < 2 * KF else KF) * P, e * UPE + (U_FF[li] + n))

        @block.scalar
        def _(act):
            def step(ins):
                bump(ins, act_step, act)

            def sig(ins, name):
                bump(ins, S(name), act)

            def free(ins, li, *key):
                release(act, ins, li, *key)

            def hi(u, cols, when=None):
                slot = u % RAW
                if when is None:
                    act.wait_ge(raw_in[slot], 16 * (u // RAW + 1))
                    if u >= SPL:
                        act.wait_ge(unit_done, u - SPL + 1)
                else:
                    i, per = when
                    act.wait_ge(raw_in[slot], i * (16 * per // RAW) + 16 * (u // RAW + 1))
                    act.wait_ge(unit_done, i * per + (u - SPL + 1))
                act.copy(whi[u % SPL][:, 0:cols], wraw[slot][:, 0:cols]).then_inc(hi_made, 1)

            def norm(r):
                for k in range(KD):
                    if r == 0:
                        act.wait_ge(x_in, 16)
                    else:
                        act.wait_ge(x_updated, [0, X_OUT[0], X_FF[0], X_OUT[1], X_FF[1]][r] - KD + k + 1)
                    if KD * r + k >= 2:
                        act.wait_ge(sq_used, KD * r + k - 1)
                    act.activation(sqb[:, k % 2, :], xT[:, k, :], ACT.Square).then_inc(sq_made, 1)
                act.wait_ge(const_in, 80)
                act.wait_ge(sq_used, KD * (r + 1))
                step(act.activation(halves(rstd[:]), psum[:, 6:8, 0:H2], ACT.Ln, scale=1.0 / D, bias=K(C_EPS, 1)))
                bump(act.activation(rstd[:], rstd[:], ACT.Exp, scale=-0.5), rstd_made, act)
                if r < 4:
                    for k in range(KD):
                        act.wait_ge(n32_made, KD * r + k + 1)
                        act.copy(xnh[:, k, :], n32[:, k % 2, :]).then_inc(nh_made, 1)

            def window(li):
                for g in range(3):
                    made(act, li, "vt", g)
                    free(act.copy(A["vt"][:, g, :, :].rearrange("p i c -> p (i c)"), bank("vt", g)), li, "vt", g)
                taken(act, li, "tm", 2)
                for g, w in enumerate(WB):
                    act.dma_start(a[f"cache{g}_s"][li, :, w - 1, :, :],
                                  A["tms"][:, 3 * P:9 * P].rearrange("b (v g d) -> b v g d", v=2, g=3)[:, :, g, :]
                                  ).then_inc(window_dma, 16)
                act.dma_start(a["kv_p"][li], proj[:, TSK:TSK + 6, 0:SEQ]).then_inc(window_dma, 16)
                act.dma_start(a["mu_out"][li], proj[:, TU:TU + 3, SEQ - 3:SEQ]).then_inc(window_dma, 16)
                act.dma_start(a["conv_s"][li, :, :, 0:2, :], cbuf[:, li, :, 1:3, :]).then_inc(window_dma, 16)
                act.dma_start(a["conv_s"][li, :, :, 2, :], proj[:, TU:TU + 3, SEQ:T]).then_inc(window_dma, 16)

                def expo(n):
                    act.wait_ge(S("max_made"), 6 * li + n + 1)
                    if n >= 2:
                        made(act, li, "pt", n - 2, 1 if n - 2 < 2 else 0)
                    w = 256 if n < 2 else P
                    for i in range(4):
                        key = ("sc", n, i // 2 if n < 2 else 0)
                        c = (i % 2) * 256 if n < 2 else i * P
                        ins = act.activation(A["pb"][:, n % 2, i * w:(i + 1) * w], bank(*key)[:, c:c + w], ACT.Exp,
                                             scale=0.125, bias=A["nm"][:, n, i:i + 1],
                                             accum_out=A["den"][:, n, i:i + 1])
                        if (n < 2 and i % 2 == 1) or i == 3:
                            free(ins, li, *key)
                        else:
                            step(ins)

                def turned(n):
                    for q in range(2 if n < 2 else 1):
                        cols = (3 if q else 4) * P
                        made(act, li, "pt", n, q)
                        if n >= 2:
                            made(act, li, "pv", n - 2)
                        free(act.copy(A["ptb"][:, n % 2, q * 512:q * 512 + cols], bank("pt", n, q)[:, 0:cols]),
                             li, "pt", n, q)

                expo(0)
                expo(1)
                for n in range(6):
                    turned(n)
                    if n + 2 < 6:
                        expo(n + 2)
                sig(act.activation(A["lse"][:], A["den"][:], ACT.Ln), "den_ln")
                act.wait_ge(S("lse_centred"), li + 1)
                sig(act.activation(A["lr"][:], A["lr"][:], ACT.Exp), "lse_exp")
                act.wait_ge(S("s_centred"), li + 1)
                sig(act.activation(A["sp"][:], A["sp"][:], ACT.Exp, scale=0.125), "s_exp")
                act.wait_ge(S("s_den"), li + 1)
                sig(act.activation(A["slse"][:], A["sden"][:], ACT.Ln), "s_den_ln")
                act.wait_ge(S("s_lse_centred"), li + 1)
                sig(act.activation(A["slse"][:], A["slse"][:], ACT.Exp), "s_lse_exp")

            def head_rms(li, n):
                act.wait_ge(S("ob_ms"), 5 * li + n + 1)
                step(act.activation(R["ss2"][:], R["ss2"][:], ACT.Ln, scale=1.0 / 64, bias=K(C_EPS, 1)))
                sig(act.activation(R["ss2"][:], R["ss2"][:], ACT.Exp, scale=-0.5), "ob_rms")

            def hgrn(li):
                act.wait_ge(S("window_end"), li + 1)
                act.wait_ge(window_dma, 112 * (li + 1))
                act.dma_start(flat(TSK, 3 * NB * 64), a["hgrn_in"][li]).then_inc(state_in, 16)
                act.dma_start(flat(TSV, 3 * NB * 65), a["mlstm_in"][li]).then_inc(state_in, 16)
                act.dma_start(R["sc8"][0:5, 24:32], a["m_in"][li]).then_inc(state_in, 16)
                if li == 0:
                    for l2 in range(2):
                        for g, w in enumerate(WB):
                            act.dma_start(a[f"cache{g}_s"][l2, :, 0:w - 1, :, :], a[f"cache{g}"][l2, :, 1:w, :, :]
                                          ).then_inc(shift_dma, 16)
                step(act.activation(proj[:, TQ:TQ + 2, :], proj[:, TQ:TQ + 2, :], ACT.Silu))
                step(act.activation(proj[0:64, TQ + 2, :], proj[0:64, TQ + 2, :], ACT.Silu))
                step(act.activation(proj[:, TG:TG + 2, :], proj[:, TG:TG + 2, :], ACT.Silu))
                step(act.activation(proj[0:64, TG + 2, :], proj[0:64, TG + 2, :], ACT.Silu))
                step(act.activation(proj[64:P, TG + 2, :], proj[64:P, TG + 2, :], ACT.Sigmoid))
                sig(act.activation(proj[:, TG + 3:TG + 5, :], proj[:, TG + 3:TG + 5, :], ACT.Sigmoid), "gates_made")
                act.wait_ge(S("z_parts"), li + 1)
                step(act.activation(R["w0"][:], R["kh"][:], ACT.Exp))
                sig(act.activation(R["w1"][:], R["bt"][:], ACT.Exp, scale=-1.0), "z_exp")
                act.wait_ge(S("z_sums"), li + 1)
                if li:
                    step(act.activation(R["w0"][:], R["w0"][:], ACT.Ln))
                sig(act.activation(R["ee"][:], R["ee"][:], ACT.Ln), "z_ln")
                for c in range(NC):
                    made(act, li, "hv", c)
                    free(act.copy(R["vh"][:, c, :], bank("hv", c)[:, 0:384]), li, "hv", c)
                act.wait_ge(S("to_last"), li + 1)
                step(act.activation(R["dl"][:], R["dl"][:], ACT.Exp))
                sig(act.activation(R["ee"][:, :, 0:SEQ], R["ee"][:, :, 0:SEQ], ACT.Exp), "to_last_exp")
                act.wait_ge(S("k_last"), li + 1)
                sig(act.activation(R["ee"][:, :, 0:SEQ], R["bt"][:, :, 0:SEQ], ACT.Exp), "from_first_exp")
                for c in range(NC):
                    made(act, li, "kh", c)
                    if c >= 2:
                        made(act, li, "su", c - 2)
                    free(act.copy(R["kt"][:, c % 2, :], bank("kh", c)[:, 0:384]), li, "kh", c)
                for l in range(LVL):
                    act.wait_ge(S("lv_diff"), LVL * li + l + 1)
                    sig(act.activation(R["ee"][:, :, 0:SEQ], R["ee"][:, :, 0:SEQ], ACT.Exp), "lv_exp")
                for n in range(2):
                    head_rms(li, n)

            def mlstm(li):
                act.wait_ge(S("conv_made"), li + 1)
                sig(act.activation(R["w0"][:], R["w0"][:], ACT.Silu), "c_made")
                act.wait_ge(S("fg_abs"), li + 1)
                step(act.activation(proj[0:5, 7, :], proj[0:5, 7, :], ACT.Exp, scale=-1.0))
                sig(act.activation(proj[0:5, 7, :], proj[0:5, 7, :], ACT.Ln, bias=K(C_ONE, 1, 5)), "fg_ln")
                for c in range(NC):
                    made(act, li, "mv", c)
                    v = bank("mv", c)
                    step(act.copy(R["va"][:, c, 0:4, 0:64], v[:, 0:256].rearrange("p (h d) -> p h d", h=4)))
                    free(act.copy(R["va"][:, c, 4, 0:64], v[:, 320:384]), li, "mv", c)
                for f in range(3):
                    for s in range(4):
                        made(act, li, "mq", f, s)
                        dst = R["bt"] if s < 2 else R["kh"]
                        c = (s % 2) * H2
                        free(act.mul(dst[:, f, c:c + H2], bank("mq", f, s)[:, 0:H2], 1.0 if s < 2 else 0.125),
                             li, "mq", f, s)
                made(act, li, "rt")
                ps = bank("rt").rearrange("p (c q h) -> p q c h", c=NC, q=4)
                for q in range(2):
                    step(act.activation(R["ec"][:, q, :, :], ps[:, q, :, 0:5], ACT.Exp))
                free(act.activation(R["ec"][:, 2, :, :], ps[:, 2, :, 0:5], ACT.Exp), li, "rt")
                for h in range(5):
                    made(act, li, "md", h)
                    if h >= 2:
                        taken(act, li, "mqk", h - 2)
                    free(act.activation(R["dw"][:, h % 2, :], bank("md", h), ACT.Exp), li, "md", h)
                    if h % 2 == 0:
                        head_rms(li, 2 + h // 2)

            def sample(li):
                act.wait_ge(S("f8_copied"), li + 1)
                sig(act.activation(R["ff"][:], R["ff"][:], ACT.Exp), "f8_exp")
                act.wait_ge(S("m8_rows"), li + 1)
                sig(act.activation(R["sc8"][0:5, 0:24], R["sc8"][0:5, 0:24], ACT.Exp), "m8_exp")
                act.wait_ge(S("obs_ms"), li + 1)
                step(act.activation(R["s10"][:], R["s10"][:], ACT.Ln, scale=1.0 / 64, bias=K(C_EPS, 1, NB)))
                sig(act.activation(R["s10"][:], R["s10"][:], ACT.Exp, scale=-0.5), "obs_rms")
                taken(act, li, "fx")
                for name, src in (("hgrn_p", R["sall"][:, NC, :, :]), ("mlstm_p", R["call"][:, NC, :, :]),
                                  ("hgrn_s", flat(TSK, 3 * NB * 64)), ("mlstm_s", flat(TSV, 3 * NB * 65)),
                                  ("m_p", proj[0:5, 5, SEQ - 1:SEQ]), ("m_s", R["sc8"][0:5, 32:40])):
                    act.dma_start(a[name][li], src).then_inc(S("state_out"), 16)
                for m in range(KD):
                    act.copy(xnh[:, m, :], proj[:, MIXT[m], :]).then_inc(mixh_made, 1)
                act.wait_ge(S("state_out"), 96 * (li + 1))

            act.wait_ge(S("lb_centred"), 1)
            sig(act.activation(lbt[:, 0:2, :], lbt[:, 0:2, :], ACT.Exp), "lb_exp")
            for li in range(2):
                norm(2 * li)
                if li == 1:
                    act.wait_ge(x_updated, X_FF[0])
                for n in range(3):
                    hi(U_IN[li] + n, KD * P)
                with act.Fori(0, (NT - 3) // 6) as i:
                    for n in range(6):
                        hi(U_IN[li] + 3 + n, KD * P, (i, 6))
                act.wait_ge(unit_done, U_OUT[li])
                act.dma_start(A["ck"][:], a["ck"][li]).then_inc(cache_in, 16)
                window(li)
                hgrn(li)
                mlstm(li)
                sample(li)
                for n in range(KD):
                    hi(U_OUT[li] + n, KD * P)
                norm(2 * li + 1)
                if li == 1:
                    act.dma_start(rw[:], a["rw"]).then_inc(rw_in, 16)
                    act.wait_ge(rw_in, 16)
                    act.copy(rwh[:], rw[:]).then_inc(rw_hi, 1)
                    act.wait_ge(S("rt_centred"), 1)
                    sig(act.activation(re[:], re[:], ACT.Exp), "rt_exp")
                with act.Fori(0, NEX[li]) as e:
                    for n in range(UPE):
                        hi(U_FF[li] + n, (KD if n < 2 * KF else KF) * P, (e, UPE))
                        if n % 2 == 1 and n < 2 * KF:
                            j = n // 2
                            act.wait_ge(unit_done, e * UPE + (U_FF[li] + n))
                            if j >= 2:
                                act.wait_ge(up_read, e * KF + (G_FF[li] + j - 1))
                            act.activation(halves(sg[:, j % 2, :]), part(U_FF[li] + 2 * j), ACT.Silu
                                           ).then_inc(gate_read, 1)
                        if n >= 2 and n % 2 == 0 and n <= 2 * KF:
                            j = n // 2 - 1
                            act.wait_ge(up_read, e * KF + (G_FF[li] + j + 1))
                            act.copy(hh[:, j, :], h32[:, j % 2, :]).then_inc(hh_made, 1)
            norm(4)
            act.wait_ge(shift_dma, 96)

        @block.tensor
        def _(pe):
            def passes(u, out, kt, xh, xl, cols=P, wh=None, wl=None):
                wh = whi[u % SPL] if wh is None else wh
                wl = wlo[u % SPL] if wl is None else wl
                for k in range(kt):
                    for w, x, first, last in ((wh, xh, True, False), (wh, xl, False, False), (wl, xh, False, True)):
                        for s in range(2):
                            ins = pe.matmul(out[:, s, :], w[:, k * cols:(k + 1) * cols], x[:, k, s * H2:(s + 1) * H2],
                                            start=(k == 0 and first), stop=(k == kt - 1 and last))
                return ins

            def unit(u, kt, xh, xl, when=None):
                pe.wait_ge(lo_made, (u if when is None else when) + 1)
                passes(u, part(u), kt, xh, xl).then_inc(unit_done, 1)

            def norm(r):
                for k in range(KD):
                    pe.wait_ge(sq_made, KD * r + k + 1)
                    if r == 0 and k == 0:
                        pe.wait_ge(const_in, 80)
                    for s in range(2):
                        ins = pe.matmul(psum[:, 6 + s, 0:H2], K(C_ONE, P), sqb[:, k % 2, s * H2:(s + 1) * H2],
                                        start=(k == 0), stop=(k == KD - 1))
                    ins.then_inc(sq_used, 1)

            class Job:
                def __init__(self, li, *key):
                    j = JOB[key]
                    self.b = j % 8
                    if j >= 8:
                        pe.wait_ge(bank_read[self.b], li * uses[self.b] + j // 8)

                def out(self, c0, n, rows=P, r0=0):
                    return psum[r0:r0 + rows, self.b, c0:c0 + n]

                def end(self):
                    self.last.then_inc(job_done, 1)

                def mm(self, c0, n, lhsT, rhs, start=True, stop=True, rows=P, r0=0):
                    self.last = pe.matmul(self.out(c0, n, rows, r0), lhsT, rhs, start=start, stop=stop,
                                          skip_group_check=True)

                def tr(self, c0, n, in_, rows, k=P):
                    self.last = pe.transpose(self.out(c0, n, rows), in_, K(C_ID, k, k))

            def window(li):
                for i in range(3):
                    j = Job(li, "tm", i)
                    for t in range(4 * i, min(4 * i + 4, 9)):
                        j.tr((t % 4) * P, P, proj[:, TSQ + t, SEQ:T], NB)
                    j.end()
                for g in range(3):
                    j = Job(li, "vt", g)
                    for i in range(4):
                        j.tr(i * P, P, perm(g, TSV + g, i), P)
                    j.end()

                def scores(n):
                    g, r0 = n // 2, 64 * (n % 2)
                    for q in range(2 if g == 0 else 1):
                        j = Job(li, "sc", n, q)
                        for i in (range(2 * q, 2 * q + 2) if g == 0 else range(4)):
                            lhs = perm(g, TSQ + g, i, r0, 64)
                            if g == 0:
                                c = (i % 2) * 256
                                j.mm(c, 256, ident, K(C_NEG1 if i else C_NEG0, 256), stop=False)
                                if i:
                                    j.mm(c, 256, lhs, proj[r0:r0 + 64, TSK, (i - 1) * P:(i + 1) * P], start=False)
                                else:
                                    j.mm(c + P, P, lhs, proj[r0:r0 + 64, TSK, 0:P], start=False)
                            else:
                                j.mm(i * P, P, ident, K(C_NEGT if g == 1 else C_NEGR, P), stop=False)
                                j.mm(i * P, P, lhs, perm(g, TSK + g, i, r0, 64), start=False)
                        j.end()

                def blocks(n):
                    if n < 2:
                        return [(0, 0, 128)] + [(i, i - 1 + s, i * 256 + s * P) for i in range(1, 4) for s in range(2)]
                    return [(i, i, i * P) for i in range(4)]

                scores(0)
                scores(1)
                for n in range(6):
                    g, bl = n // 2, blocks(n)
                    taken(pe, li, "sc", n, 1 if n < 2 else 0)
                    for q in range(2 if n < 2 else 1):
                        j = Job(li, "pt", n, q)
                        for b, (_, _, c) in enumerate(bl[4 * q:4 * q + 4]):
                            j.tr(b * P, P, A["pb"][:, n % 2, c:c + P], P)
                        j.end()
                    if n + 2 < 6:
                        scores(n + 2)
                    j = Job(li, "pv", n)
                    taken(pe, li, "pt", n, 1 if n < 2 else 0)
                    for i in range(4):
                        mine = [(b, kt) for b, (qt, kt, _) in enumerate(bl) if qt == i]
                        for b, kt in mine:
                            j.mm(i * 64, 64, A["ptb"][:, n % 2, b * P:(b + 1) * P],
                                 A["vt"][:, g, kt, 64 * (n % 2):64 * (n % 2) + 64],
                                 start=(b == mine[0][0]), stop=(b == mine[-1][0]))
                    j.end()
                    if n % 2:
                        j = Job(li, "st", g)
                        taken(pe, li, "pv", n)
                        for i in range(4):
                            j.tr(i * P, P, A["os"][:, g % 2, i, :], P)
                        j.end()
                pe.wait_ge(S("lse_made"), li + 1)
                for g in range(3):
                    j = Job(li, "lt", g)
                    for i in range(4):
                        j.tr(i * P, P, A["lse"][:, 2 * g:2 * g + 2, i], 2)
                    j.end()
                pe.wait_ge(S("alpha_made"), li + 1)
                for g in range(3):
                    j = Job(li, "al", g)
                    j.mm(0, SEQ, K(C_S2, P, 2), A["lr"][:, g, :])
                    j.end()
                for g in range(3):
                    rows = ROWS_G[g]
                    pe.wait_ge(S("dq_made"), 3 * li + g + 1)
                    for q in range(2):
                        j = Job(li, "qb", g, q)
                        j.mm(0, 512, K(C_ONE, rows, NB), A["dq"][:, 4 * q:4 * q + 4, :], rows=rows)
                        j.end()
                for g in range(3):
                    rows = ROWS_G[g]
                    pe.wait_ge(S("s_dots"), 3 * li + g + 1)
                    j = Job(li, "sct", g)
                    for h in range(2):
                        j.tr(h * P, rows, A["scr"][0:rows, g, h, :], NB, rows)
                    j.end()
                pe.wait_ge(S("sp_made"), li + 1)
                j = Job(li, "ppt")
                for gh in range(6):
                    j.tr(gh * NB, NB, A["sp"][:, gh, 0:ROWS_G[gh // 2]], ROWS_G[gh // 2], NB)
                j.end()
                j = Job(li, "spv")
                taken(pe, li, "ppt")
                for gh in range(6):
                    g, rows = gh // 2, ROWS_G[gh // 2]
                    for n in range(NB):
                        c = P + 64 * (gh % 2)
                        j.mm(gh * 64, 64, A["pm"][0:rows, gh, n, :], A["ck"][0:rows, g, n, c:c + 64],
                             start=(n == 0), stop=(n == NB - 1), rows=NB)
                j.end()

            def turn_heads(li, m):
                j = Job(li, "mt", m)
                pe.wait_ge(S("ob_normed"), 5 * li + m + 1)
                for c in range(NC):
                    j.tr(c * P, P, R["ob"][:, m % 2, c, :], P)
                j.end()

            def hgrn(li):
                pe.wait_ge(S("window_end"), li + 1)
                for c in range(NC):
                    j = Job(li, "hv", c)
                    for n, t in enumerate((TI, TI + 1, TF + 2)):
                        j.tr(n * P, P, proj[:, t, c * P:(c + 1) * P], P)
                    j.end()
                for n, tiles in enumerate(((TI, TI + 1, TF + 2), (TV, TV + 1, TU + 2))):
                    j = Job(li, "th", n)
                    for i, t in enumerate(tiles):
                        j.tr(i * P, P, proj[:, t, SEQ:T], NB)
                    j.end()
                pe.wait_ge(S("k_last"), li + 1)
                pe.wait_ge(S("scratch_clear"), li + 1)
                for c in range(NC):
                    j = Job(li, "kh", c)
                    for f in range(3):
                        j.tr(f * P, P, R["w1"][:, f, c * P:(c + 1) * P], P)
                    j.end()
                    j = Job(li, "su", c)
                    taken(pe, li, "kh", c)
                    taken(pe, li, "hv", c)
                    for h in range(5):
                        rows, r0 = (64, 64 * (h % 2)) if h < 4 else (P, 0)
                        j.mm((h // 2) * 64, 64, R["kt"][:, c % 2, h * 64:h * 64 + rows],
                             R["vh"][:, c, v_col(h):v_col(h) + 64], rows=rows, r0=r0)
                    j.end()
                for l in range(LVL + 1):
                    if l < LVL:
                        pe.wait_ge(S("lv_made"), LVL * li + l + 1)
                    for h in range(5):
                        f, r = h // 2, slice(64 * (h % 2), 64 * (h % 2) + 64)
                        w = R["w0"] if l % 2 == 0 else R["w1"]
                        j = Job(li, "at", h, l)
                        for c in range(NC):
                            t = slice(c * P, (c + 1) * P)
                            if l < LVL:
                                j.mm(c * P, P, w[r, f, t], w[r, f, t])
                            else:
                                j.mm(c * P, P, R["kh"][r, f, t], proj[r, TQ + f, t])
                        j.end()
                pe.wait_ge(S("qe_made"), li + 1)
                for h in range(5):
                    f, r = h // 2, slice(64 * (h % 2), 64 * (h % 2) + 64)
                    j = Job(li, "ho", h)
                    taken(pe, li, "at", h, LVL)
                    if h == 0:
                        taken(pe, li, "su", NC - 1)
                    for c in range(NC):
                        t = slice(c * P, (c + 1) * P)
                        j.mm(c * 64, 64, R["att"][:, h, t], R["vh"][:, c, v_col(h):v_col(h) + 64], stop=False)
                        j.mm(c * 64, 64, proj[r, TF + f, t], R["sall"][r, c, f, :], start=False)
                    j.end()
                    if h in (1, 3):
                        turn_heads(li, h // 2)

            def mlstm(li):
                for c in range(NC):
                    j = Job(li, "mv", c)
                    for n, t in enumerate((TV, TV + 1, TU + 2)):
                        j.tr(n * P, P, proj[:, t, c * P:(c + 1) * P], P)
                    j.end()
                pe.wait_ge(S("c_made"), li + 1)
                for f in range(3):
                    for s in range(4):
                        j = Job(li, "mq", f, s)
                        c = (s % 2) * H2
                        j.mm(0, H2, bd[:, li, s // 2, f, :], R["w0"][:, f, c:c + H2])
                        j.end()
                pe.wait_ge(S("rows_made"), li + 1)
                j = Job(li, "rt")
                for c in range(NC):
                    j.tr(c * P, P, R["rows"][:, c * P:(c + 1) * P], P)
                j.end()
                j = Job(li, "ac")
                taken(pe, li, "rt")
                j.mm(0, NC * 5, bc(K(C_ID + P - 1, 1), P, P), R["ec"][:, 0, :, :])
                j.end()
                taken(pe, li, "mq", 2, 3)
                for c in range(NC):
                    j = Job(li, "kt", c)
                    for f in range(3):
                        j.tr(f * P, P, R["kh"][:, f, c * P:(c + 1) * P], P)
                    j.end()
                    j = Job(li, "cu", c)
                    taken(pe, li, "kt", c)
                    taken(pe, li, "mv", c)
                    for h in range(5):
                        rows, r0, heads = (64, 64 * (h % 2), 1) if h < 4 else (P, 0, 2)
                        j.mm((h // 2) * 65, 65, R["kw"][:, c % 2, h:h + heads, :], R["va"][:, c, h, :],
                             rows=rows, r0=r0)
                    j.end()
                for h in range(5):
                    f, r = h // 2, slice(64 * (h % 2), 64 * (h % 2) + 64)
                    j = Job(li, "md", h)
                    pick = bc(K(C_ID + h, 1, 5), 5, P)
                    j.mm(0, SEQ, pick, proj[0:5, 7, 0:SEQ], stop=False)
                    for c in range(NC):
                        j.mm(c * P, P, proj[0:5, 3, c * P:(c + 1) * P], pick, start=False, stop=False)
                    for c in range(NC):
                        j.mm(c * P, P, ident, K(C_NEGC, P), start=False)
                    j.end()
                    j = Job(li, "mqk", h)
                    for c in range(NC):
                        t = slice(c * P, (c + 1) * P)
                        j.mm(c * P, P, R["kh"][r, f, t], R["bt"][r, f, t])
                    j.end()
                    j = Job(li, "mi", h)
                    if h == 0:
                        taken(pe, li, "cu", NC - 1)
                    for c in range(NC):
                        j.mm(c * 65, 65, R["bt"][r, f, c * P:(c + 1) * P], R["call"][r, c, f, :])
                    j.end()
                    j = Job(li, "mo", h)
                    taken(pe, li, "mqk", h)
                    for c in range(NC):
                        j.mm(c * 65, 65, R["qd"][:, h % 2, c * P:(c + 1) * P], R["va"][:, c, h, :])
                    j.end()
                    if h % 2 == 0:
                        turn_heads(li, 2 + h // 2)

            def sample(li):
                S8 = flat(TSK, 3 * NB * 64).rearrange("p (f b v) -> p f b v", f=3, b=NB)
                C8 = flat(TSV, 3 * NB * 65).rearrange("p (f b v) -> p f b v", f=3, b=NB)

                def spread(kind):
                    for f in range(3):
                        j = Job(li, kind, f)
                        even = R["ee"][0:NB, :, :].rearrange("p f t -> p (f t)")[:, f * 512:(f + 1) * 512]
                        odd = R["w1"][0:NB, :, :].rearrange("p f t -> p (f t)")[:, f * 512:(f + 1) * 512]
                        if f < 2:
                            j.mm(0, 512, K(C_ONE, 64, NB), even, rows=64)
                            j.mm(0, 512, K(C_ONE, 64, NB), odd, rows=64, r0=64)
                        else:
                            j.mm(0, 512, K(C_ONE, P, NB), even)
                        j.end()

                def query(kind, state, w):
                    for s in range(2):
                        j = Job(li, kind, s)
                        r = slice(64 * s, 64 * s + 64)
                        for f in range(3 - s):
                            for b in range(NB):
                                j.mm(f * w, w, R["qm8"][r, f, b, :], state[r, f, b, :], start=(b == 0),
                                     stop=(b == NB - 1), rows=NB)
                        j.end()

                pe.wait_ge(S("dv_made"), 2 * li + 1)
                spread("vb")
                pe.wait_ge(S("s8_made"), li + 1)
                query("so", S8, 64)
                pe.wait_ge(S("m8_exp"), li + 1)
                j = Job(li, "rs")
                j.tr(0, 5, R["sc8"][0:5, 16:24], NB, 5)
                j.end()
                j = Job(li, "aw")
                for f in range(3):
                    j.mm(f * 2 * NB, 2 * NB, K(C_HP + f * P, P, 5), R["sc8"][0:5, 0:2 * NB])
                j.end()
                pe.wait_ge(S("dv_made"), 2 * li + 2)
                spread("vc")
                pe.wait_ge(S("c8_made"), li + 1)
                query("co", C8, 65)
                pe.wait_ge(S("obs_normed"), li + 1)
                j = Job(li, "fx")
                for m in range(KD):
                    src = R["obs"][:, 2 * m:2 * m + 2, :].rearrange("b h d -> b (h d)") if m < 5 \
                        else osw[:, (m - 5) * P:(m - 4) * P]
                    j.tr(m * NB, NB, src, P, NB)
                j.end()

            for li in range(2):
                norm(2 * li)
                pe.wait_ge(nl_made, KD * (2 * li + 1))
                for n in range(NPS):
                    unit(U_IN[li] + n, KD, xnh, xnl)
                with pe.Fori(0, (NT - 3) // 6) as i:
                    for n in range(6):
                        u = U_IN[li] + 3 + n
                        pe.wait_ge(proj_read, i * 6 + (NT * li + n + 1))
                        unit(u, KD, xnh, xnl, i * 6 + u)
                pe.wait_ge(proj_read, NT * (li + 1))
                window(li)
                hgrn(li)
                mlstm(li)
                sample(li)
                pe.wait_ge(mixl_made, KD * (li + 1))
                for n in range(KD):
                    if n >= NPS:
                        pe.wait_ge(x_updated, X_OUT[li] - KD + n - NPS + 1)
                    unit(U_OUT[li] + n, KD, xnh, xnl)
                norm(2 * li + 1)
                pe.wait_ge(nl_made, KD * (2 * li + 2))
                if li == 1:
                    pe.wait_ge(rw_lo, 1)
                    pe.wait_ge(rstd_made, 4)
                    passes(0, psum[0:8, 6:8, 0:H2], KD, xnh, xnl, 8, rwh, rwl).then_inc(rt_done, 1)
                    pe.wait_ge(rt_read, 1)
                    for t in range(5):
                        n = P if t < 4 else NB
                        ins = pe.transpose(psum[0:n, 6, t * 8:t * 8 + 8], lg[:, t * P:t * P + n], K(C_ID, 8, 8))
                    ins.then_inc(rt_done, 1)
                    pe.wait_ge(rt_read, 2)
                    for t in range(5):
                        n = P if t < 4 else NB
                        ins = pe.transpose(psum[0:8, 7 if t < 4 else 6, (t % 4) * P:(t % 4) * P + n], re[0:n, t, :],
                                           K(C_ID, n, n))
                    ins.then_inc(rt_done, 1)
                    for e in range(8):
                        pe.wait_ge(rt_read, 3 + e)
                        for s in range(2):
                            ins = pe.matmul(psum[:, 6 + s, 0:H2], bc(K(C_ID + e, 1, 8), 8, P), gT[:, s * H2:(s + 1) * H2],
                                            start=True, stop=True)
                        ins.then_inc(rt_done, 1)
                with pe.Fori(0, NEX[li]) as e:
                    for n in range(UPE):
                        p_ = n - NPS
                        before, back = (p_, 0) if p_ >= 0 else (p_ + UPE, 1)
                        if before >= 2 * KF:
                            pe.wait_ge(x_updated, e * KD + (X_OUT[li] - back * KD + before - 2 * KF + 1))
                        elif before % 2 == 0:
                            pe.wait_ge(gate_read, e * KF + (G_FF[li] + before // 2 + 1))
                        else:
                            pe.wait_ge(up_read, e * KF + (G_FF[li] + before // 2 + 1))
                        if n < 2 * KF:
                            unit(U_FF[li] + n, KD, xnh, xnl, e * UPE + (U_FF[li] + n))
                        else:
                            if n == 2 * KF:
                                pe.wait_ge(hl_made, e * KF + (G_FF[li] + KF))
                            unit(U_FF[li] + n, KF, hh, hl, e * UPE + (U_FF[li] + n))
            norm(4)

        @block.vector
        def _(v):
            def step(ins):
                bump(ins, dve_step, v)

            def sig(ins, name):
                bump(ins, S(name), v)

            def free(ins, li, *key):
                release(v, ins, li, *key)

            tt, ts, stt = v.tensor_tensor, v.tensor_scalar, v.scalar_tensor_tensor

            def norm(r):
                if r:
                    v.wait_ge(x_updated, [0, X_OUT[0], X_FF[0], X_OUT[1], X_FF[1]][r])
                v.wait_ge(rstd_made, r + 1)
                for k in range(KD):
                    gain = par(r // 2, (PR_G1, PR_G2)[r % 2] + k) if r < 4 else par(0, PR_GF + k)
                    if r == 4:
                        stt(yout[:, k, :], xT[:, k, :], gain, rstd[:], ALU.mult, ALU.mult).then_inc(y_made, 1)
                        continue
                    if KD * r + k >= 2:
                        v.wait_ge(nl_made, KD * r + k - 1)
                    stt(n32[:, k % 2, :], xT[:, k, :], gain, rstd[:], ALU.mult, ALU.mult).then_inc(n32_made, 1)

            def window(li):
                for i in range(3):
                    made(v, li, "tm", i)
                    cols = (4 if i < 2 else 1) * P
                    free(v.tensor_copy(A["tms"][:, i * 512:i * 512 + cols], bank("tm", i)[0:NB, 0:cols]), li, "tm", i)

                def maxima(n):
                    for q in range(2 if n < 2 else 1):
                        made(v, li, "sc", n, q)
                        w = 256 if n < 2 else P
                        k = 512 // w
                        step(v.tensor_reduce(A["mx"][:, n, q * k:(q + 1) * k],
                                             bank("sc", n, q).rearrange("p (i s) -> p i s", s=w), AX, ALU.max))
                    sig(ts(A["nm"][:, n, :], A["mx"][:, n, :], -0.125, None, ALU.mult), "max_made")

                maxima(0)
                maxima(1)
                for n in range(6):
                    g, h = n // 2, n % 2
                    if n + 2 < 6:
                        maxima(n + 2)
                    made(v, li, "pv", n)
                    step(v.reciprocal(A["rd"][:, n, :], A["den"][:, n, :]))
                    free(tt(A["os"][:, g % 2, :, 64 * h:64 * h + 64],
                            bank("pv", n)[:, 0:256].rearrange("p (i d) -> p i d", i=4),
                            bc(A["rd"][:, n, :].unsqueeze(2), P, 4, 64), ALU.mult), li, "pv", n)
                    if h:
                        made(v, li, "st", g)
                        free(v.tensor_copy(natural(g, proj[:, TSQ + g, 0:SEQ]), grouped(g, bank("st", g))), li, "st", g)
                v.wait_ge(S("den_ln"), li + 1)
                sig(stt(A["lse"][:], A["mx"][:], 0.125, A["lse"][:], ALU.mult, ALU.add), "lse_made")
                for g in range(3):
                    made(v, li, "lt", g)
                    free(v.tensor_copy(natural(g, A["lr"][:, g, :]), grouped(g, bank("lt", g)[0:2, :])), li, "lt", g)
                lr, lm = A["lr"], A["lm"]
                step(tt(lm[:], lr[:, 0, :], lr[:, 1, :], ALU.max))
                step(tt(lm[:], lm[:], lr[:, 2, :], ALU.max))
                sig(tt(lr[:], lr[:], bc(lm[:].unsqueeze(1), 2, 3, SEQ), ALU.subtract), "lse_centred")
                v.wait_ge(S("lse_exp"), li + 1)
                step(tt(lm[:], lr[:, 0, :], lr[:, 1, :], ALU.add))
                step(tt(lm[:], lm[:], lr[:, 2, :], ALU.add))
                step(v.reciprocal(lm[:], lm[:]))
                sig(tt(lr[:], lr[:], bc(lm[:].unsqueeze(1), 2, 3, SEQ), ALU.mult), "alpha_made")
                for g in range(3):
                    made(v, li, "al", g)
                    free(tt(proj[:, TSQ + g, 0:SEQ], proj[:, TSQ + g, 0:SEQ], bank("al", g), ALU.mult), li, "al", g)
                tms = A["tms"]
                own = A["own"][:].rearrange("b h d -> b (h d)")
                step(v.memset(A["ss"][:], NEG))
                step(tt(own, tms[:, 0:384], tms[:, 384:768], ALU.mult))
                step(v.tensor_reduce(A["ss"][:, :, 128], A["own"][:], AX, ALU.add))
                v.wait_ge(cache_in, 16 * (li + 1))
                for g in range(3):
                    rows = ROWS_G[g]
                    if g:
                        made(v, li, "qb", g - 1, 1)
                    sig(tt(A["dq"][:], bc(tms[:, g * P:(g + 1) * P].unsqueeze(1), NB, NB, P),
                           bc(K(C_ID, NB, NB).unsqueeze(2), NB, NB, P), ALU.mult), "dq_made")
                    for q in range(2):
                        made(v, li, "qb", g, q)
                        free(tt(A["pr"][0:rows, :].rearrange("p (n c) -> p n c", n=4),
                                bank("qb", g, q)[0:rows, :].rearrange("p (n c) -> p n c", n=4),
                                A["ck"][0:rows, g, 4 * q:4 * q + 4, 0:P], ALU.mult), li, "qb", g, q)
                        ins = v.tensor_reduce(A["scr"][0:rows, g, :, 4 * q:4 * q + 4].rearrange("p h n -> p n h"),
                                              A["pr"][0:rows, :].rearrange("p (n h d) -> p n h d", n=4, h=2), AX, ALU.add)
                        if q:
                            sig(ins, "s_dots")
                        else:
                            step(ins)
                for g in range(3):
                    rows = ROWS_G[g]
                    made(v, li, "sct", g)
                    free(v.tensor_copy(A["ss"][:, 2 * g:2 * g + 2, 0:rows],
                                       bank("sct", g)[0:NB, 0:2 * P].rearrange("b (h s) -> b h s", h=2)[:, :, 0:rows]),
                         li, "sct", g)
                step(v.tensor_reduce(A["smx"][:], A["ss"][:], AX, ALU.max))
                sig(tt(A["sp"][:], A["ss"][:], bc(A["smx"][:].unsqueeze(2), NB, 6, 129), ALU.subtract), "s_centred")
                v.wait_ge(S("s_exp"), li + 1)
                sig(v.tensor_reduce(A["sden"][:], A["sp"][:], AX, ALU.add), "s_den")
                v.wait_ge(S("s_den_ln"), li + 1)
                by_head = A["slse"][:].rearrange("b (g h) -> b h g", g=3)
                m2 = bc(A["sm2"][:].unsqueeze(2), NB, 2, 3)
                step(stt(A["slse"][:], A["smx"][:], 0.125, A["slse"][:], ALU.mult, ALU.add))
                step(v.tensor_reduce(A["sm2"][:], by_head, AX, ALU.max))
                sig(tt(by_head, by_head, m2, ALU.subtract), "s_lse_centred")
                v.wait_ge(S("s_lse_exp"), li + 1)
                step(v.tensor_reduce(A["sm2"][:], by_head, AX, ALU.add))
                step(v.reciprocal(A["sm2"][:], A["sm2"][:]))
                step(tt(by_head, by_head, m2, ALU.mult))
                step(v.reciprocal(A["sden"][:], A["sden"][:]))
                step(tt(A["slse"][:], A["slse"][:], A["sden"][:], ALU.mult))
                sig(tt(A["sp"][:], A["sp"][:], bc(A["slse"][:].unsqueeze(2), NB, 6, 129), ALU.mult), "sp_made")
                made(v, li, "ppt")
                for g in range(3):
                    rows = ROWS_G[g]
                    ins = tt(A["pm"][0:rows, 2 * g:2 * g + 2, :, :].rearrange("p h n m -> p (h n) m"),
                             bc(bank("ppt")[0:rows, 2 * g * NB:(2 * g + 2) * NB].unsqueeze(2), rows, 2 * NB, NB),
                             K(C_DM, 2 * NB * NB, rows).rearrange("p (n m) -> p n m", m=NB), ALU.mult)
                    if g < 2:
                        step(ins)
                    else:
                        free(ins, li, "ppt")
                step(tt(A["own"][:], tms[:, 768:1152].rearrange("b (h d) -> b h d", h=6),
                        bc(A["sp"][:, :, 128:129], NB, 6, 64), ALU.mult))
                made(v, li, "spv")
                free(tt(osw[:], bank("spv")[0:NB, 0:384], own, ALU.add), li, "spv")
                v.wait_ge(window_dma, 112 * (li + 1))
                sig(v.memset(A["mx"][:], 0.0), "window_end")

            def normalise(li, m):
                ob = R["ob"][:, m % 2, :, :]
                heads = ob.rearrange("p c (h d) -> p (c h) d", h=2)
                step(tt(R["sqo"][:], ob, ob, ALU.mult))
                sig(v.tensor_reduce(R["ss2"][:], R["sqo"][:].rearrange("p c (h d) -> p (c h) d", h=2), AX, ALU.add), "ob_ms")
                v.wait_ge(S("ob_rms"), 5 * li + m + 1)
                sig(tt(heads, heads, bc(R["ss2"][:].unsqueeze(2), P, 8, 64), ALU.mult), "ob_normed")
                made(v, li, "mt", m)
                gate = proj[:, TG + m, 0:SEQ]
                free(stt(gate, bank("mt", m), par(li, PR_ON + m), gate, ALU.mult, ALU.mult), li, "mt", m)

            def hgrn(li):
                z, kh, bt, ee, w0, w1 = proj[:, TF:TF + 3, :], R["kh"], R["bt"], R["ee"], R["w0"], R["w1"]
                q = proj[:, TQ:TQ + 3, :]
                step(ts(kh[:], z, 0.0, None, ALU.min))
                sig(ts(bt[:], z, 0.0, None, ALU.max), "z_parts")
                v.wait_ge(S("z_exp"), li + 1)
                step(tt(ee[:], w0[:], w1[:], ALU.add))
                step(v.reciprocal(bt[:], ee[:]))
                step(tt(bt[:], bt[:], w1[:], ALU.mult))
                if li:
                    for f in range(3):
                        step(stt(w0[:, f, :], w1[:, f, :], lbt[:, 2, f:f + 1], w0[:, f, :], ALU.mult, ALU.add))
                    step(ts(w0[:], w0[:], 2.0 ** -63, None, ALU.max))
                sig(v.memset(R["ss2"][:], 0.0), "z_sums")
                v.wait_ge(S("z_ln"), li + 1)
                if li:
                    step(tt(w0[:], w0[:], kh[:], ALU.max))
                    step(tt(w0[:], w0[:], ee[:], ALU.subtract))
                    for f in range(3):
                        step(ts(kh[:, f, :], bt[:, f, :], lbt[:, 3, f:f + 1], None, ALU.mult))
                else:
                    step(tt(w0[:], kh[:], ee[:], ALU.subtract))
                    step(v.tensor_copy(kh[:], bt[:]))
                sig(v.tensor_copy(R["ff"][:], w0[:, :, SEQ:T]), "f8_copied")
                step(v.tensor_copy(R["k8"][:], kh[:, :, SEQ:T]))
                for f in range(3):
                    step(v.tensor_tensor_scan(bt[:, f, 0:SEQ], K(C_RST, SEQ), w0[:, f, 0:SEQ], 0.0, ALU.mult, ALU.add))
                b4 = bt[:, :, 0:SEQ].rearrange("p f (c j) -> p f c j", j=CH)
                e4 = ee[:, :, 0:SEQ].rearrange("p f (c j) -> p f c j", j=CH)
                step(v.tensor_copy(R["dl"][:], b4[:, :, :, CH - 1]))
                for f in range(3):
                    ins = tt(e4[:, f], bc(b4[:, f, :, CH - 1:CH], P, NC, CH), b4[:, f], ALU.subtract)
                    if f < 2:
                        step(ins)
                    else:
                        sig(ins, "to_last")
                v.wait_ge(S("to_last_exp"), li + 1)
                sig(tt(w1[:, :, 0:SEQ], kh[:, :, 0:SEQ], ee[:, :, 0:SEQ], ALU.mult), "k_last")
                v.wait_ge(S("gates_made"), li + 1)
                v.wait_ge(S("from_first_exp"), li + 1)
                taken(v, li, "hv", NC - 1)
                for n in range(2):
                    made(v, li, "th", n)
                    free(v.tensor_copy(R["thm"][:, n * 384:(n + 1) * 384], bank("th", n)[0:NB, 0:384]), li, "th", n)
                sig(tt(proj[:, TF:TF + 3, 0:SEQ], q[:, :, 0:SEQ], ee[:, :, 0:SEQ], ALU.mult), "qe_made")

                def state(c):
                    made(v, li, "su", c)
                    s0, s1 = R["sall"][:, c, :, :], R["sall"][:, c + 1, :, :]
                    step(tt(s1, s0, bc(R["dl"][:, :, c:c + 1], P, 3, 64), ALU.mult))
                    free(tt(s1, s1, bank("su", c)[:, 0:192].rearrange("p (f d) -> p f d", f=3), ALU.add), li, "su", c)

                v.wait_ge(S("scratch_clear"), li + 1)

                def level(l):
                    n = CH >> (l + 1)
                    w = w0 if l % 2 == 0 else w1

                    def cut(ap, half, f):
                        return ap[:, f, 0:SEQ].rearrange("p (m s j) -> p m s j", s=2, j=n)[:, :, half, :]

                    for f in range(3):
                        first, second = cut(bt, 0, f), cut(bt, 1, f)
                        mid = bc(first[:, :, n - 1:n], P, SEQ // (2 * n), n)
                        step(tt(cut(ee, 0, f), mid, first, ALU.subtract))
                        ins = tt(cut(ee, 1, f), second, mid, ALU.subtract)
                        if f < 2:
                            step(ins)
                        else:
                            sig(ins, "lv_diff")

                    def finish():
                        v.wait_ge(S("lv_exp"), LVL * li + l + 1)
                        if l >= 2:
                            made(v, li, "at", 4, l - 2)
                        for f in range(3):
                            step(tt(cut(w, 0, f), cut(kh, 0, f), cut(ee, 0, f), ALU.mult))
                            ins = tt(cut(w, 1, f), cut(q, 1, f), cut(ee, 1, f), ALU.mult)
                            if f < 2:
                                step(ins)
                            else:
                                sig(ins, "lv_made")
                    return finish

                def gather(l):
                    for h in range(5):
                        made(v, li, "at", h, l)
                        free(v.copy_predicated(R["att"][:, h, :].rearrange("p (c t) -> p c t", c=NC),
                                               bc(lvm[:, l, :].unsqueeze(1), P, NC, CH),
                                               bank("at", h, l).rearrange("p (c t) -> p c t", c=NC)), li, "at", h, l)

                for c in range(NC):
                    state(c)
                for l in range(LVL):
                    level(l)()
                    if l:
                        gather(l - 1)
                gather(LVL - 1)
                gather(LVL)
                for h in range(5):
                    made(v, li, "ho", h)
                    free(v.tensor_copy(R["ob"][:, (h // 2) % 2, :, 64 * (h % 2):64 * (h % 2) + 64],
                                       bank("ho", h)[:, 0:256].rearrange("p (c d) -> p c d", c=NC)), li, "ho", h)
                    if h in (1, 3):
                        normalise(li, h // 2)

            def mlstm(li):
                w0, mu = R["w0"], proj[:, TU:TU + 3, :]
                step(v.memset(R["va"][:, :, :, 64:65], 1.0))
                step(v.memset(R["kw"][:, :, 5, :], 0.0))
                for f in range(3):
                    def tap(j):
                        return par(li, PR_CW + 4 * f + j)
                    step(ts(w0[:, f, :], mu[:, f, :], tap(3), par(li, PR_CB + f), ALU.mult, ALU.add))
                    for j in range(3):
                        s = 3 - j
                        step(stt(w0[:, f, s:SEQ], mu[:, f, 0:SEQ - s], tap(j), w0[:, f, s:SEQ], ALU.mult, ALU.add))
                        ins = stt(w0[:, f, SEQ:T], cbuf[:, li, f, j, :], tap(j), w0[:, f, SEQ:T], ALU.mult, ALU.add)
                        if f == 2 and j == 2:
                            sig(ins, "conv_made")
                        else:
                            step(ins)
                ig, lf, m, F, t4 = (proj[0:5, n, :] for n in (3, 4, 5, 6, 7))
                step(ts(ig, proj[64:69, TQ + 2, :], par(li, PR_IB, 1, 5, 64), None, ALU.add))
                step(ts(lf, proj[96:101, TQ + 2, :], par(li, PR_FB, 1, 5, 96), None, ALU.add))
                sig(stt(t4, lf, -1.0, lf, ALU.mult, ALU.max), "fg_abs")
                v.wait_ge(S("fg_ln"), li + 1)
                step(stt(lf, lf, 0.0, t4, ALU.min, ALU.subtract))
                step(v.tensor_tensor_scan(m[:, 0:SEQ], lf[:, 0:SEQ], ig[:, 0:SEQ], 0.0, ALU.add, ALU.max))
                step(v.tensor_tensor_scan(F[:, 0:SEQ], K(C_RST, SEQ, 5), lf[:, 0:SEQ], 0.0, ALU.mult, ALU.add))
                step(tt(t4[:, 0:SEQ], F[:, 0:SEQ], m[:, 0:SEQ], ALU.subtract))
                step(tt(ig[:, 0:SEQ], ig[:, 0:SEQ], F[:, 0:SEQ], ALU.subtract))
                rows = R["rows"]

                def ch(ap):
                    return ap[:, 0:SEQ].rearrange("p (c j) -> p c j", j=CH)
                step(v.tensor_copy(rows[0:5, 0:CH], t4[:, 0:CH]))
                step(tt(ch(rows[0:5, :])[:, 1:NC, :], ch(t4)[:, 1:NC, :],
                        bc(ch(m)[:, 0:NC - 1, CH - 1:CH], 5, NC - 1, CH), ALU.add))
                step(tt(ch(rows[32:37, :]), ch(ig), bc(ch(t4)[:, :, CH - 1:CH], 5, NC, CH), ALU.add))
                sig(ts(rows[64:69, :], m[:, 0:SEQ], -1.0, None, ALU.mult), "rows_made")
                made(v, li, "ac")
                ac = bank("ac")[:, 0:NC * 5].rearrange("p (c h) -> p c h", c=NC)
                step(v.tensor_copy(R["acb"][0:64, :, :], ac[0:64, :, 0:5:2]))
                free(v.tensor_copy(R["acb"][64:P, :, 0:2], ac[64:P, :, 1:5:2]), li, "ac")
                for c in range(NC):
                    made(v, li, "kt", c)
                    free(tt(R["kw"][:, c % 2, 0:5, :], bank("kt", c)[:, 0:320].rearrange("p (h d) -> p h d", h=5),
                            bc(R["ec"][:, 1, c, :].unsqueeze(2), P, 5, 64), ALU.mult), li, "kt", c)
                    made(v, li, "cu", c)
                    s0, s1 = R["call"][:, c, :, :], R["call"][:, c + 1, :, :]
                    step(tt(s1, s0, bc(R["acb"][:, c, :].unsqueeze(2), P, 3, 65), ALU.mult))
                    free(tt(s1, s1, bank("cu", c)[:, 0:195].rearrange("p (f d) -> p f d", f=3), ALU.add), li, "cu", c)
                for h in range(5):
                    made(v, li, "mqk", h)
                    taken(v, li, "md", h)
                    free(tt(R["qd"][:, h % 2, :], bank("mqk", h), R["dw"][:, h % 2, :], ALU.mult), li, "mqk", h)
                    num, t1 = R["num"], R["t1"]
                    made(v, li, "mi", h)
                    free(tt(t1[:], bank("mi", h)[:, 0:260].rearrange("p (c d) -> p c d", c=NC),
                            bc(R["ec"][:, 0, :, h:h + 1], P, NC, 65), ALU.mult), li, "mi", h)
                    made(v, li, "mo", h)
                    free(tt(num[:], bank("mo", h)[:, 0:260].rearrange("p (c d) -> p c d", c=NC), t1[:], ALU.add), li, "mo", h)
                    nq = num[:, :, 64]
                    step(stt(R["rden"][:], nq, -1.0, nq, ALU.mult, ALU.max))
                    step(tt(R["rden"][:], R["rden"][:], R["ec"][:, 2, :, h], ALU.max))
                    step(v.reciprocal(R["rden"][:], R["rden"][:]))
                    n = 5 + h
                    step(tt(R["ob"][:, (n // 2) % 2, :, 64 * (n % 2):64 * (n % 2) + 64], num[:, :, 0:64],
                            bc(R["rden"][:].unsqueeze(2), P, NC, 64), ALU.mult))
                    if n % 2:
                        normalise(li, n // 2)

            def sample(li):
                S8 = flat(TSK, 3 * NB * 64).rearrange("p (n d) -> p n d", d=64)
                C8 = flat(TSV, 3 * NB * 65).rearrange("p (n d) -> p n d", d=65)
                tmp = R["w0"][:].rearrange("p f t -> p (f t)")[:, 0:3 * NB * 64].rearrange("p (n d) -> p n d", d=64)
                ff = R["ff"][:].rearrange("p f b -> p (f b)")

                def diag(n):
                    th = R["thm"][:, n * 384:(n + 1) * 384]
                    even, odd = (R[k][0:NB, :, :].rearrange("p f t -> p (f t)")[:, 0:1536].rearrange(
                        "p (f b d) -> p f b d", f=3, b=NB) for k in ("ee", "w1"))
                    eye = bc(K(C_ID, NB, NB).unsqueeze(2), NB, NB, 64)
                    for f in range(3):
                        c = f * P if f < 2 else 320
                        ins = tt(even[:, f], bc(th[:, c:c + 64].unsqueeze(1), NB, NB, 64), eye, ALU.mult)
                        if f == 2:
                            sig(ins, "dv_made")
                            break
                        step(ins)
                        step(tt(odd[:, f], bc(th[:, c + 64:c + P].unsqueeze(1), NB, NB, 64), eye, ALU.mult))

                def outer(kind, kcol):
                    for f in range(3):
                        made(v, li, kind, f)
                        free(tt(tmp[:, f * NB:(f + 1) * NB, :], bank(kind, f).rearrange("p (b d) -> p b d", b=NB),
                                bc(kcol[:, f * NB:(f + 1) * NB].unsqueeze(2), P, NB, 64), ALU.mult), li, kind, f)

                def masked_query(src):
                    for f in range(3):
                        ins = tt(R["qm8"][:, f], bc(src[:, f, SEQ:T].unsqueeze(2), P, NB, NB),
                                 K(C_DM, NB * NB).rearrange("p (n m) -> p n m", m=NB), ALU.mult)
                        step(ins)

                diag(0)
                v.wait_ge(S("f8_exp"), li + 1)
                v.wait_ge(state_in, 48 * (li + 1))
                step(tt(S8, S8, bc(ff.unsqueeze(2), P, 3 * NB, 64), ALU.mult))
                outer("vb", R["k8"][:].rearrange("p f b -> p (f b)"))
                masked_query(proj[:, TQ:TQ + 3, :])
                sig(tt(S8, S8, tmp, ALU.add), "s8_made")
                sc8 = R["sc8"]
                ig8, lf8 = proj[0:5, 3, SEQ:T], proj[0:5, 4, SEQ:T]
                step(tt(sc8[0:5, 0:8], lf8, sc8[0:5, 24:32], ALU.add))
                step(tt(sc8[0:5, 32:40], sc8[0:5, 0:8], ig8, ALU.max))
                step(tt(sc8[0:5, 0:8], sc8[0:5, 0:8], sc8[0:5, 32:40], ALU.subtract))
                step(tt(sc8[0:5, 8:16], ig8, sc8[0:5, 32:40], ALU.subtract))
                sig(ts(sc8[0:5, 16:24], sc8[0:5, 32:40], -1.0, None, ALU.mult), "m8_rows")
                for s in range(2):
                    made(v, li, "so", s)
                    free(v.tensor_copy(R["obs"][:, s:5:2, :],
                                       bank("so", s)[0:NB, 0:64 * (3 - s)].rearrange("b (h d) -> b h d", d=64)),
                         li, "so", s)
                made(v, li, "rs")
                free(v.tensor_copy(R["e8"][:], bank("rs")[0:NB, 0:5]), li, "rs")
                made(v, li, "aw")
                free(v.tensor_copy(R["aw"][:].rearrange("p f b -> p (f b)"), bank("aw")[:, 0:48]), li, "aw")
                diag(1)
                a8, w8 = R["aw"][:, :, 0:NB], R["aw"][:, :, NB:2 * NB]
                step(tt(R["ff"][:], R["kh"][:, :, SEQ:T], w8, ALU.mult))
                step(v.tensor_copy(R["k8"][:], a8))
                step(tt(C8, C8, bc(R["k8"][:].rearrange("p f b -> p (f b)").unsqueeze(2), P, 3 * NB, 65), ALU.mult))
                outer("vc", ff)
                masked_query(R["bt"][:])
                step(tt(C8[:, :, 64], C8[:, :, 64], ff, ALU.add))
                sig(tt(C8[:, :, 0:64], C8[:, :, 0:64], tmp, ALU.add), "c8_made")
                n8, d8 = R["n8"], R["d8"]
                for s in range(2):
                    made(v, li, "co", s)
                    free(v.tensor_copy(n8[:, s:5:2, :],
                                       bank("co", s)[0:NB, 0:65 * (3 - s)].rearrange("b (h d) -> b h d", d=65)),
                         li, "co", s)
                step(stt(d8[:], n8[:, :, 64], -1.0, n8[:, :, 64], ALU.mult, ALU.max))
                step(tt(d8[:], d8[:], R["e8"][:], ALU.max))
                step(v.reciprocal(d8[:], d8[:]))
                step(tt(R["obs"][:, 5:10, :], n8[:, :, 0:64], bc(d8[:].unsqueeze(2), NB, 5, 64), ALU.mult))
                step(tt(R["sq8"][:], R["obs"][:], R["obs"][:], ALU.mult))
                sig(v.tensor_reduce(R["s10"][:], R["sq8"][:], AX, ALU.add), "obs_ms")
                v.wait_ge(S("obs_rms"), li + 1)
                sig(tt(R["obs"][:], R["obs"][:], bc(R["s10"][:].unsqueeze(2), NB, 10, 64), ALU.mult), "obs_normed")
                made(v, li, "fx")
                fx = bank("fx")[:, 0:64].rearrange("p (m b) -> p m b", b=NB)
                step(tt(R["fx"][:], fx[:, 0:5, :], bc(par(li, PR_ON, 5).unsqueeze(2), P, 5, NB), ALU.mult))
                step(tt(proj[:, TG:TG + 5, SEQ:T], proj[:, TG:TG + 5, SEQ:T], R["fx"][:], ALU.mult))
                free(v.tensor_copy(proj[:, TSQ:TSQ + 3, SEQ:T], fx[:, 5:8, :]), li, "fx")

            v.wait_ge(const_in, 80)
            p0, p1 = par(0, PR_LB, 3), par(1, PR_LB, 3)
            step(tt(lbt[:, 2, :], p0, p1, ALU.max))
            step(tt(lbt[:, 0, :], p0, lbt[:, 2, :], ALU.subtract))
            sig(tt(lbt[:, 1, :], p1, lbt[:, 2, :], ALU.subtract), "lb_centred")
            v.wait_ge(S("lb_exp"), 1)
            step(tt(lbt[:, 3, :], lbt[:, 0, :], lbt[:, 1, :], ALU.add))
            step(v.reciprocal(lbt[:, 3, :], lbt[:, 3, :]))
            step(tt(lbt[:, 2, :], lbt[:, 1, :], lbt[:, 3, :], ALU.mult))
            step(ts(lbt[:, 3, :], lbt[:, 2, :], -1.0, 1.0, ALU.mult, ALU.add))

            for li in range(2):
                norm(2 * li)
                for n in range(3):
                    v.wait_ge(unit_done, U_IN[li] + n + 1)
                    v.tensor_copy(halves(proj[:, n, :]), part(U_IN[li] + n)).then_inc(proj_read, 1)
                with v.Fori(0, (NT - 3) // 6) as i:
                    for n in range(6):
                        u = U_IN[li] + 3 + n
                        v.wait_ge(unit_done, i * 6 + (u + 1))
                        dst = proj[:, bass.ds(i * 6 + (3 + n), 1), :].rearrange("p o (s t) -> p (o s) t", s=2)
                        v.tensor_copy(dst, part(u)).then_inc(proj_read, 1)
                window(li)
                hgrn(li)
                mlstm(li)
                sample(li)
                for n in range(KD):
                    v.wait_ge(unit_done, U_OUT[li] + n + 1)
                    x = halves(xT[:, n, :])
                    tt(x, part(U_OUT[li] + n), x, ALU.add).then_inc(x_updated, 1)
                norm(2 * li + 1)
                if li == 1:
                    v.wait_ge(rt_done, 1)
                    bump(ts(halves(lg[:]), psum[0:8, 6:8, 0:H2], par(1, PR_RB, 1, 8), None, ALU.add), rt_read, v)
                    step(v.memset(rl[:], 0.0))
                    v.wait_ge(rt_done, 2)
                    step(v.tensor_copy(rl[:, 0:4, :], psum[:, 6, 0:32].rearrange("p (t e) -> p t e", e=8)))
                    step(v.tensor_copy(rl[0:8, 4, :], psum[0:8, 6, 32:40]))
                    step(v.tensor_reduce(rm[:], rl[:], AX, ALU.max))
                    sig(tt(re[:], rl[:], bc(rm[:].unsqueeze(2), P, 5, 8), ALU.subtract), "rt_centred")
                    for t in range(5):
                        other = bc(rl[:, t, :].unsqueeze(1), P, 8, 8)
                        mine = bc(rl[:, t, :].unsqueeze(2), P, 8, 8)
                        step(tt(c1[:, 8 * t:8 * t + 8, :], other, mine, ALU.is_gt))
                        step(tt(c2[:, 8 * t:8 * t + 8, :], other, mine, ALU.is_equal))
                        step(tt(c2[:, 8 * t:8 * t + 8, :], c2[:, 8 * t:8 * t + 8, :],
                                K(C_LT, 64).rearrange("p (e j) -> p e j", j=8), ALU.mult))
                    step(tt(c1[:], c1[:], c2[:], ALU.add))
                    step(v.tensor_reduce(rk[:], c1[:], AX, ALU.add))
                    step(ts(rk[:], rk[:], TOP_K - 0.5, None, ALU.is_lt))
                    v.wait_ge(S("rt_exp"), 1)
                    re2 = re[:].rearrange("p t e -> p (t e)")
                    step(tt(re2, re2, rk[:], ALU.mult))
                    step(v.tensor_reduce(rm[:], re[:], AX, ALU.add))
                    step(v.reciprocal(rm[:], rm[:]))
                    bump(tt(re[:], re[:], bc(rm[:].unsqueeze(2), P, 5, 8), ALU.mult), rt_read, v)
                    v.wait_ge(rt_done, 3)
                    step(v.tensor_copy(gT[:, 0:SEQ], psum[0:8, 7, :]))
                    bump(v.tensor_copy(gT[:, SEQ:T], psum[0:8, 6, 0:NB]), rt_read, v)
                    for e in range(8):
                        v.wait_ge(rt_done, 4 + e)
                        bump(v.tensor_copy(halves(gb[:, e, :]), psum[:, 6:8, 0:H2]), rt_read, v)
                with v.Fori(0, NEX[li]) as e:
                    def hidden_lo(j):
                        v.wait_ge(hh_made, e * KF + (G_FF[li] + j + 1))
                        tt(hl[:, j, :], h32[:, j % 2, :], hh[:, j, :].bitcast(F32), ALU.subtract).then_inc(hl_made, 1)

                    for j in range(KF):
                        v.wait_ge(unit_done, e * UPE + (U_FF[li] + 2 * j + 2))
                        v.wait_ge(gate_read, e * KF + (G_FF[li] + j + 1))
                        if j >= 2:
                            v.wait_ge(hl_made, e * KF + (G_FF[li] + j - 1))
                        tt(halves(h32[:, j % 2, :]), part(U_FF[li] + 2 * j + 1), halves(sg[:, j % 2, :]), ALU.mult
                           ).then_inc(up_read, 1)
                        if j:
                            hidden_lo(j - 1)
                    hidden_lo(KF - 1)
                    v.wait_ge(hl_made, e * KF + (G_FF[li] + KF))
                    for m in range(KD):
                        u = U_FF[li] + 2 * KF + m
                        v.wait_ge(unit_done, e * UPE + (u + 1))
                        x = halves(xT[:, m, :])
                        if li == 0:
                            tt(x, part(u), x, ALU.add).then_inc(x_updated, 1)
                        else:
                            y = halves(ytmp[:, m % 2, :])
                            gate = gb[:, bass.ds(e, 1), :].rearrange("p o (s t) -> p (o s) t", s=2)
                            if m >= 2:
                                v.wait_ge(x_updated, e * KD + (X_OUT[li] + m - 1))
                            tt(y, part(u), gate, ALU.mult).then_inc(y_scaled, 1)
                            v.wait_ge(y_scaled, e * KD + (m + 1))
                            tt(x, x, y, ALU.add).then_inc(x_updated, 1)
                    v.wait_ge(x_updated, e * KD + (X_OUT[li] + KD))
            norm(4)


IN_SHAPES = {
    "x": [P, KD, T], "cst": [P, C_END], "lvm": [P, LVL + 1, P], "prm": [P, 2, PR_END], "bd": [P, 2, 2, 3, P],
    "cbuf": [P, 2, 3, CONV - 1, NB], "w_in": [2, NT, P, KD * P], "w_out": [2, KD, P, KD * P],
    "ffn_gu": [2, 2 * KF, P, KD * P], "ffn_dn": [2, KD, P, KF * P],
    "moe_gu": [8, 2 * KF, P, KD * P], "moe_dn": [8, KD, P, KF * P], "rw": [P, KD * 8],
    "ck": [2, P, 3, NB, 256], "hgrn_in": [2, P, 3 * NB * 64], "mlstm_in": [2, P, 3 * NB * 65], "m_in": [2, 5, NB],
    "cache0": [2, NB, WB[0], 2, P], "cache1": [2, NB, WB[1], 2, P], "cache2": [2, NB, WB[2], 2, P],
}
OUT_SHAPES = {
    "y": [P, KD, T], "hgrn_p": [2, P, 3, 64], "hgrn_s": [2, P, 3 * NB * 64], "mlstm_p": [2, P, 3, 65],
    "mlstm_s": [2, P, 3 * NB * 65], "m_p": [2, 5, 1], "m_s": [2, 5, NB], "mu_out": [2, P, 3, 3], "conv_s": [2, P, 3, 3, NB],
    "kv_p": [2, P, 6, SEQ], "cache0_s": [2, NB, WB[0], 2, P], "cache1_s": [2, NB, WB[1], 2, P],
    "cache2_s": [2, NB, WB[2], 2, P],
}


def constants(np):
    c = np.zeros((P, C_END), np.float32)
    n = np.arange(P)
    c[:, C_ID:C_ID + P] = np.eye(P)
    c[:, C_ONE:C_ONE + P] = 1.0
    q, k = n[:, None], n[None, :]
    c[:, C_NEGC:C_NEGC + P] = np.where(k >= q, 0.0, NEG)
    causal = np.where(k <= q, 0.0, NEG)
    c[:, C_NEG0:C_NEG0 + 256] = np.concatenate([np.full((P, P), NEG), causal], 1)
    c[:, C_NEG1:C_NEG1 + 256] = np.concatenate([np.where(k >= q, 0.0, NEG), causal], 1)
    c[:, C_NEGT:C_NEGT + P] = causal
    c[:, C_NEGR:C_NEGR + P] = np.where((q % 4 == k % 4) & (k <= q), 0.0, NEG)
    for f in range(3):
        for h in range(2):
            if 2 * f + h < 5:
                c[2 * f + h, C_HP + f * P + 64 * h:C_HP + f * P + 64 * h + 64] = 1.0
    c[:, C_DM:C_DM + 2 * NB * NB] = np.tile(np.eye(NB).reshape(1, -1), (P, 2))
    for h in range(2):
        c[h, C_S2 + 64 * h:C_S2 + 64 * h + 64] = 1.0
    c[:, C_RST:C_RST + SEQ] = (np.arange(SEQ) % CH != 0)[None, :]
    c[:, C_EPS] = EPS
    e = np.arange(8)
    c[:, C_LT:C_LT + 64] = (e[None, :] < e[:, None]).reshape(1, -1)
    x = n[:, None] ^ n[None, :]
    m = np.zeros((P, LVL + 1, P), np.int32)
    for l in range(LVL):
        half = CH >> (l + 1)
        m[:, l, :] = (x >= half) & (x < 2 * half) & (n[:, None] < n[None, :])
    m[:, LVL, :] = x == 0
    return c, m


def kernel(**inputs):
    import numpy as np
    import concourse.bacc as bacc
    from concourse.bass_utils import run_bass_kernel_spmd

    v = {k: np.asarray(x) for k, x in inputs.items()}
    f32 = np.float32

    def fm(x):
        y = x.reshape(x.shape[:-1] + (-1, P))
        return np.moveaxis(y, -1, 0)

    def pad(x, n):
        return np.concatenate([x, np.zeros(x.shape[:-1] + (n - x.shape[-1],), f32)], -1)

    def ktile(w):
        k, m = w.shape
        return w.reshape(k // P, P, m // P, P).transpose(2, 1, 0, 3).reshape(m // P, P, k)

    d = {}
    d["cst"], d["lvm"] = constants(np)
    x = np.concatenate([v["x_prompt"][0], v["x_sample"][:, 0]], 0)
    d["x"] = x.T.reshape(KD, P, T).transpose(1, 0, 2)
    prm = np.zeros((P, 2, PR_END), f32)
    bd = np.zeros((P, 2, 2, 3, P), f32)
    w_in = np.zeros((2, NT, P, KD * P), f32)
    z64 = np.zeros((D, 64), f32)
    for li in range(2):
        prm[:, li, PR_G1:PR_G1 + KD] = fm(v["norm1_g"][li])
        prm[:, li, PR_G2:PR_G2 + KD] = fm(v["norm2_g"][li])
        prm[:, li, PR_GF:PR_GF + KD] = fm(v["final_norm_g"])
        prm[:, li, PR_ON:PR_ON + 5] = fm(np.concatenate([v["hgrn_onorm_g"][li], v["mlstm_onorm_g"][li]]))
        cw = fm(pad(v["mlstm_conv_w"][li], 384))
        prm[:, li, PR_CW:PR_CW + 12] = cw.transpose(0, 2, 1).reshape(P, 12)
        prm[:, li, PR_CB:PR_CB + 3] = fm(pad(v["mlstm_conv_b"][li], 384))
        prm[:, li, PR_LB:PR_LB + 3] = fm(pad(v["hgrn_lb_param"][li], 384))
        prm[64:69, li, PR_IB] = v["mlstm_ig_b"][li]
        prm[96:101, li, PR_FB] = v["mlstm_fg_b"][li]
        prm[0:8, li, PR_RB] = v["moe_router_b"][0]
        for s, name in enumerate(("mlstm_wq", "mlstm_wk")):
            for h in range(5):
                r = 64 * (h % 2)
                bd[r:r + 64, li, s, h // 2, r:r + 64] = v[name][li, h]
        w = v["w_in"][li]
        hq, hf, hi, hg, mu, mv, mo = (w[:, 320 * n:320 * (n + 1)] for n in range(7))
        gates = np.zeros((D, 64), f32)
        gates[:, 0:5] = w[:, 2240:2245]
        gates[:, 32:37] = w[:, 2245:2250]
        cols = np.concatenate([hq, gates, hf, hi[:, 256:320], hi[:, 0:256], hg, mo, mu, mv[:, 256:320], mv[:, 0:256],
                               w[:, 2250:3402]], 1)
        w_in[li] = ktile(cols)
    d["prm"], d["bd"], d["w_in"] = prm, bd, w_in
    cb = fm(pad(v["state_mlstm_conv"], 384))
    d["cbuf"] = cb.transpose(0, 1, 4, 3, 2)
    d["w_out"] = np.stack([ktile(v["w_out"][li]) for li in range(2)])

    def gu(wg, wu):
        g, u = ktile(wg), ktile(wu)
        return np.stack([g, u], 1).reshape(2 * KF, P, KD * P)

    d["ffn_gu"] = np.stack([gu(v["ffn_w_gate"][0][:, e * EFF:(e + 1) * EFF], v["ffn_w_up"][0][:, e * EFF:(e + 1) * EFF])
                            for e in range(2)])
    d["ffn_dn"] = np.stack([ktile(v["ffn_w_down"][0][e * EFF:(e + 1) * EFF]) for e in range(2)])
    d["moe_gu"] = np.stack([gu(v["moe_w_gate"][0, e], v["moe_w_up"][0, e]) for e in range(8)])
    d["moe_dn"] = np.stack([ktile(v["moe_w_down"][0, e]) for e in range(8)])
    d["rw"] = v["moe_router_w"][0].reshape(KD, P, 8).transpose(1, 0, 2).reshape(P, KD * 8)
    ck = np.zeros((2, P, 3, NB, 256), f32)
    for g, (name, dil) in enumerate((("cache_swa_w128", 1), ("cache_swa_w512", 4), ("cache_swa_w2048", 16))):
        c = v[name].reshape(2, NB, WB[g], 256)
        d[f"cache{g}"] = c.reshape(2, NB, WB[g], 2, P)
        ck[:, 0:ROWS_G[g], g] = c[:, :, ::dil].transpose(0, 2, 1, 3)
    d["ck"] = ck

    def heads_in(s):
        s = np.concatenate([s, np.zeros_like(s[:, :, 0:1])], 2)
        w = s.shape[-1]
        return s.reshape(2, NB, 3, 2, 64, w).transpose(0, 3, 4, 2, 1, 5).reshape(2, P, 3 * NB * w)

    d["hgrn_in"] = heads_in(v["state_hgrn"])
    d["mlstm_in"] = heads_in(np.concatenate([v["state_mlstm_C"], v["state_mlstm_n"][..., None]], -1))
    d["m_in"] = v["state_mlstm_m"].transpose(0, 2, 1)

    nc = bacc.Bacc("TRN2", target_bir_lowering=False, num_devices=1)
    arrays, args = {}, {}
    for name, shape in IN_SHAPES.items():
        arr = np.ascontiguousarray(d[name])
        assert list(arr.shape) == shape, (name, arr.shape, shape)
        arrays["in_" + name] = arr
        args[name] = nc.dram_tensor("in_" + name, arr.shape, mybir.dt.from_np(arr.dtype), kind="ExternalInput").ap()
    for name, shape in OUT_SHAPES.items():
        args[name] = nc.dram_tensor("out_" + name, tuple(shape), F32, kind="ExternalOutput").ap()
    program(nc, args)
    res = run_bass_kernel_spmd(nc, [arrays], core_ids=[0]).results[0]
    o = {name: np.asarray(res["out_" + name]) for name in OUT_SHAPES}

    y = o["y"].transpose(2, 1, 0).reshape(T, D)

    def heads_out(s, n, w):
        s = s.reshape(2, 2, 64, 3, n, w).transpose(0, 4, 3, 1, 2, 5).reshape(2, n, 6, 64, w)
        return np.ascontiguousarray(s[:, :, 0:5])

    C_p, C_s = heads_out(o["mlstm_p"], 1, 65), heads_out(o["mlstm_s"], NB, 65)
    mu = o["mu_out"].transpose(0, 3, 2, 1).reshape(2, 3, 384)[:, :, 0:320]
    conv_s = o["conv_s"].transpose(0, 4, 3, 2, 1).reshape(2, NB, 3, 384)[..., 0:320]
    kv = o["kv_p"].reshape(2, P, 2, 3, SEQ).transpose(0, 3, 4, 2, 1)
    out = [y[None, 0:SEQ], y[SEQ:, None], heads_out(o["hgrn_p"], 1, 64), heads_out(o["hgrn_s"], NB, 64),
           C_p[..., 0:64], C_s[..., 0:64], C_p[..., 64], C_s[..., 64],
           o["m_p"].transpose(0, 2, 1), o["m_s"].transpose(0, 2, 1), mu[:, None], conv_s]
    for g, w in enumerate((128, 512, 512)):
        out.append(kv[:, g, SEQ - w:].reshape(2, 1, w, 2, 2, 64))
        out.append(o[f"cache{g}_s"].reshape(2, NB, WB[g], 2, 2, 64))
    return tuple(np.ascontiguousarray(x) for x in out)
```

```python
from contextlib import ExitStack

import concourse.bass as bass
from concourse import mybir

F32 = mybir.dt.float32
F32R = mybir.dt.float32r
I32 = mybir.dt.int32
ALU = mybir.AluOpType
ACT = mybir.ActivationFunctionType
AX = mybir.AxisListType.X

P = 128
SEQ = 512
NB = 8
T = SEQ + NB
H2 = T // 2
D = 1024
KD = D // P
CH = 128
NC = SEQ // CH
NT = 27
EFF = 1408
KF = EFF // P
UPE = 2 * KF + KD
RAW = 3
SPL = 2
NPS = 3
LVL = 7
CONV = 4
WB = (128, 256, 256)
TOP_K = 2
SLOTS = 160
NPASS = -(-T // SLOTS)
WIDE = 256
RWX = 6
HIX = 3
WHOLE = (0, 24)
SPARE = 8
EPS = 1e-6
NEG = -1e30
TQ, TF, TI, TG, TU, TV, TSQ, TSK, TSV = 0, 3, 6, 8, 13, 16, 18, 21, 24
MIXT = [8, 9, 10, 11, 12, 18, 19, 20]
ROWS_G = (128, 64, 16)
C_ID, C_ONE, C_NEGC, C_NEG0, C_NEG1, C_NEGR, C_NEGT, C_HP, C_DM, C_S2, C_RST, C_LT, C_EPS, C_VM, C_TRI, C_IOTA, C_END = \
    0, 128, 256, 384, 640, 896, 1024, 1152, 1536, 1664, 1792, 2304, 2368, 2369, 2374, 2502, 2502 + WIDE
PR_G1, PR_G2, PR_ON, PR_CW, PR_CB, PR_LB, PR_IB, PR_FB, PR_RB, PR_GF, PR_END = 0, 8, 16, 21, 33, 36, 39, 40, 41, 42, 50


def mixer_jobs():
    jobs = [("tm", i) for i in range(3)] + [("vt", g) for g in range(3)]

    def sc(n):
        return [("sc", n, p) for p in range(2 if n < 2 else 1)]

    def pt(n):
        return [("pt", n, p) for p in range(2 if n < 2 else 1)]

    jobs += sc(0) + sc(1)
    for n in range(6):
        jobs += pt(n)
        if n + 2 < 6:
            jobs += sc(n + 2)
        jobs += [("pv", n)]
        if n % 2:
            jobs += [("st", n // 2)]
    jobs += [("lt", g) for g in range(3)] + [("al", g) for g in range(3)]
    jobs += [("qb", g, p) for g in range(3) for p in range(2)] + [("sct", g) for g in range(3)]
    jobs += [("ppt",), ("spv",)]
    jobs += [("hv", c) for c in range(NC)] + [("th", i) for i in range(2)]
    for c in range(NC):
        jobs += [("kh", c), ("su", c)]
    jobs += [("at", h, l) for l in [LVL] + list(range(LVL)) for h in range(5)]
    jobs += [("ho", 0), ("ho", 1), ("ho", 2), ("ho", 3), ("mt", 0), ("ho", 4), ("mt", 1)]
    jobs += [("mv", c) for c in range(NC)]
    jobs += [("mq", f, s) for f in range(3) for s in range(4)]
    jobs += [("rt",), ("ac",)]
    for c in range(NC):
        jobs += [("kt", c), ("cu", c)]
    jobs += [("md", 0), ("mqk", 0)]
    for h in range(5):
        if h + 1 < 5:
            jobs += [("md", h + 1), ("mqk", h + 1)]
        jobs += [("mi", h), ("mo", h)]
        jobs += {2: [("mt", 2)], 4: [("mt", 3), ("mt", 4)]}.get(h, [])
    jobs += [("vb", f) for f in range(3)] + [("so", 0), ("so", 1)]
    jobs += [("rs",), ("aw",)] + [("vc", f) for f in range(3)] + [("co", 0), ("co", 1)] + [("fx",)]
    return jobs


def program(nc, a):
    jobs = mixer_jobs()
    NJ = len(jobs)
    JOB = {k: n for n, k in enumerate(jobs)}
    uses = [len(range(b, NJ, 8)) for b in range(8)]
    U_IN = [0, NT + KD + 2 * UPE]
    U_OUT = [u + NT for u in U_IN]
    U_FF = [u + KD for u in U_OUT]
    NEX = [2, 8]
    X_OUT = [KD, 4 * KD]
    X_FF = [3 * KD, 13 * KD]
    G_FF = [0, 2 * KF]
    with ExitStack() as ctx:
        def sem(name):
            return ctx.enter_context(nc.semaphore(name))

        top = [16512]
        END = 229344

        def at(name, shape, dt=F32, off=None):
            n = 4
            for s in shape[1:]:
                n *= s
            n = (n + 31) // 32 * 32
            if off is None:
                off = top[0]
                top[0] += n
            assert off + n <= END, (name, off + n - END)
            return nc.alloc_sbuf_tensor_at(name, shape, dt, offset=off), off + n

        xT, _ = at("xT", [P, KD, T])
        xn_off = top[0]
        xnh, _ = at("xnh", [P, KD, T], F32R)
        xnl, _ = at("xnl", [P, KD, T], F32R)
        xn_end = top[0]
        ring_off = top[0]
        wraw = [at(f"wraw{n}", [P, KF * P])[0] for n in range(RAW)]
        whi = [at(f"whi{n}", [P, KF * P], F32R)[0] for n in range(SPL)]
        wlo = [at(f"wlo{n}", [P, KF * P], F32R)[0] for n in range(SPL)]
        cst, _ = at("cst", [P, C_END])
        lvm, _ = at("lvm", [P, LVL + 1, P], I32)
        prm, _ = at("prm", [P, 2, PR_END])
        bd, _ = at("bd", [P, 2, 2, 3, P])
        cbuf, _ = at("cbuf", [P, 2, 3, CONV - 1, NB])
        lbt, _ = at("lbt", [P, 4, 3])
        osw, _ = at("osw", [NB, 3 * P])
        mkr, _ = at("mkr", [P, 2, P], F32R)
        proj_off = top[0]
        proj, _ = at("proj", [P, NT, T])
        scr_off = top[0]

        o = proj_off
        hh, o = at("hh", [P, KF, T], F32R, o)
        hl, o = at("hl", [P, KF, T], F32R, o)
        sg, o = at("sg", [P, 2, T], F32, o)
        h32, o = at("h32", [P, 2, T], F32, o)
        assert o <= scr_off
        o = scr_off
        sqb, o = at("sqb", [P, 2, T], F32, o)
        n32, o = at("n32", [P, 2, T], F32, o)
        rw, o = at("rw", [P, KD * 8], F32, o)
        rwh, o = at("rwh", [P, KD * 8], F32R, o)
        rwl, o = at("rwl", [P, KD * 8], F32R, o)
        lg, o = at("lg", [8, T], F32, o)
        rl, o = at("rl", [P, 5, 8], F32, o)
        re, o = at("re", [P, 5, 8], F32, o)
        rk, o = at("rk", [P, 40], F32, o)
        rsel, o = at("rsel", [P, 5, 8], F32, o)
        rm, o = at("rm", [P, 5], F32, o)
        c1, o = at("c1", [P, 40, 8], F32, o)
        c2, o = at("c2", [P, 40, 8], F32, o)
        pos, o = at("pos", [P, 5, SPARE + 1], F32, o)
        ghl, o = at("ghl", [P, 5, SPARE + 1, 2], F32R, o)
        tot, o = at("tot", [P, 8], F32, o)
        flag, o = at("flag", [P, 1], I32, o)
        rstd, o = at("rstd", [P, T], F32, o)
        sel, o = at("sel", [P, 5, WIDE], F32R, o)
        selT, o = at("selT", [P, 2, T], F32R, o)
        ge, o = at("ge", [P, 5, 2], F32R, o)
        gslot, o = at("gslot", [P, 2], F32, o)
        gs2, o = at("gs2", [P, 2, 2], F32, o)
        esg, o = at("esg", [P, 2, SLOTS], F32, o)
        e32, o = at("e32", [P, 2, SLOTS], F32, o)
        g32, o = at("g32", [P, 2, SLOTS], F32, o)
        u32, o = at("u32", [P, 2, SLOTS], F32, o)
        slots = [ring_off + n * KF * P * 4 for n in range(7)] + [o, scr_off]
        assert o + KF * P * 4 <= END and KF * P <= 4 * T
        xraw = [at(f"xraw{n}", [P, KF * P], F32, slots[n])[0] for n in range(RWX)]
        xlo = [at(f"xlo{n}", [P, KF * P], F32R, slots[n])[0] for n in range(RWX)]
        xhi = [at(f"xhi{n}", [P, KF * P], F32R, slots[RWX + n])[0] for n in range(HIX)]
        o = proj_off
        xth, o = at("xth", [P, 5, D], F32R, o)
        xtl, o = at("xtl", [P, 5, D], F32R, o)
        ehl, o = at("ehl", [P, KF, 2 * SLOTS], F32R, o)
        assert o <= scr_off
        o = xn_off
        yh, o = at("yh", [P, 2, D], F32R, o)
        yl, o = at("yl", [P, 2, D], F32R, o)
        xg, o = at("xg", [P, KD, 2 * SLOTS], F32R, o)
        yf, o = at("yf", [P, KD, SLOTS], F32, o)
        assert o <= xn_end
        yout = at("yout", [P, KD, T], F32, proj_off)[0]

        A = {}
        o = scr_off
        for name, shape in (("vt", [P, 3, 4, P]), ("pb", [P, 2, 1024]), ("ptb", [P, 2, 1024]), ("os", [P, 2, 4, P]),
                            ("mx", [P, 6, 4]), ("nm", [P, 6, 4]), ("den", [P, 6, 4]), ("rd", [P, 6, 4]),
                            ("lse", [P, 6, 4]), ("lr", [2, 3, SEQ]), ("lm", [2, SEQ]), ("tms", [NB, 9 * P]),
                            ("scr", [P, 3, 2, NB]), ("smx", [NB, 6]), ("sden", [NB, 6]), ("slse", [NB, 6]),
                            ("sm2", [NB, 2])):
            if name == "pb":
                probs_off = o
            A[name], o = at("a_" + name, shape, F32, o)
        o = probs_off
        for name, shape in (("ss", [NB, 6, 129]), ("sp", [NB, 6, 129]), ("pm", [P, 6, NB, NB])):
            A[name], o = at("a_" + name, shape, F32, o)
        o = xn_off
        for name, shape in (("ck", [P, 3, NB, 256]), ("dq", [NB, NB, P]), ("pr", [P, 512]), ("own", [NB, 6, 64])):
            A[name], o = at("a_" + name, shape, F32, o)
        assert o <= xn_end

        R = {}
        o = xn_off
        for name in ("kh", "bt", "ee", "w0", "w1"):
            R[name], o = at("r_" + name, [P, 3, T], F32, o)
        assert o <= xn_end
        o = scr_off
        R["dw"], _ = at("r_dw", [P, 2, SEQ], F32, o)
        R["qd"], _ = at("r_qd", [P, 2, SEQ], F32, o + 2 * SEQ * 4)
        o2 = o
        for name, shape in (("obs", [NB, 10, 64]), ("sq8", [NB, 10, 64]), ("n8", [NB, 5, 65]), ("s10", [NB, 10]),
                            ("e8", [NB, 5]), ("d8", [NB, 5]), ("fx", [P, 5, NB])):
            R[name], o2 = at("r_" + name, shape, F32, o2)
        for name, shape in (("att", [P, 5, SEQ]), ("vh", [P, NC, 384]), ("kt", [P, 2, 384]),
                            ("sall", [P, NC + 1, 3, 64]), ("rows", [P, SEQ]), ("dl", [P, 3, NC]),
                            ("call", [P, NC + 1, 3, 65]),
                            ("num", [P, NC, 65]), ("t1", [P, NC, 65]), ("ec", [P, 4, NC, 5]), ("acb", [P, NC, 3]),
                            ("ob", [P, 2, NC, P]), ("sqo", [P, NC, P]), ("ss2", [P, 8]), ("rden", [P, NC]),
                            ("thm", [NB, 6 * P]), ("ff", [P, 3, NB]), ("k8", [P, 3, NB]), ("qm8", [P, 3, NB, NB]),
                            ("aw", [P, 3, 2 * NB]), ("sc8", [NB, 48])):
            if name == "vh":
                R["va"], _ = at("r_va", [P, NC, 5, 65], F32, o)
            if name == "call":
                R["cvt"], _ = at("r_cvt", [P, T], F32, o)
            if name == "num":
                R["cv2"], _ = at("r_cv2", [P, T], F32, o)
            if name == "kt":
                R["kw"], _ = at("r_kw", [P, 2, 6, 64], F32, o)
            if name == "ob":
                R["e2"], _ = at("r_e2", [P, 3, SEQ], F32, o)
            R[name], o = at("r_" + name, shape, F32, o)

        psum = ctx.enter_context(nc.psum_tensor("psum", [P, 8, 512], F32))

        const_in, cst_in, x_in = sem("const_in"), sem("cst_in"), sem("x_in")
        raw_in = [sem(f"raw_in{n}") for n in range(RAW)]
        xraw_in = [sem(f"xraw_in{n}") for n in range(RWX)]
        hi_made, lo_made, unit_done = sem("hi_made"), sem("lo_made"), sem("unit_done")
        proj_read, x_updated, gate_read, up_read = sem("proj_read"), sem("x_updated"), sem("gate_read"), sem("up_read")
        hh_made, hl_made = sem("hh_made"), sem("hl_made")
        lo_pool, lo_dve = sem("lo_pool"), sem("lo_dve")
        (sel_made, gathered, xg_made, selT_made, turned_sel, gsl, yf_made, yf_turned, yh_made, yl_made, scattered, xt_turned,
         xt_made) = (sem(n) for n in ("sel_made", "gathered", "xg_made", "selT_made", "turned_sel", "gsl", "yf_made",
                                      "yf_turned", "yh_made", "yl_made", "scattered", "xt_turned", "xt_made"))
        sq_made, sq_used, rstd_made = sem("sq_made"), sem("sq_used"), sem("rstd_made")
        n32_made, nh_made, (nl_pool, nl_dve) = sem("n32_made"), sem("nh_made"), (sem("nl_pool"), sem("nl_dve"))
        job_done = sem("job_done")
        bank_read = [sem(f"bank_read{b}") for b in range(8)]
        mixh_made, mixl_pool, mixl_dve = sem("mixh_made"), sem("mixl_pool"), sem("mixl_dve")
        dve_step, act_step, pool_step = sem("dve_step"), sem("act_step"), sem("pool_step")
        cache_in, state_in, out_dma, shift_dma, window_dma = (
            sem(n) for n in ("cache_in", "state_in", "out_dma", "shift_dma", "window_dma"))
        rw_in, rw_hi, rw_lo, rt_done, rt_read, y_made = (
            sem(n) for n in ("rw_in", "rw_hi", "rw_lo", "rt_done", "rt_read", "y_made"))
        named = {}

        def S(name):
            if name not in named:
                named[name] = sem(name)
            return named[name]

        counts = {}

        def bump(ins, s, eng):
            counts[s.name] = counts.get(s.name, 0) + 1
            ins.then_inc(s, 1)
            eng.wait_ge(s, counts[s.name])

        def K(c0, n, rows=P, r0=0):
            return cst[r0:r0 + rows, c0:c0 + n]

        ident = K(C_ID, P)

        def par(li, c, n=1, rows=P, r0=0):
            return prm[r0:r0 + rows, li, c:c + n]

        def bc(ap, *shape):
            return ap.broadcast_to(list(shape))

        def flat(tile0, cols):
            return proj[:, tile0:tile0 + 3, :].rearrange("p f t -> p (f t)")[:, 0:cols]

        def perm(g, tile, i, r0=0, rows=P):
            v = proj[r0:r0 + rows, tile, 0:SEQ]
            if g == 0:
                return v[:, i * P:(i + 1) * P]
            return v.rearrange("p (j r) -> p r j", r=4)[:, i, :]

        def natural(g, ap):
            return ap if g == 0 else ap.rearrange("p (j r) -> p r j", r=4)

        def grouped(g, ap):
            return ap if g == 0 else ap.rearrange("p (r j) -> p r j", r=4)

        def bank(*key):
            return psum[:, JOB[key] % 8, :]

        def made(eng, li, *key):
            eng.wait_ge(job_done, li * NJ + JOB[key] + 1)

        def taken(eng, li, *key):
            j = JOB[key]
            eng.wait_ge(bank_read[j % 8], li * uses[j % 8] + j // 8 + 1)

        def release(eng, ins, li, *key):
            ins.then_inc(bank_read[JOB[key] % 8], 1)
            taken(eng, li, *key)

        def split_lo(eng, u, cols, made_):
            eng.wait_ge(hi_made, u + 1)
            eng.tensor_tensor(wlo[u % SPL][:, 0:cols], wraw[u % RAW][:, 0:cols],
                              whi[u % SPL][:, 0:cols].bitcast(F32), ALU.subtract).then_inc(made_, 1)

        def expert_lo(eng, n, i, made_, c0=0, c1=None):
            c1 = lo_cols(n)[1] if c1 is None else c1
            eng.wait_ge(hi_made, i * UPE + (U_FF[1] + n + 1))
            eng.tensor_tensor(xlo[n % RWX][:, c0:c1], xraw[n % RWX][:, c0:c1],
                              xhi[n % HIX][:, c0:c1].bitcast(F32), ALU.subtract).then_inc(made_, 1)

        def lo_cols(n):
            cols = (KD if n < 2 * KF else KF) * P
            return (0 if n % 3 else cols if n in WHOLE else cols * 5 // 8), cols

        def wait_expert_lo(eng, n, i):
            if n % 3 == 0:
                eng.wait_ge(lo_pool, i * (UPE // 3) + (KD // 2 + n // 3 + 1))
            if n not in WHOLE:
                eng.wait_ge(lo_dve, i * (UPE - len(WHOLE)) + (KD // 2 + n + 1 - sum(w < n for w in WHOLE)))

        def conv_out(f):
            return proj[:, TI + f, :] if f < 2 else R["cv2"][:]

        def v_col(h):
            return h * 64 if h < 4 else 320

        def epart(n):
            return psum[:, 2 * ((U_FF[1] + n) % NPS), 0:2 * SLOTS]

        def two(n):
            return epart(n).rearrange("p (s t) -> p t s", s=2)

        def scatter_bank(m):
            return (psum[:, 1:4:2, 0:H2], psum[:, 6:8, 0:H2])[m % 2]

        def y_piece(q):
            return (P, SLOTS - P)[q // 2], q // 2, 512 * (q % 2), (1, 3, 5, 7)[q]

        def xt_piece(n):
            src, t, c = n // 10, (n // 2) % 5, 512 * (n % 2)
            return src, P if t < 4 else NB, t, c

        def part(u):
            s = 2 * (u % NPS)
            return psum[:, s:s + 2, 0:H2]

        def halves(ap):
            return ap.rearrange("p (s t) -> p s t", s=2)

        block = ctx.enter_context(nc.Block())

        @block.sync
        def _(sp):
            def load(u, src, cols, when=None):
                if when is not None or u >= RAW:
                    sp.wait_ge(lo_made, (u if when is None else when) - RAW + 1)
                sp.dma_start(wraw[u % RAW][:, 0:cols], src).then_inc(raw_in[u % RAW], 16)

            def expert(gu, dn, e, n):
                name, m, cols = (gu, n, KD * P) if n < 2 * KF else (dn, n - 2 * KF, KF * P)
                return a[name][bass.ds(e, 1), m].rearrange("o p c -> (o p) c"), cols

            for n in range(SPL):
                load(U_IN[0] + n, a["w_in"][0, n], KD * P)
            sp.dma_start(xT[:], a["x"]).then_inc(x_in, 16)
            sp.dma_start(cst[:], a["cst"]).then_inc(cst_in, 16)
            for name, dst in (("prm", prm), ("lvm", lvm), ("bd", bd), ("cbuf", cbuf)):
                sp.dma_start(dst[:], a[name]).then_inc(const_in, 16)
            for li in range(2):
                for n in range(0 if li else SPL, RAW):
                    load(U_IN[li] + n, a["w_in"][li, n], KD * P)
                with sp.Fori(0, (NT - RAW) // RAW) as i:
                    for n in range(RAW):
                        u = U_IN[li] + RAW + n
                        src = a["w_in"][li, bass.ds(i * RAW + (RAW + n), 1)].rearrange("o p c -> (o p) c")
                        load(u, src, KD * P, i * RAW + u)
                for n in range(KD):
                    if li == 1 and n >= RAW:
                        sp.wait_ge((lo_pool, lo_dve)[(n - RAW) % 2], (n - RAW) // 2 + 1)
                        sp.dma_start(wraw[(U_OUT[1] + n) % RAW][:, 0:KD * P], a["w_out"][li, n]
                                     ).then_inc(raw_in[(U_OUT[1] + n) % RAW], 16)
                    else:
                        load(U_OUT[li] + n, a["w_out"][li, n], KD * P)
                    if li == 0 and n == RAW - 1:
                        for l2 in range(2):
                            for g, w in enumerate(WB):
                                sp.dma_start(a[f"cache{g}_s"][l2, :, 0:w - 1, :, :], a[f"cache{g}"][l2, :, 1:w, :, :]
                                             ).then_inc(shift_dma, 16)
                if li == 0:
                    with sp.Fori(0, NEX[li]) as e:
                        for n in range(UPE):
                            u = U_FF[li] + n
                            src, cols = expert("ffn_gu", "ffn_dn", e, n)
                            load(u, src, cols, e * UPE + u)

            def experts(c):
                with sp.Fori(0, 8) as e:
                    p_ = c * 8 + e
                    for n in range(UPE):
                        sp.wait_ge(unit_done, p_ * UPE + (U_FF[1] + n - RWX + 1))
                        src, cols = expert("moe_gu", "moe_dn", e, n)
                        sp.dma_start(xraw[n % RWX][:, 0:cols], src).then_inc(xraw_in[n % RWX], 16)

            sp.wait_ge(unit_done, U_FF[1])
            experts(0)
            sp.wait_ge(S("flag_made"), 1)
            with sp.If(sp.value_load(flag[0:1, 0:1], min_val=0, max_val=1) > 0):
                with sp.Fori(0, NPASS - 1) as k:
                    experts(k + 1)
            sp.wait_ge(y_made, KD)
            sp.dma_start(a["y"], yout[:]).then_inc(out_dma, 16)
            sp.wait_ge(out_dma, 16)

        @block.gpsimd
        def _(pool):
            def lo(u, cols, when=None):
                pool.wait_ge(hi_made, (u if when is None else when) + 1)
                pool.tensor_tensor(wlo[u % SPL][:, 0:cols], wraw[u % RAW][:, 0:cols],
                                   whi[u % SPL][:, 0:cols].bitcast(F32), ALU.subtract).then_inc(lo_made, 1)

            def norm_lo(r):
                for k in range(0, KD, 2):
                    pool.wait_ge(nh_made, KD * r + k + 1)
                    pool.tensor_tensor(xnl[:, k, :], n32[:, k % 2, :], xnh[:, k, :].bitcast(F32),
                                       ALU.subtract).then_inc(nl_pool, 1)

            def step(ins):
                bump(ins, pool_step, pool)

            for li in range(2):
                for n in range(SPL):
                    lo(U_IN[li] + n, KD * P)
                norm_lo(2 * li)
                lo(U_IN[li] + SPL, KD * P)
                with pool.Fori(0, (NT - 3) // 6) as i:
                    for n in range(6):
                        lo(U_IN[li] + 3 + n, KD * P, i * 6 + (U_IN[li] + 3 + n))
                if li == 0:
                    for n in range(SPL):
                        lo(U_OUT[0] + n, KD * P)
                else:
                    split_lo(pool, U_OUT[1], KD * P, lo_pool)
                pool.wait_ge(S("window_end"), li + 1)
                step(pool.memset(R["att"][:], 0.0))
                step(pool.memset(R["rows"][:], 0.0))
                step(pool.memset(R["sall"][:, 0, :, :], 0.0))
                bump(pool.memset(R["acb"][:], 0.0), S("scratch_clear"), pool)
                pool.wait_ge(job_done, li * NJ + JOB[("th", 0)] + 1)
                for f in range(3):
                    mu, out = proj[:, TU + f, :], conv_out(f)

                    def tap(j):
                        return par(li, PR_CW + 4 * f + j)
                    step(pool.tensor_scalar(out, mu, tap(3), par(li, PR_CB + f), ALU.mult, ALU.add))
                    for j in range(3):
                        n = 3 - j
                        step(pool.tensor_scalar(R["cvt"][:, 0:SEQ - n], mu[:, 0:SEQ - n], tap(j), None, ALU.mult))
                        step(pool.tensor_scalar(R["cvt"][:, SEQ:T], cbuf[:, li, f, j, :], tap(j), None, ALU.mult))
                        step(pool.tensor_tensor(out[:, n:SEQ], R["cvt"][:, 0:SEQ - n], out[:, n:SEQ], ALU.add))
                        ins = pool.tensor_tensor(out[:, SEQ:T], R["cvt"][:, SEQ:T], out[:, SEQ:T], ALU.add)
                        bump(ins, S("conv_made") if f == 2 and j == 2 else pool_step, pool)
                bump(pool.memset(R["call"][:, 0, :, :], 0.0), S("call_clear"), pool)
                for m in range(0, KD, 2):
                    pool.wait_ge(mixh_made, KD * li + m + 1)
                    pool.tensor_tensor(xnl[:, m, :], proj[:, MIXT[m], :], xnh[:, m, :].bitcast(F32),
                                       ALU.subtract).then_inc(mixl_pool, 1)
                if li == 0:
                    for n in range(SPL, KD):
                        lo(U_OUT[li] + n, KD * P)
                    norm_lo(1)
                    with pool.Fori(0, NEX[0]) as e:
                        for n in range(UPE):
                            lo(U_FF[0] + n, (KD if n < 2 * KF else KF) * P, e * UPE + (U_FF[0] + n))
            for n in range(2, KD, 2):
                split_lo(pool, U_OUT[1] + n, KD * P, lo_pool)
            norm_lo(3)
            pool.wait_ge(rw_hi, 1)
            pool.tensor_tensor(rwl[:], rw[:], rwh[:].bitcast(F32), ALU.subtract).then_inc(rw_lo, 1)

            def experts(c):
                with pool.Fori(0, 8) as e:
                    for n in range(0, UPE, 3):
                        expert_lo(pool, n, c * 8 + e, lo_pool, 0, lo_cols(n)[0])

            experts(0)
            pool.wait_ge(S("flag_made"), 1)
            with pool.If(pool.value_load(flag[0:1, 0:1], min_val=0, max_val=1) > 0):
                with pool.Fori(0, NPASS - 1) as k:
                    experts(k + 1)

        @block.scalar
        def _(act):
            def step(ins):
                bump(ins, act_step, act)

            def sig(ins, name):
                bump(ins, S(name), act)

            def free(ins, li, *key):
                release(act, ins, li, *key)

            def hi(u, cols, when=None):
                slot = u % RAW
                if when is None:
                    act.wait_ge(raw_in[slot], 16 * (u // RAW + 1))
                    if u >= SPL:
                        act.wait_ge(unit_done, u - SPL + 1)
                else:
                    i, per = when
                    act.wait_ge(raw_in[slot], i * (16 * per // RAW) + 16 * (u // RAW + 1))
                    act.wait_ge(unit_done, i * per + (u - SPL + 1))
                act.copy(whi[u % SPL][:, 0:cols], wraw[slot][:, 0:cols]).then_inc(hi_made, 1)

            def norm(r):
                for k in range(KD):
                    if r == 0:
                        act.wait_ge(x_in, 16)
                    else:
                        act.wait_ge(x_updated, [0, X_OUT[0], X_FF[0], X_OUT[1], X_FF[1]][r] - KD + k + 1)
                    if KD * r + k >= 2:
                        act.wait_ge(sq_used, KD * r + k - 1)
                    act.activation(sqb[:, k % 2, :], xT[:, k, :], ACT.Square).then_inc(sq_made, 1)
                act.wait_ge(cst_in, 16)
                act.wait_ge(sq_used, KD * (r + 1))
                step(act.activation(halves(rstd[:]), psum[:, 6:8, 0:H2], ACT.Ln, scale=1.0 / D, bias=K(C_EPS, 1)))
                bump(act.activation(rstd[:], rstd[:], ACT.Exp, scale=-0.5), rstd_made, act)
                if r < 4:
                    for k in range(KD):
                        act.wait_ge(n32_made, KD * r + k + 1)
                        act.copy(xnh[:, k, :], n32[:, k % 2, :]).then_inc(nh_made, 1)

            def window(li):
                for g in range(3):
                    made(act, li, "vt", g)
                    free(act.copy(A["vt"][:, g, :, :].rearrange("p i c -> p (i c)"), bank("vt", g)), li, "vt", g)
                taken(act, li, "tm", 2)
                for g, w in enumerate(WB):
                    act.dma_start(a[f"cache{g}_s"][li, :, w - 1, :, :],
                                  A["tms"][:, 3 * P:9 * P].rearrange("b (v g d) -> b v g d", v=2, g=3)[:, :, g, :]
                                  ).then_inc(window_dma, 16)
                act.dma_start(a["kv_p"][li], proj[:, TSK:TSK + 6, 0:SEQ]).then_inc(window_dma, 16)
                act.dma_start(a["mu_out"][li], proj[:, TU:TU + 3, SEQ - 3:SEQ]).then_inc(window_dma, 16)
                act.dma_start(a["conv_s"][li, :, :, 0:2, :], cbuf[:, li, :, 1:3, :]).then_inc(window_dma, 16)
                act.dma_start(a["conv_s"][li, :, :, 2, :], proj[:, TU:TU + 3, SEQ:T]).then_inc(window_dma, 16)

                def expo(n):
                    act.wait_ge(S("max_made"), 6 * li + n + 1)
                    if n >= 2:
                        made(act, li, "pt", n - 2, 1 if n - 2 < 2 else 0)
                    w = 256 if n < 2 else P
                    for i in range(4):
                        key = ("sc", n, i // 2 if n < 2 else 0)
                        c = (i % 2) * 256 if n < 2 else i * P
                        ins = act.activation(A["pb"][:, n % 2, i * w:(i + 1) * w], bank(*key)[:, c:c + w], ACT.Exp,
                                             scale=0.125, bias=A["nm"][:, n, i:i + 1],
                                             accum_out=A["den"][:, n, i:i + 1])
                        if (n < 2 and i % 2 == 1) or i == 3:
                            free(ins, li, *key)
                        else:
                            step(ins)

                def turned(n):
                    for q in range(2 if n < 2 else 1):
                        cols = (3 if q else 4) * P
                        made(act, li, "pt", n, q)
                        if n >= 2:
                            made(act, li, "pv", n - 2)
                        free(act.copy(A["ptb"][:, n % 2, q * 512:q * 512 + cols], bank("pt", n, q)[:, 0:cols]),
                             li, "pt", n, q)

                expo(0)
                expo(1)
                for n in range(6):
                    turned(n)
                    if n + 2 < 6:
                        expo(n + 2)
                sig(act.activation(A["lse"][:], A["den"][:], ACT.Ln), "den_ln")
                act.wait_ge(S("lse_centred"), li + 1)
                sig(act.activation(A["lr"][:], A["lr"][:], ACT.Exp), "lse_exp")
                step(act.activation(proj[:, TQ:TQ + 2, :], proj[:, TQ:TQ + 2, :], ACT.Silu))
                step(act.activation(proj[0:64, TQ + 2, :], proj[0:64, TQ + 2, :], ACT.Silu))
                step(act.activation(proj[:, TG:TG + 2, :], proj[:, TG:TG + 2, :], ACT.Silu))
                step(act.activation(proj[0:64, TG + 2, :], proj[0:64, TG + 2, :], ACT.Silu))
                step(act.activation(proj[64:P, TG + 2, :], proj[64:P, TG + 2, :], ACT.Sigmoid))
                sig(act.activation(proj[:, TG + 3:TG + 5, :], proj[:, TG + 3:TG + 5, :], ACT.Sigmoid), "gates_made")
                act.wait_ge(S("s_centred"), li + 1)
                sig(act.activation(A["sp"][:], A["sp"][:], ACT.Exp, scale=0.125), "s_exp")
                act.wait_ge(S("s_den"), li + 1)
                sig(act.activation(A["slse"][:], A["sden"][:], ACT.Ln), "s_den_ln")
                act.wait_ge(S("s_lse_centred"), li + 1)
                sig(act.activation(A["slse"][:], A["slse"][:], ACT.Exp), "s_lse_exp")

            def head_rms(li, n):
                act.wait_ge(S("ob_ms"), 5 * li + n + 1)
                step(act.activation(R["ss2"][:], R["ss2"][:], ACT.Ln, scale=1.0 / 64, bias=K(C_EPS, 1)))
                sig(act.activation(R["ss2"][:], R["ss2"][:], ACT.Exp, scale=-0.5), "ob_rms")

            def hgrn(li):
                act.wait_ge(S("window_end"), li + 1)
                act.wait_ge(window_dma, 112 * (li + 1))
                act.dma_start(flat(TSK, 3 * NB * 64), a["hgrn_in"][li]).then_inc(state_in, 16)
                act.dma_start(flat(TSV, 3 * NB * 65), a["mlstm_in"][li]).then_inc(state_in, 16)
                act.dma_start(R["sc8"][0:5, 24:32], a["m_in"][li]).then_inc(state_in, 16)
                act.wait_ge(S("z_parts"), li + 1)
                step(act.activation(R["w0"][:], R["kh"][:], ACT.Exp))
                sig(act.activation(R["w1"][:], R["bt"][:], ACT.Exp, scale=-1.0), "z_exp")
                act.wait_ge(S("z_sums"), li + 1)
                if li:
                    step(act.activation(R["w0"][:], R["w0"][:], ACT.Ln))
                sig(act.activation(R["ee"][:], R["ee"][:], ACT.Ln), "z_ln")
                act.wait_ge(S("k_arg"), li + 1)
                sig(act.activation(R["w1"][:], R["bt"][:], ACT.Exp, scale=-1.0), "k_exp")
                for c in range(NC):
                    made(act, li, "hv", c)
                    free(act.copy(R["vh"][:, c, :], bank("hv", c)[:, 0:384]), li, "hv", c)
                act.wait_ge(S("to_last"), li + 1)
                step(act.activation(R["dl"][:], R["dl"][:], ACT.Exp))
                sig(act.activation(R["ee"][:, :, 0:SEQ], R["ee"][:, :, 0:SEQ], ACT.Exp), "to_last_exp")
                act.wait_ge(S("k_last"), li + 1)
                sig(act.activation(R["ee"][:, :, 0:SEQ], R["bt"][:, :, 0:SEQ], ACT.Exp), "from_first_exp")

                def level(l):
                    x = (R["e2"][:], R["ee"][:, :, 0:SEQ])[l % 2]
                    act.wait_ge(S("lv_diff"), LVL * li + l + 1)
                    sig(act.activation(x, x, ACT.Exp), "lv_exp")

                level(0)
                for c in range(NC):
                    made(act, li, "kh", c)
                    if c >= 2:
                        made(act, li, "su", c - 2)
                    free(act.copy(R["kt"][:, c % 2, :], bank("kh", c)[:, 0:384]), li, "kh", c)
                for l in range(1, LVL):
                    level(l)
                act.wait_ge(S("conv_made"), li + 1)
                made(act, li, "at", 4, LVL - 1)
                for f in range(3):
                    ins = act.activation(R["w0"][:, f, :], conv_out(f), ACT.Silu)
                    if f < 2:
                        step(ins)
                    else:
                        sig(ins, "c_made")
                for n in range(2):
                    head_rms(li, n)

            def mlstm(li):
                act.wait_ge(S("fg_abs"), li + 1)
                step(act.activation(proj[0:5, 7, :], proj[0:5, 7, :], ACT.Exp, scale=-1.0))
                sig(act.activation(proj[0:5, 7, :], proj[0:5, 7, :], ACT.Ln, bias=K(C_ONE, 1, 5)), "fg_ln")
                for c in range(NC):
                    made(act, li, "mv", c)
                    v = bank("mv", c)
                    step(act.copy(R["va"][:, c, 0:4, 0:64], v[:, 0:256].rearrange("p (h d) -> p h d", h=4)))
                    free(act.copy(R["va"][:, c, 4, 0:64], v[:, 320:384]), li, "mv", c)
                for f in range(3):
                    for s in range(4):
                        made(act, li, "mq", f, s)
                        dst = R["bt"] if s < 2 else R["kh"]
                        c = (s % 2) * H2
                        free(act.mul(dst[:, f, c:c + H2], bank("mq", f, s)[:, 0:H2], 1.0 if s < 2 else 0.125),
                             li, "mq", f, s)
                made(act, li, "rt")
                ps = bank("rt").rearrange("p (c q h) -> p q c h", c=NC, q=4)
                for q in range(2):
                    step(act.activation(R["ec"][:, q, :, :], ps[:, q, :, 0:5], ACT.Exp))
                step(act.activation(R["ec"][:, 2, :, :], ps[:, 2, :, 0:5], ACT.Exp))
                free(act.copy(R["ec"][:, 3, :, :], ps[:, 3, :, 0:5]), li, "rt")
                for h in range(5):
                    made(act, li, "md", h)
                    if h >= 2:
                        taken(act, li, "mqk", h - 2)
                    for c in range(NC):
                        t = slice(c * P, (c + 1) * P)
                        ins = act.activation(R["dw"][:, h % 2, t], bank("md", h)[:, t], ACT.Exp,
                                             bias=R["ec"][:, 3, c, h:h + 1])
                        if c < NC - 1:
                            step(ins)
                    free(ins, li, "md", h)
                    if h in (2, 4):
                        head_rms(li, 1 + h // 2)
                head_rms(li, 4)

            def sample(li):
                act.wait_ge(S("f8_copied"), li + 1)
                sig(act.activation(R["ff"][:], R["ff"][:], ACT.Exp), "f8_exp")
                act.wait_ge(S("m8_rows"), li + 1)
                sig(act.activation(R["sc8"][0:5, 0:24], R["sc8"][0:5, 0:24], ACT.Exp), "m8_exp")
                act.wait_ge(S("obs_ms"), li + 1)
                step(act.activation(R["s10"][:], R["s10"][:], ACT.Ln, scale=1.0 / 64, bias=K(C_EPS, 1, NB)))
                sig(act.activation(R["s10"][:], R["s10"][:], ACT.Exp, scale=-0.5), "obs_rms")
                taken(act, li, "fx")
                for name, src in (("hgrn_p", R["sall"][:, NC, :, :]), ("mlstm_p", R["call"][:, NC, :, :]),
                                  ("hgrn_s", flat(TSK, 3 * NB * 64)), ("mlstm_s", flat(TSV, 3 * NB * 65)),
                                  ("m_p", proj[0:5, 5, SEQ - 1:SEQ]), ("m_s", R["sc8"][0:5, 32:40])):
                    act.dma_start(a[name][li], src).then_inc(S("state_out"), 16)
                for m in range(KD):
                    act.copy(xnh[:, m, :], proj[:, MIXT[m], :]).then_inc(mixh_made, 1)
                act.wait_ge(S("state_out"), 96 * (li + 1))

            for li in range(2):
                for n in range(SPL):
                    hi(U_IN[li] + n, KD * P)
                norm(2 * li)
                if li == 0:
                    step(act.copy(mkr[:, 0, :], ident))
                    sig(act.copy(mkr[:, 1, :], K(C_NEGC, P)), "mask_made")
                    act.wait_ge(S("lb_centred"), 1)
                    sig(act.activation(lbt[:, 0:2, :], lbt[:, 0:2, :], ACT.Exp), "lb_exp")
                hi(U_IN[li] + SPL, KD * P)
                with act.Fori(0, (NT - 3) // 6) as i:
                    for n in range(6):
                        hi(U_IN[li] + 3 + n, KD * P, (i, 6))
                act.wait_ge(unit_done, U_OUT[li])
                act.dma_start(A["ck"][:], a["ck"][li]).then_inc(cache_in, 16)
                window(li)
                for n in range(SPL):
                    hi(U_OUT[li] + n, KD * P)
                hgrn(li)
                mlstm(li)
                sample(li)
                for n in range(SPL, KD):
                    hi(U_OUT[li] + n, KD * P)
                norm(2 * li + 1)
                if li == 1:
                    act.dma_start(rw[:], a["rw"]).then_inc(rw_in, 16)
                    act.wait_ge(rw_in, 16)
                    act.copy(rwh[:], rw[:]).then_inc(rw_hi, 1)

                    def turned_tokens(n):
                        act.wait_ge(xt_turned, n + 1)
                        src, rows, t, c = xt_piece(n)
                        act.copy((xth, xtl)[src][0:rows, t, c:c + 512], psum[0:rows, n % 6, :]).then_inc(xt_made, 1)

                    for n in range(6):
                        turned_tokens(n)
                    act.wait_ge(S("rt_centred"), 1)
                    sig(act.activation(re[:], re[:], ACT.Exp), "rt_exp")
                else:
                    with act.Fori(0, NEX[0]) as e:
                        for n in range(UPE):
                            hi(U_FF[0] + n, (KD if n < 2 * KF else KF) * P, (e, UPE))
                            if n % 2 == 1 and n < 2 * KF:
                                j = n // 2
                                act.wait_ge(unit_done, e * UPE + (U_FF[0] + n))
                                if j >= 2:
                                    act.wait_ge(up_read, e * KF + (j - 1))
                                act.activation(halves(sg[:, j % 2, :]), part(U_FF[0] + 2 * j), ACT.Silu
                                               ).then_inc(gate_read, 1)
                            if n >= 2 and n % 2 == 0 and n <= 2 * KF:
                                j = n // 2 - 1
                                act.wait_ge(up_read, e * KF + (j + 1))
                                act.copy(hh[:, j, :], h32[:, j % 2, :]).then_inc(hh_made, 1)

            for n in range(6, 20):
                turned_tokens(n)

            def gathered_to_sbuf(g):
                for k in range(KD):
                    act.wait_ge(gathered, g * KD + (k + 1))
                    act.copy(xg[:, k, :].rearrange("p (s t) -> p s t", s=2),
                             psum[:, 6 + k % 2, :].rearrange("p (s t) -> p s t", s=2)[:, :, 0:SLOTS]).then_inc(xg_made, 1)

            def weighted_hi(f, q):
                rows, st, c0, b = y_piece(q)
                act.wait_ge(gsl, f + 1)
                act.wait_ge(yf_turned, f * 4 + (q + 1))
                act.activation(yh[0:rows, st, c0:c0 + 512], psum[0:rows, b, :], ACT.Copy,
                               scale=gslot[0:rows, st:st + 1]).then_inc(yh_made, 1)

            def experts(c):
                gathered_to_sbuf(c * 9)
                with act.Fori(0, 8) as e:
                    p_, f_ = c * 8 + e, c * 9 + e

                    def hidden_hi(j):
                        act.wait_ge(S("e32_made"), p_ * KF + (j + 1))
                        act.copy(ehl[:, j, 0:SLOTS], e32[:, j % 2, :]).then_inc(hh_made, 1)

                    for n in range(UPE):
                        cols = (KD if n < 2 * KF else KF) * P
                        act.wait_ge(xraw_in[n % RWX], p_ * (16 * UPE // RWX) + 16 * (n // RWX + 1))
                        act.wait_ge(unit_done, p_ * UPE + (U_FF[1] + n - HIX + 1))
                        act.copy(xhi[n % HIX][:, 0:cols], xraw[n % RWX][:, 0:cols]).then_inc(hi_made, 1)
                        if n in (4, 6, 8, 10):
                            weighted_hi(f_, n // 2 - 2)
                        if n % 2 == 1 and 3 <= n < 2 * KF + 2:
                            j = n // 2 - 1
                            act.wait_ge(gate_read, p_ * KF + (G_FF[1] + j + 1))
                            if j >= 2:
                                act.wait_ge(S("e32_made"), p_ * KF + (j - 1))
                            act.activation(esg[:, j % 2, :], g32[:, j % 2, :], ACT.Silu).then_inc(S("silu_made"), 1)
                        if n % 2 == 0 and 6 <= n <= 2 * KF:
                            hidden_hi(n // 2 - 3)
                        if n == 2 * KF + 1:
                            hidden_hi(KF - 2)
                            hidden_hi(KF - 1)
                        if n == 2 * KF + 3:
                            gathered_to_sbuf(f_ + 1)
                for q in range(4):
                    weighted_hi(c * 9 + 8, q)

            act.wait_ge(unit_done, U_FF[1])
            experts(0)
            act.wait_ge(S("flag_made"), 1)
            with act.If(act.value_load(flag[0:1, 0:1], min_val=0, max_val=1) > 0):
                with act.Fori(0, NPASS - 1) as k:
                    experts(k + 1)
                act.wait_ge(x_updated, X_FF[1] + (NPASS - 1) * 9 * KD)
            norm(4)
            act.wait_ge(shift_dma, 96)

        @block.tensor
        def _(pe):
            def passes(u, out, kt, xh, xl, cols=P, wh=None, wl=None, ready=None):
                wh = whi[u % SPL] if wh is None else wh
                wl = wlo[u % SPL] if wl is None else wl
                for k in range(kt):
                    if ready:
                        ready(k)
                    for w, x, first, last in ((wh, xh, True, False), (wh, xl, False, False), (wl, xh, False, True)):
                        for s in range(2):
                            ins = pe.matmul(out[:, s, :], w[:, k * cols:(k + 1) * cols], x[:, k, s * H2:(s + 1) * H2],
                                            start=(k == 0 and first), stop=(k == kt - 1 and last))
                return ins

            def unit(u, kt, xh, xl, when=None, ready=None):
                pe.wait_ge(lo_made, (u if when is None else when) + 1)
                passes(u, part(u), kt, xh, xl, ready=ready).then_inc(unit_done, 1)

            def normed(r):
                return lambda k: pe.wait_ge((nl_pool, nl_dve)[k % 2], 4 * r + k // 2 + 1)

            def mixed(li):
                return lambda k: pe.wait_ge((mixl_pool, mixl_dve)[k % 2], 4 * li + k // 2 + 1)

            def norm(r):
                for k in range(KD):
                    pe.wait_ge(sq_made, KD * r + k + 1)
                    if r == 0 and k == 0:
                        pe.wait_ge(cst_in, 16)
                    for s in range(2):
                        ins = pe.matmul(psum[:, 6 + s, 0:H2], K(C_ONE, P), sqb[:, k % 2, s * H2:(s + 1) * H2],
                                        start=(k == 0), stop=(k == KD - 1))
                    ins.then_inc(sq_used, 1)

            class Job:
                def __init__(self, li, *key):
                    j = JOB[key]
                    self.b = j % 8
                    if j >= 8:
                        pe.wait_ge(bank_read[self.b], li * uses[self.b] + j // 8)

                def out(self, c0, n, rows=P, r0=0):
                    return psum[r0:r0 + rows, self.b, c0:c0 + n]

                def end(self):
                    self.last.then_inc(job_done, 1)

                def mm(self, c0, n, lhsT, rhs, start=True, stop=True, rows=P, r0=0):
                    self.last = pe.matmul(self.out(c0, n, rows, r0), lhsT, rhs, start=start, stop=stop,
                                          skip_group_check=True)

                def tr(self, c0, n, in_, rows, k=P):
                    self.last = pe.transpose(self.out(c0, n, rows), in_, K(C_ID, k, k))

            def window(li):
                for i in range(3):
                    j = Job(li, "tm", i)
                    for t in range(4 * i, min(4 * i + 4, 9)):
                        j.tr((t % 4) * P, P, proj[:, TSQ + t, SEQ:T], NB)
                    j.end()
                for g in range(3):
                    j = Job(li, "vt", g)
                    for i in range(4):
                        j.tr(i * P, P, perm(g, TSV + g, i), P)
                    j.end()

                def scores(n):
                    g, r0 = n // 2, 64 * (n % 2)
                    for q in range(2 if g == 0 else 1):
                        j = Job(li, "sc", n, q)
                        for i in (range(2 * q, 2 * q + 2) if g == 0 else range(4)):
                            lhs = perm(g, TSQ + g, i, r0, 64)
                            if g == 0:
                                c = (i % 2) * 256
                                j.mm(c, 256, ident, K(C_NEG1 if i else C_NEG0, 256), stop=False)
                                if i:
                                    j.mm(c, 256, lhs, proj[r0:r0 + 64, TSK, (i - 1) * P:(i + 1) * P], start=False)
                                else:
                                    j.mm(c + P, P, lhs, proj[r0:r0 + 64, TSK, 0:P], start=False)
                            else:
                                j.mm(i * P, P, ident, K(C_NEGT if g == 1 else C_NEGR, P), stop=False)
                                j.mm(i * P, P, lhs, perm(g, TSK + g, i, r0, 64), start=False)
                        j.end()

                def blocks(n):
                    if n < 2:
                        return [(0, 0, 128)] + [(i, i - 1 + s, i * 256 + s * P) for i in range(1, 4) for s in range(2)]
                    return [(i, i, i * P) for i in range(4)]

                scores(0)
                scores(1)
                for n in range(6):
                    g, bl = n // 2, blocks(n)
                    taken(pe, li, "sc", n, 1 if n < 2 else 0)
                    for q in range(2 if n < 2 else 1):
                        j = Job(li, "pt", n, q)
                        for b, (_, _, c) in enumerate(bl[4 * q:4 * q + 4]):
                            j.tr(b * P, P, A["pb"][:, n % 2, c:c + P], P)
                        j.end()
                    if n + 2 < 6:
                        scores(n + 2)
                    j = Job(li, "pv", n)
                    taken(pe, li, "pt", n, 1 if n < 2 else 0)
                    for i in range(4):
                        mine = [(b, kt) for b, (qt, kt, _) in enumerate(bl) if qt == i]
                        for b, kt in mine:
                            j.mm(i * 64, 64, A["ptb"][:, n % 2, b * P:(b + 1) * P],
                                 A["vt"][:, g, kt, 64 * (n % 2):64 * (n % 2) + 64],
                                 start=(b == mine[0][0]), stop=(b == mine[-1][0]))
                    j.end()
                    if n % 2:
                        j = Job(li, "st", g)
                        taken(pe, li, "pv", n)
                        for i in range(4):
                            j.tr(i * P, P, A["os"][:, g % 2, i, :], P)
                        j.end()
                pe.wait_ge(S("lse_made"), li + 1)
                for g in range(3):
                    j = Job(li, "lt", g)
                    for i in range(4):
                        j.tr(i * P, P, A["lse"][:, 2 * g:2 * g + 2, i], 2)
                    j.end()
                pe.wait_ge(S("alpha_made"), li + 1)
                for g in range(3):
                    j = Job(li, "al", g)
                    j.mm(0, SEQ, K(C_S2, P, 2), A["lr"][:, g, :])
                    j.end()
                for g in range(3):
                    rows = ROWS_G[g]
                    pe.wait_ge(S("dq_made"), 3 * li + g + 1)
                    for q in range(2):
                        j = Job(li, "qb", g, q)
                        j.mm(0, 512, K(C_ONE, rows, NB), A["dq"][:, 4 * q:4 * q + 4, :], rows=rows)
                        j.end()
                for g in range(3):
                    rows = ROWS_G[g]
                    pe.wait_ge(S("s_dots"), 3 * li + g + 1)
                    j = Job(li, "sct", g)
                    for h in range(2):
                        j.tr(h * P, rows, A["scr"][0:rows, g, h, :], NB, rows)
                    j.end()
                pe.wait_ge(S("sp_made"), li + 1)
                j = Job(li, "ppt")
                for gh in range(6):
                    j.tr(gh * NB, NB, A["sp"][:, gh, 0:ROWS_G[gh // 2]], ROWS_G[gh // 2], NB)
                j.end()
                j = Job(li, "spv")
                taken(pe, li, "ppt")
                for gh in range(6):
                    g, rows = gh // 2, ROWS_G[gh // 2]
                    for n in range(NB):
                        c = P + 64 * (gh % 2)
                        j.mm(gh * 64, 64, A["pm"][0:rows, gh, n, :], A["ck"][0:rows, g, n, c:c + 64],
                             start=(n == 0), stop=(n == NB - 1), rows=NB)
                j.end()

            def turn_heads(li, m):
                j = Job(li, "mt", m)
                pe.wait_ge(S("ob_normed"), 5 * li + m + 1)
                for c in range(NC):
                    j.tr(c * P, P, R["ob"][:, m % 2, c, :], P)
                j.end()

            def hgrn(li):
                pe.wait_ge(S("window_end"), li + 1)
                for c in range(NC):
                    j = Job(li, "hv", c)
                    for n, t in enumerate((TI, TI + 1, TF + 2)):
                        j.tr(n * P, P, proj[:, t, c * P:(c + 1) * P], P)
                    j.end()
                for n, tiles in enumerate(((TI, TI + 1, TF + 2), (TV, TV + 1, TU + 2))):
                    j = Job(li, "th", n)
                    for i, t in enumerate(tiles):
                        j.tr(i * P, P, proj[:, t, SEQ:T], NB)
                    j.end()
                pe.wait_ge(S("k_last"), li + 1)
                pe.wait_ge(S("scratch_clear"), li + 1)
                for c in range(NC):
                    j = Job(li, "kh", c)
                    for f in range(3):
                        j.tr(f * P, P, R["w1"][:, f, c * P:(c + 1) * P], P)
                    j.end()
                    j = Job(li, "su", c)
                    taken(pe, li, "kh", c)
                    taken(pe, li, "hv", c)
                    for h in range(5):
                        rows, r0 = (64, 64 * (h % 2)) if h < 4 else (P, 0)
                        j.mm((h // 2) * 64, 64, R["kt"][:, c % 2, h * 64:h * 64 + rows],
                             R["vh"][:, c, v_col(h):v_col(h) + 64], rows=rows, r0=r0)
                    j.end()
                pe.wait_ge(S("gates_made"), li + 1)
                for l in [LVL] + list(range(LVL)):
                    if l < LVL:
                        pe.wait_ge(S("lv_made"), LVL * li + l + 1)
                    for h in range(5):
                        f, r = h // 2, slice(64 * (h % 2), 64 * (h % 2) + 64)
                        w = R["w0"] if l % 2 == 0 else R["w1"]
                        j = Job(li, "at", h, l)
                        for c in range(NC):
                            t = slice(c * P, (c + 1) * P)
                            if l < LVL:
                                later = w[r, f, t].rearrange("p (m s j) -> p m s j", s=2, j=CH >> (l + 1))[:, :, 1, :]
                                j.mm(c * 64, 64, w[r, f, t], later)
                            else:
                                j.mm(c * P, P, R["kh"][r, f, t], proj[r, TQ + f, t])
                        j.end()
                pe.wait_ge(S("qe_made"), li + 1)
                for h in range(5):
                    f, r = h // 2, slice(64 * (h % 2), 64 * (h % 2) + 64)
                    j = Job(li, "ho", h)
                    taken(pe, li, "at", h, LVL - 1)
                    if h == 0:
                        taken(pe, li, "su", NC - 1)
                    for c in range(NC):
                        t = slice(c * P, (c + 1) * P)
                        j.mm(c * 64, 64, R["att"][:, h, t], R["vh"][:, c, v_col(h):v_col(h) + 64], stop=False)
                        j.mm(c * 64, 64, proj[r, TF + f, t], R["sall"][r, c, f, :], start=False)
                    j.end()
                    if h > 2:
                        turn_heads(li, h - 3)

            def mlstm(li):
                for c in range(NC):
                    j = Job(li, "mv", c)
                    for n, t in enumerate((TV, TV + 1, TU + 2)):
                        j.tr(n * P, P, proj[:, t, c * P:(c + 1) * P], P)
                    j.end()
                pe.wait_ge(S("c_made"), li + 1)
                for f in range(3):
                    for s in range(4):
                        j = Job(li, "mq", f, s)
                        c = (s % 2) * H2
                        j.mm(0, H2, bd[:, li, s // 2, f, :], R["w0"][:, f, c:c + H2])
                        j.end()
                pe.wait_ge(S("rows_made"), li + 1)
                j = Job(li, "rt")
                for c in range(NC):
                    j.tr(c * P, P, R["rows"][:, c * P:(c + 1) * P], P)
                j.end()
                j = Job(li, "ac")
                taken(pe, li, "rt")
                j.mm(0, NC * 5, bc(K(C_ID + P - 1, 1), P, P), R["ec"][:, 0, :, :])
                j.end()
                taken(pe, li, "mq", 2, 3)
                for c in range(NC):
                    j = Job(li, "kt", c)
                    for f in range(3):
                        j.tr(f * P, P, R["kh"][:, f, c * P:(c + 1) * P], P)
                    j.end()
                    j = Job(li, "cu", c)
                    taken(pe, li, "kt", c)
                    taken(pe, li, "mv", c)
                    for h in range(5):
                        rows, r0, heads = (64, 64 * (h % 2), 1) if h < 4 else (P, 0, 2)
                        j.mm((h // 2) * 65, 65, R["kw"][:, c % 2, h:h + heads, :], R["va"][:, c, h, :],
                             rows=rows, r0=r0)
                    j.end()
                def decay_and_scores(h):
                    f, r = h // 2, slice(64 * (h % 2), 64 * (h % 2) + 64)
                    j = Job(li, "md", h)
                    pick = bc(K(C_ID + h, 1, 5), 5, P)
                    j.mm(0, SEQ, pick, proj[0:5, 7, 0:SEQ], stop=False)
                    j.mm(0, SEQ, mkr[:, 0, :], bc(mkr[:, 1, :].unsqueeze(1), P, NC, P), start=False)
                    j.end()
                    j = Job(li, "mqk", h)
                    for c in range(NC):
                        t = slice(c * P, (c + 1) * P)
                        j.mm(c * P, P, R["kh"][r, f, t], R["bt"][r, f, t])
                    j.end()

                pe.wait_ge(S("mask_made"), 1)
                decay_and_scores(0)
                for h in range(5):
                    f, r = h // 2, slice(64 * (h % 2), 64 * (h % 2) + 64)
                    if h + 1 < 5:
                        decay_and_scores(h + 1)
                    j = Job(li, "mi", h)
                    if h == 0:
                        taken(pe, li, "cu", NC - 1)
                    for c in range(NC):
                        j.mm(c * 65, 65, R["bt"][r, f, c * P:(c + 1) * P], R["call"][r, c, f, :])
                    j.end()
                    j = Job(li, "mo", h)
                    taken(pe, li, "mqk", h)
                    for c in range(NC):
                        j.mm(c * 65, 65, R["qd"][:, h % 2, c * P:(c + 1) * P], R["va"][:, c, h, :])
                    j.end()
                    if h == 2:
                        turn_heads(li, 2)
                turn_heads(li, 3)
                turn_heads(li, 4)

            def sample(li):
                S8 = flat(TSK, 3 * NB * 64).rearrange("p (f b v) -> p f b v", f=3, b=NB)
                C8 = flat(TSV, 3 * NB * 65).rearrange("p (f b v) -> p f b v", f=3, b=NB)

                def spread(kind):
                    for f in range(3):
                        j = Job(li, kind, f)
                        even = R["ee"][0:NB, :, :].rearrange("p f t -> p (f t)")[:, f * 512:(f + 1) * 512]
                        odd = R["w1"][0:NB, :, :].rearrange("p f t -> p (f t)")[:, f * 512:(f + 1) * 512]
                        if f < 2:
                            j.mm(0, 512, K(C_ONE, 64, NB), even, rows=64)
                            j.mm(0, 512, K(C_ONE, 64, NB), odd, rows=64, r0=64)
                        else:
                            j.mm(0, 512, K(C_ONE, P, NB), even)
                        j.end()

                def query(kind, state, w):
                    for s in range(2):
                        j = Job(li, kind, s)
                        r = slice(64 * s, 64 * s + 64)
                        for f in range(3 - s):
                            for b in range(NB):
                                j.mm(f * w, w, R["qm8"][r, f, b, :], state[r, f, b, :], start=(b == 0),
                                     stop=(b == NB - 1), rows=NB)
                        j.end()

                pe.wait_ge(S("dv_made"), 2 * li + 1)
                spread("vb")
                pe.wait_ge(S("s8_made"), li + 1)
                query("so", S8, 64)
                pe.wait_ge(S("m8_exp"), li + 1)
                j = Job(li, "rs")
                j.tr(0, 5, R["sc8"][0:5, 16:24], NB, 5)
                j.end()
                j = Job(li, "aw")
                for f in range(3):
                    j.mm(f * 2 * NB, 2 * NB, K(C_HP + f * P, P, 5), R["sc8"][0:5, 0:2 * NB])
                j.end()
                pe.wait_ge(S("dv_made"), 2 * li + 2)
                spread("vc")
                pe.wait_ge(S("c8_made"), li + 1)
                query("co", C8, 65)
                pe.wait_ge(S("obs_normed"), li + 1)
                j = Job(li, "fx")
                for m in range(KD):
                    src = R["obs"][:, 2 * m:2 * m + 2, :].rearrange("b h d -> b (h d)") if m < 5 \
                        else osw[:, (m - 5) * P:(m - 4) * P]
                    j.tr(m * NB, NB, src, P, NB)
                j.end()

            for li in range(2):
                norm(2 * li)
                for n in range(NPS):
                    unit(U_IN[li] + n, KD, xnh, xnl, ready=None if n else normed(2 * li))
                with pe.Fori(0, (NT - 3) // 6) as i:
                    for n in range(6):
                        u = U_IN[li] + 3 + n
                        pe.wait_ge(proj_read, i * 6 + (NT * li + n + 1))
                        unit(u, KD, xnh, xnl, i * 6 + u)
                pe.wait_ge(proj_read, NT * (li + 1))
                window(li)
                hgrn(li)
                mlstm(li)
                sample(li)
                for n in range(KD):
                    if n >= NPS:
                        pe.wait_ge(x_updated, X_OUT[li] - KD + n - NPS + 1)
                    u = U_OUT[li] + n
                    if li == 0:
                        unit(u, KD, xnh, xnl, ready=None if n else mixed(0))
                    else:
                        pe.wait_ge((lo_pool, lo_dve)[n % 2], n // 2 + 1)
                        passes(u, part(u), KD, xnh, xnl, ready=None if n else mixed(1)).then_inc(unit_done, 1)
                norm(2 * li + 1)
                if li == 1:
                    pe.wait_ge(rw_lo, 1)
                    pe.wait_ge(rstd_made, 4)
                    passes(0, psum[0:8, 6:8, 0:H2], KD, xnh, xnl, 8, rwh, rwl, normed(3)).then_inc(rt_done, 1)

                    def turn_tokens(n):
                        src, rows, t, c = xt_piece(n)
                        if n >= 6:
                            pe.wait_ge(xt_made, n - 5)
                        for k in range(4):
                            x = (xnh, xnl)[src][:, c // P + k, t * P:t * P + rows].bitcast(F32)
                            ins = pe.transpose(psum[0:rows, n % 6, k * P:(k + 1) * P], x, ident)
                        ins.then_inc(xt_turned, 1)

                    for n in range(6):
                        turn_tokens(n)
                    pe.wait_ge(rt_read, 1)
                    for t in range(5):
                        n = P if t < 4 else NB
                        ins = pe.transpose(psum[0:n, 6, t * 8:t * 8 + 8], lg[:, t * P:t * P + n], K(C_ID, 8, 8))
                    ins.then_inc(rt_done, 1)
                    for n in range(6, 20):
                        turn_tokens(n)
                    pe.wait_ge(rt_read, 2)
                    for t in range(5):
                        for t2 in range(t + 1):
                            pe.matmul(psum[:, 6, 8 * t:8 * t + 8], K(C_TRI if t2 == t else C_ONE, P), rsel[:, t2, :],
                                      start=(t2 == 0), stop=(t2 == t))
                    for t in range(5):
                        ins = pe.matmul(psum[:, 7, 0:8], K(C_ONE, P), rsel[:, t, :], start=(t == 0), stop=(t == 4))
                    ins.then_inc(rt_done, 1)
                else:
                    for k in (KD - 2, KD - 1):
                        normed(1)(k)
                    with pe.Fori(0, NEX[0]) as e:
                        for n in range(UPE):
                            p_ = n - NPS
                            before, back = (p_, 0) if p_ >= 0 else (p_ + UPE, 1)
                            if before >= 2 * KF:
                                pe.wait_ge(x_updated, e * KD + (X_OUT[0] - back * KD + before - 2 * KF + 1))
                            elif before % 2 == 0:
                                pe.wait_ge(gate_read, e * KF + (before // 2 + 1))
                            else:
                                pe.wait_ge(up_read, e * KF + (before // 2 + 1))
                            if n < 2 * KF:
                                unit(U_FF[0] + n, KD, xnh, xnl, e * UPE + (U_FF[0] + n))
                            else:
                                if n == 2 * KF:
                                    pe.wait_ge(hl_made, e * KF + KF)
                                unit(U_FF[0] + n, KF, hh, hl, e * UPE + (U_FF[0] + n))

            def gather(g):
                pe.wait_ge(sel_made, g + 1)
                for k in range(KD):
                    if k >= 2:
                        pe.wait_ge(xg_made, g * KD + (k - 1))
                    for s_ in range(2):
                        for t in range(5):
                            n = P if t < 4 else NB
                            ins = pe.matmul(psum[:, 6 + k % 2, s_ * WIDE:(s_ + 1) * WIDE],
                                            (xth, xtl)[s_][0:n, t, k * P:(k + 1) * P], sel[0:n, t, :],
                                            start=(t == 0), stop=(t == 4))
                    ins.then_inc(gathered, 1)

            def turn_results(f, q):
                rows, st, c0, b = y_piece(q)
                pe.wait_ge(yf_made, f * KD + KD)
                pe.wait_ge(selT_made, f * 2 + 2)
                pe.wait_ge(gsl, f + 1)
                for m in range(4):
                    ins = pe.transpose(psum[0:rows, b, m * P:(m + 1) * P], yf[:, c0 // P + m, st * P:st * P + rows], ident)
                ins.then_inc(yf_turned, 1)

            def scatter(f):
                pe.wait_ge(yl_made, f * 4 + 4)
                for m in range(KD):
                    if m >= 2:
                        pe.wait_ge(x_updated, f * KD + (X_OUT[1] + m - 1))
                    for s_ in range(2):
                        for st in range(2):
                            rows = (P, SLOTS - P)[st]
                            for y_ in (yh, yl):
                                ins = pe.matmul(scatter_bank(m)[:, s_, :], y_[0:rows, st, m * P:(m + 1) * P],
                                                selT[0:rows, st, s_ * H2:(s_ + 1) * H2],
                                                start=(st == 0 and y_ is yh), stop=(st == 1 and y_ is yl))
                    ins.then_inc(scattered, 1)

            def turn_selection(f):
                for st in range(2):
                    pe.wait_ge(x_updated, f * KD + (X_OUT[1] + 7 + st))
                    rows = (P, SLOTS - P)[st]
                    for t in range(5):
                        n = P if t < 4 else NB
                        b = (1, 3)[t // 4] if st == 0 else (6, 7)[t // 4]
                        ins = pe.transpose(psum[0:rows, b, (t % 4) * P:(t % 4) * P + n],
                                           sel[0:n, t, st * P:st * P + rows].bitcast(F32), K(C_ID, n, n))
                    ins.then_inc(turned_sel, 1)
                for st in range(2):
                    rows = (P, SLOTS - P)[st]
                    for t in range(5):
                        n = P if t < 4 else NB
                        ins = pe.matmul(psum[0:rows, 5, 2 * st:2 * st + 2], sel[0:n, t, st * P:st * P + rows],
                                        ge[0:n, t, :], start=(t == 0), stop=(t == 4))
                ins.then_inc(turned_sel, 1)

            def experts(c):
                gather(c * 9)
                with pe.Fori(0, 8) as e:
                    p_, f_ = c * 8 + e, c * 9 + e
                    for n in range(UPE):
                        before = n - NPS
                        if n == 0:
                            pe.wait_ge(xg_made, f_ * KD + KD)
                            pe.wait_ge(yf_made, f_ * KD + KD)
                        if n == 2 * KF:
                            scatter(f_)
                            turn_selection(f_)
                            pe.wait_ge(hl_made, p_ * KF + (G_FF[1] + KF))
                        if n == 2 * KF + 2:
                            pe.wait_ge(selT_made, f_ * 2 + 4)
                            gather(f_ + 1)
                        if before >= 2 * KF:
                            pe.wait_ge(yf_made, f_ * KD + (KD + before - 2 * KF + 1))
                        elif before >= 0:
                            pe.wait_ge((gate_read, up_read)[before % 2], p_ * KF + (G_FF[1] + before // 2 + 1))
                        wait_expert_lo(pe, n, p_)
                        kt, x_ = (KD, xg) if n < 2 * KF else (KF, ehl)
                        for k in range(kt):
                            pe.matmul(epart(n), xhi[n % HIX][:, k * P:(k + 1) * P], x_[:, k, :], start=(k == 0),
                                      stop=False, skip_group_check=True)
                            ins = pe.matmul(epart(n)[:, 0:WIDE], xlo[n % RWX][:, k * P:(k + 1) * P], x_[:, k, 0:WIDE],
                                            start=False, stop=(k == kt - 1), skip_group_check=True)
                        ins.then_inc(unit_done, 1)
                        if n in (2, 4, 6, 8):
                            turn_results(f_, n // 2 - 1)
                for q in range(4):
                    turn_results(c * 9 + 8, q)
                scatter(c * 9 + 8)
                pe.wait_ge(x_updated, c * 9 * KD + (X_OUT[1] + 9 * KD))

            pe.wait_ge(rt_read, 3)
            pe.wait_ge(xt_made, 20)
            experts(0)
            pe.wait_ge(S("flag_made"), 1)
            with pe.If(pe.value_load(flag[0:1, 0:1], min_val=0, max_val=1) > 0):
                with pe.Fori(0, NPASS - 1) as k:
                    experts(k + 1)
            norm(4)

        @block.vector
        def _(v):
            def step(ins):
                bump(ins, dve_step, v)

            def sig(ins, name):
                bump(ins, S(name), v)

            def free(ins, li, *key):
                release(v, ins, li, *key)

            tt, ts, stt = v.tensor_tensor, v.tensor_scalar, v.scalar_tensor_tensor

            def odd_lo(r, k):
                v.wait_ge(nh_made, KD * r + k + 1)
                tt(xnl[:, k, :], n32[:, k % 2, :], xnh[:, k, :].bitcast(F32), ALU.subtract).then_inc(nl_dve, 1)

            def norm(r):
                if r:
                    v.wait_ge(x_updated, [0, X_OUT[0], X_FF[0], X_OUT[1], X_FF[1]][r])
                v.wait_ge(rstd_made, r + 1)
                for k in range(KD):
                    gain = par(r // 2, (PR_G1, PR_G2)[r % 2] + k) if r < 4 else par(0, PR_GF + k)
                    if r == 4:
                        stt(yout[:, k, :], xT[:, k, :], gain, rstd[:], ALU.mult, ALU.mult).then_inc(y_made, 1)
                        continue
                    if k % 2:
                        if k > 2 or r:
                            v.wait_ge(nl_dve, 4 * r + k // 2)
                    elif k or r:
                        v.wait_ge(nl_pool, 4 * r + k // 2)
                    stt(n32[:, k % 2, :], xT[:, k, :], gain, rstd[:], ALU.mult, ALU.mult).then_inc(n32_made, 1)
                    if k >= 2 and k % 2 == 0:
                        odd_lo(r, k - 1)
                if r < 4:
                    odd_lo(r, KD - 1)

            def window(li):
                for i in range(3):
                    made(v, li, "tm", i)
                    cols = (4 if i < 2 else 1) * P
                    free(v.tensor_copy(A["tms"][:, i * 512:i * 512 + cols], bank("tm", i)[0:NB, 0:cols]), li, "tm", i)

                def maxima(n):
                    for q in range(2 if n < 2 else 1):
                        made(v, li, "sc", n, q)
                        w = 256 if n < 2 else P
                        k = 512 // w
                        step(v.tensor_reduce(A["mx"][:, n, q * k:(q + 1) * k],
                                             bank("sc", n, q).rearrange("p (i s) -> p i s", s=w), AX, ALU.max))
                    sig(ts(A["nm"][:, n, :], A["mx"][:, n, :], -0.125, None, ALU.mult), "max_made")

                maxima(0)
                maxima(1)
                for n in range(6):
                    g, h = n // 2, n % 2
                    if n + 2 < 6:
                        maxima(n + 2)
                    made(v, li, "pv", n)
                    step(v.reciprocal(A["rd"][:, n, :], A["den"][:, n, :]))
                    free(tt(A["os"][:, g % 2, :, 64 * h:64 * h + 64],
                            bank("pv", n)[:, 0:256].rearrange("p (i d) -> p i d", i=4),
                            bc(A["rd"][:, n, :].unsqueeze(2), P, 4, 64), ALU.mult), li, "pv", n)
                    if h:
                        made(v, li, "st", g)
                        free(v.tensor_copy(natural(g, proj[:, TSQ + g, 0:SEQ]), grouped(g, bank("st", g))), li, "st", g)
                v.wait_ge(S("den_ln"), li + 1)
                sig(stt(A["lse"][:], A["mx"][:], 0.125, A["lse"][:], ALU.mult, ALU.add), "lse_made")
                for g in range(3):
                    made(v, li, "lt", g)
                    free(v.tensor_copy(natural(g, A["lr"][:, g, :]), grouped(g, bank("lt", g)[0:2, :])), li, "lt", g)
                lr, lm = A["lr"], A["lm"]
                step(tt(lm[:], lr[:, 0, :], lr[:, 1, :], ALU.max))
                step(tt(lm[:], lm[:], lr[:, 2, :], ALU.max))
                sig(tt(lr[:], lr[:], bc(lm[:].unsqueeze(1), 2, 3, SEQ), ALU.subtract), "lse_centred")
                v.wait_ge(S("lse_exp"), li + 1)
                step(tt(lm[:], lr[:, 0, :], lr[:, 1, :], ALU.add))
                step(tt(lm[:], lm[:], lr[:, 2, :], ALU.add))
                step(v.reciprocal(lm[:], lm[:]))
                sig(tt(lr[:], lr[:], bc(lm[:].unsqueeze(1), 2, 3, SEQ), ALU.mult), "alpha_made")
                for g in range(3):
                    made(v, li, "al", g)
                    free(tt(proj[:, TSQ + g, 0:SEQ], proj[:, TSQ + g, 0:SEQ], bank("al", g), ALU.mult), li, "al", g)
                tms = A["tms"]
                own = A["own"][:].rearrange("b h d -> b (h d)")
                step(v.memset(A["ss"][:], NEG))
                step(tt(own, tms[:, 0:384], tms[:, 384:768], ALU.mult))
                step(v.tensor_reduce(A["ss"][:, :, 128], A["own"][:], AX, ALU.add))
                v.wait_ge(cache_in, 16 * (li + 1))
                for g in range(3):
                    rows = ROWS_G[g]
                    if g:
                        made(v, li, "qb", g - 1, 1)
                    sig(tt(A["dq"][:], bc(tms[:, g * P:(g + 1) * P].unsqueeze(1), NB, NB, P),
                           bc(K(C_ID, NB, NB).unsqueeze(2), NB, NB, P), ALU.mult), "dq_made")
                    for q in range(2):
                        made(v, li, "qb", g, q)
                        free(tt(A["pr"][0:rows, :].rearrange("p (n c) -> p n c", n=4),
                                bank("qb", g, q)[0:rows, :].rearrange("p (n c) -> p n c", n=4),
                                A["ck"][0:rows, g, 4 * q:4 * q + 4, 0:P], ALU.mult), li, "qb", g, q)
                        ins = v.tensor_reduce(A["scr"][0:rows, g, :, 4 * q:4 * q + 4].rearrange("p h n -> p n h"),
                                              A["pr"][0:rows, :].rearrange("p (n h d) -> p n h d", n=4, h=2), AX, ALU.add)
                        if q:
                            sig(ins, "s_dots")
                        else:
                            step(ins)
                for g in range(3):
                    rows = ROWS_G[g]
                    made(v, li, "sct", g)
                    free(v.tensor_copy(A["ss"][:, 2 * g:2 * g + 2, 0:rows],
                                       bank("sct", g)[0:NB, 0:2 * P].rearrange("b (h s) -> b h s", h=2)[:, :, 0:rows]),
                         li, "sct", g)
                step(v.tensor_reduce(A["smx"][:], A["ss"][:], AX, ALU.max))
                sig(tt(A["sp"][:], A["ss"][:], bc(A["smx"][:].unsqueeze(2), NB, 6, 129), ALU.subtract), "s_centred")
                v.wait_ge(S("s_exp"), li + 1)
                sig(v.tensor_reduce(A["sden"][:], A["sp"][:], AX, ALU.add), "s_den")
                v.wait_ge(S("s_den_ln"), li + 1)
                by_head = A["slse"][:].rearrange("b (g h) -> b h g", g=3)
                m2 = bc(A["sm2"][:].unsqueeze(2), NB, 2, 3)
                step(stt(A["slse"][:], A["smx"][:], 0.125, A["slse"][:], ALU.mult, ALU.add))
                step(v.tensor_reduce(A["sm2"][:], by_head, AX, ALU.max))
                sig(tt(by_head, by_head, m2, ALU.subtract), "s_lse_centred")
                v.wait_ge(S("s_lse_exp"), li + 1)
                step(v.tensor_reduce(A["sm2"][:], by_head, AX, ALU.add))
                step(v.reciprocal(A["sm2"][:], A["sm2"][:]))
                step(tt(by_head, by_head, m2, ALU.mult))
                step(v.reciprocal(A["sden"][:], A["sden"][:]))
                step(tt(A["slse"][:], A["slse"][:], A["sden"][:], ALU.mult))
                sig(tt(A["sp"][:], A["sp"][:], bc(A["slse"][:].unsqueeze(2), NB, 6, 129), ALU.mult), "sp_made")
                made(v, li, "ppt")
                for g in range(3):
                    rows = ROWS_G[g]
                    ins = tt(A["pm"][0:rows, 2 * g:2 * g + 2, :, :].rearrange("p h n m -> p (h n) m"),
                             bc(bank("ppt")[0:rows, 2 * g * NB:(2 * g + 2) * NB].unsqueeze(2), rows, 2 * NB, NB),
                             K(C_DM, 2 * NB * NB, rows).rearrange("p (n m) -> p n m", m=NB), ALU.mult)
                    if g < 2:
                        step(ins)
                    else:
                        free(ins, li, "ppt")
                step(tt(A["own"][:], tms[:, 768:1152].rearrange("b (h d) -> b h d", h=6),
                        bc(A["sp"][:, :, 128:129], NB, 6, 64), ALU.mult))
                made(v, li, "spv")
                free(tt(osw[:], bank("spv")[0:NB, 0:384], own, ALU.add), li, "spv")
                v.wait_ge(window_dma, 112 * (li + 1))
                sig(v.memset(A["mx"][:], 0.0), "window_end")

            def heads_of(m):
                return R["ob"][:, m % 2, :, :].rearrange("p c (h d) -> p (c h) d", h=2)

            def mean_squares(li, m):
                ob = R["ob"][:, m % 2, :, :]
                step(tt(R["sqo"][:], ob, ob, ALU.mult))
                sig(v.tensor_reduce(R["ss2"][:], R["sqo"][:].rearrange("p c (h d) -> p (c h) d", h=2), AX, ALU.add), "ob_ms")

            def normalise(li, m):
                v.wait_ge(S("ob_rms"), 5 * li + m + 1)
                sig(tt(heads_of(m), heads_of(m), bc(R["ss2"][:].unsqueeze(2), P, 8, 64), ALU.mult), "ob_normed")

            def gate_heads(li, m):
                made(v, li, "mt", m)
                gate = proj[:, TG + m, 0:SEQ]
                free(stt(gate, bank("mt", m), par(li, PR_ON + m), gate, ALU.mult, ALU.mult), li, "mt", m)

            def hgrn(li):
                z, kh, bt, ee, w0, w1 = proj[:, TF:TF + 3, :], R["kh"], R["bt"], R["ee"], R["w0"], R["w1"]
                q = proj[:, TQ:TQ + 3, :]
                step(ts(kh[:], z, 0.0, None, ALU.min))
                sig(ts(bt[:], z, 0.0, None, ALU.max), "z_parts")
                v.wait_ge(S("z_exp"), li + 1)
                step(tt(ee[:], w0[:], w1[:], ALU.add))
                if li:
                    for f in range(3):
                        step(stt(w0[:, f, :], w1[:, f, :], lbt[:, 2, f:f + 1], w0[:, f, :], ALU.mult, ALU.add))
                    step(ts(w0[:], w0[:], 2.0 ** -63, None, ALU.max))
                sig(v.memset(R["ss2"][:], 0.0), "z_sums")
                v.wait_ge(S("z_ln"), li + 1)
                sig(tt(bt[:], bt[:], ee[:], ALU.add), "k_arg")
                if li:
                    step(tt(w0[:], w0[:], kh[:], ALU.max))
                    step(tt(w0[:], w0[:], ee[:], ALU.subtract))
                else:
                    step(tt(w0[:], kh[:], ee[:], ALU.subtract))
                sig(v.tensor_copy(R["ff"][:], w0[:, :, SEQ:T]), "f8_copied")
                v.wait_ge(S("k_exp"), li + 1)
                if li:
                    for f in range(3):
                        step(ts(kh[:, f, :], w1[:, f, :], lbt[:, 3, f:f + 1], None, ALU.mult))
                else:
                    step(v.tensor_copy(kh[:], w1[:]))
                step(v.tensor_copy(R["k8"][:], kh[:, :, SEQ:T]))
                for f in range(3):
                    step(v.tensor_tensor_scan(bt[:, f, 0:SEQ], K(C_RST, SEQ), w0[:, f, 0:SEQ], 0.0, ALU.mult, ALU.add))
                b4 = bt[:, :, 0:SEQ].rearrange("p f (c j) -> p f c j", j=CH)
                e4 = ee[:, :, 0:SEQ].rearrange("p f (c j) -> p f c j", j=CH)
                step(v.tensor_copy(R["dl"][:], b4[:, :, :, CH - 1]))
                for f in range(3):
                    ins = tt(e4[:, f], bc(b4[:, f, :, CH - 1:CH], P, NC, CH), b4[:, f], ALU.subtract)
                    if f < 2:
                        step(ins)
                    else:
                        sig(ins, "to_last")
                v.wait_ge(S("to_last_exp"), li + 1)
                sig(tt(w1[:, :, 0:SEQ], kh[:, :, 0:SEQ], ee[:, :, 0:SEQ], ALU.mult), "k_last")
                def halved(ap, half, l):
                    return ap[:, :, 0:SEQ].rearrange("p f (m s j) -> p f m s j", s=2, j=CH >> (l + 1))[:, :, :, half, :]

                def diff(l):
                    n = CH >> (l + 1)
                    e = (R["e2"], ee)[l % 2]
                    first, second = halved(bt, 0, l), halved(bt, 1, l)
                    mid = bc(first[:, :, :, n - 1:n], P, 3, SEQ // (2 * n), n)
                    step(tt(halved(e, 0, l), mid, first, ALU.subtract))
                    sig(tt(halved(e, 1, l), second, mid, ALU.subtract), "lv_diff")

                def level(l):
                    w, e = (w0, w1)[l % 2], (R["e2"], ee)[l % 2]
                    v.wait_ge(S("lv_exp"), LVL * li + l + 1)
                    if l >= 2:
                        made(v, li, "at", 4, l - 2)
                    step(tt(halved(w, 0, l), halved(kh, 0, l), halved(e, 0, l), ALU.mult))
                    sig(tt(halved(w, 1, l), halved(q, 1, l), halved(e, 1, l), ALU.mult), "lv_made")

                diff(0)
                v.wait_ge(S("gates_made"), li + 1)
                v.wait_ge(S("from_first_exp"), li + 1)
                taken(v, li, "hv", NC - 1)
                for n in range(2):
                    made(v, li, "th", n)
                    free(v.tensor_copy(R["thm"][:, n * 384:(n + 1) * 384], bank("th", n)[0:NB, 0:384]), li, "th", n)
                sig(tt(proj[:, TF:TF + 3, 0:SEQ], q[:, :, 0:SEQ], ee[:, :, 0:SEQ], ALU.mult), "qe_made")

                def state(c):
                    made(v, li, "su", c)
                    s0, s1 = R["sall"][:, c, :, :], R["sall"][:, c + 1, :, :]
                    step(tt(s1, s0, bc(R["dl"][:, :, c:c + 1], P, 3, 64), ALU.mult))
                    free(tt(s1, s1, bank("su", c)[:, 0:192].rearrange("p (f d) -> p f d", f=3), ALU.add), li, "su", c)

                v.wait_ge(S("scratch_clear"), li + 1)

                def gather(l):
                    for h in range(5):
                        made(v, li, "at", h, l)
                        if l == LVL:
                            views = (R["att"][:, h, :].rearrange("p (c t) -> p c t", c=NC),
                                     bc(lvm[:, l, :].unsqueeze(1), P, NC, CH),
                                     bank("at", h, l).rearrange("p (c t) -> p c t", c=NC))
                        else:
                            n = CH >> (l + 1)
                            mask = lvm[:, l, :].rearrange("p (m s j) -> p m s j", s=2, j=n)[:, :, 1, :]
                            views = (R["att"][:, h, :].rearrange("p (c m s j) -> p c m s j", c=NC, s=2, j=n)[:, :, :, 1, :],
                                     bc(mask.unsqueeze(1), P, NC, 64 // n, n),
                                     bank("at", h, l)[:, 0:256].rearrange("p (c m j) -> p c m j", c=NC, j=n))
                        free(v.copy_predicated(*views), li, "at", h, l)

                for c in range(NC):
                    state(c)
                gather(LVL)
                for l in range(LVL):
                    if l + 1 < LVL:
                        diff(l + 1)
                    level(l)
                    if l:
                        gather(l - 1)
                gather(LVL - 1)
                for h in range(5):
                    made(v, li, "ho", h)
                    free(v.tensor_copy(R["ob"][:, (h // 2) % 2, :, 64 * (h % 2):64 * (h % 2) + 64],
                                       bank("ho", h)[:, 0:256].rearrange("p (c d) -> p c d", c=NC)), li, "ho", h)
                    if h in (1, 3):
                        mean_squares(li, h // 2)
                    if h in (2, 4):
                        normalise(li, h // 2 - 1)
                    if h > 2:
                        gate_heads(li, h - 3)

            def mlstm(li):
                w0, mu = R["w0"], proj[:, TU:TU + 3, :]
                step(v.memset(R["va"][:, :, :, 64:65], 1.0))
                step(v.memset(R["kw"][:, :, 5, :], 0.0))
                v.wait_ge(S("c_made"), li + 1)
                v.wait_ge(S("call_clear"), li + 1)
                ig, lf, m, F, t4 = (proj[0:5, n, :] for n in (3, 4, 5, 6, 7))
                step(ts(ig, proj[64:69, TQ + 2, :], par(li, PR_IB, 1, 5, 64), None, ALU.add))
                step(ts(lf, proj[96:101, TQ + 2, :], par(li, PR_FB, 1, 5, 96), None, ALU.add))
                sig(stt(t4, lf, -1.0, lf, ALU.mult, ALU.max), "fg_abs")
                v.wait_ge(S("fg_ln"), li + 1)
                step(stt(lf, lf, 0.0, t4, ALU.min, ALU.subtract))
                step(v.tensor_tensor_scan(m[:, 0:SEQ], lf[:, 0:SEQ], ig[:, 0:SEQ], 0.0, ALU.add, ALU.max))
                step(v.tensor_tensor_scan(F[:, 0:SEQ], K(C_RST, SEQ, 5), lf[:, 0:SEQ], 0.0, ALU.mult, ALU.add))
                step(tt(t4[:, 0:SEQ], F[:, 0:SEQ], m[:, 0:SEQ], ALU.subtract))
                step(tt(ig[:, 0:SEQ], ig[:, 0:SEQ], F[:, 0:SEQ], ALU.subtract))
                rows = R["rows"]

                def ch(ap):
                    return ap[:, 0:SEQ].rearrange("p (c j) -> p c j", j=CH)
                step(v.tensor_copy(rows[0:5, 0:CH], t4[:, 0:CH]))
                step(tt(ch(rows[0:5, :])[:, 1:NC, :], ch(t4)[:, 1:NC, :],
                        bc(ch(m)[:, 0:NC - 1, CH - 1:CH], 5, NC - 1, CH), ALU.add))
                step(tt(ch(rows[32:37, :]), ch(ig), bc(ch(t4)[:, :, CH - 1:CH], 5, NC, CH), ALU.add))
                step(ts(rows[64:69, :], m[:, 0:SEQ], -1.0, None, ALU.mult))
                sig(v.tensor_copy(rows[96:101, :], ig[:, 0:SEQ]), "rows_made")
                made(v, li, "ac")
                ac = bank("ac")[:, 0:NC * 5].rearrange("p (c h) -> p c h", c=NC)
                step(v.tensor_copy(R["acb"][0:64, :, :], ac[0:64, :, 0:5:2]))
                free(v.tensor_copy(R["acb"][64:P, :, 0:2], ac[64:P, :, 1:5:2]), li, "ac")
                for c in range(NC):
                    made(v, li, "kt", c)
                    free(tt(R["kw"][:, c % 2, 0:5, :], bank("kt", c)[:, 0:320].rearrange("p (h d) -> p h d", h=5),
                            bc(R["ec"][:, 1, c, :].unsqueeze(2), P, 5, 64), ALU.mult), li, "kt", c)
                    made(v, li, "cu", c)
                    s0, s1 = R["call"][:, c, :, :], R["call"][:, c + 1, :, :]
                    step(tt(s1, s0, bc(R["acb"][:, c, :].unsqueeze(2), P, 3, 65), ALU.mult))
                    free(tt(s1, s1, bank("cu", c)[:, 0:195].rearrange("p (f d) -> p f d", f=3), ALU.add), li, "cu", c)
                def decayed(h):
                    made(v, li, "mqk", h)
                    taken(v, li, "md", h)
                    free(tt(R["qd"][:, h % 2, :], bank("mqk", h), R["dw"][:, h % 2, :], ALU.mult), li, "mqk", h)

                decayed(0)
                for h in range(5):
                    if h + 1 < 5:
                        decayed(h + 1)
                    num, t1 = R["num"], R["t1"]
                    made(v, li, "mi", h)
                    free(tt(t1[:], bank("mi", h)[:, 0:260].rearrange("p (c d) -> p c d", c=NC),
                            bc(R["ec"][:, 0, :, h:h + 1], P, NC, 65), ALU.mult), li, "mi", h)
                    made(v, li, "mo", h)
                    free(tt(num[:], bank("mo", h)[:, 0:260].rearrange("p (c d) -> p c d", c=NC), t1[:], ALU.add), li, "mo", h)
                    nq = num[:, :, 64]
                    step(stt(R["rden"][:], nq, -1.0, nq, ALU.mult, ALU.max))
                    step(tt(R["rden"][:], R["rden"][:], R["ec"][:, 2, :, h], ALU.max))
                    step(v.reciprocal(R["rden"][:], R["rden"][:]))
                    n = 5 + h
                    step(tt(R["ob"][:, (n // 2) % 2, :, 64 * (n % 2):64 * (n % 2) + 64], num[:, :, 0:64],
                            bc(R["rden"][:].unsqueeze(2), P, NC, 64), ALU.mult))
                    if n % 2:
                        mean_squares(li, n // 2)
                    if h in (2, 4):
                        gate_heads(li, n // 2 - 1)
                    if h in (1, 3, 4):
                        normalise(li, 2 + h // 2)
                gate_heads(li, 4)

            def sample(li):
                S8 = flat(TSK, 3 * NB * 64).rearrange("p (n d) -> p n d", d=64)
                C8 = flat(TSV, 3 * NB * 65).rearrange("p (n d) -> p n d", d=65)
                tmp = R["w0"][:].rearrange("p f t -> p (f t)")[:, 0:3 * NB * 64].rearrange("p (n d) -> p n d", d=64)
                ff = R["ff"][:].rearrange("p f b -> p (f b)")

                def diag(n):
                    th = R["thm"][:, n * 384:(n + 1) * 384]
                    even, odd = (R[k][0:NB, :, :].rearrange("p f t -> p (f t)")[:, 0:1536].rearrange(
                        "p (f b d) -> p f b d", f=3, b=NB) for k in ("ee", "w1"))
                    eye = bc(K(C_ID, NB, NB).unsqueeze(2), NB, NB, 64)
                    for f in range(3):
                        c = f * P if f < 2 else 320
                        ins = tt(even[:, f], bc(th[:, c:c + 64].unsqueeze(1), NB, NB, 64), eye, ALU.mult)
                        if f == 2:
                            sig(ins, "dv_made")
                            break
                        step(ins)
                        step(tt(odd[:, f], bc(th[:, c + 64:c + P].unsqueeze(1), NB, NB, 64), eye, ALU.mult))

                def outer(kind, kcol):
                    for f in range(3):
                        made(v, li, kind, f)
                        free(tt(tmp[:, f * NB:(f + 1) * NB, :], bank(kind, f).rearrange("p (b d) -> p b d", b=NB),
                                bc(kcol[:, f * NB:(f + 1) * NB].unsqueeze(2), P, NB, 64), ALU.mult), li, kind, f)

                def masked_query(src):
                    for f in range(3):
                        ins = tt(R["qm8"][:, f], bc(src[:, f, SEQ:T].unsqueeze(2), P, NB, NB),
                                 K(C_DM, NB * NB).rearrange("p (n m) -> p n m", m=NB), ALU.mult)
                        step(ins)

                diag(0)
                v.wait_ge(S("f8_exp"), li + 1)
                v.wait_ge(state_in, 48 * (li + 1))
                step(tt(S8, S8, bc(ff.unsqueeze(2), P, 3 * NB, 64), ALU.mult))
                outer("vb", R["k8"][:].rearrange("p f b -> p (f b)"))
                masked_query(proj[:, TQ:TQ + 3, :])
                sig(tt(S8, S8, tmp, ALU.add), "s8_made")
                sc8 = R["sc8"]
                ig8, lf8 = proj[0:5, 3, SEQ:T], proj[0:5, 4, SEQ:T]
                step(tt(sc8[0:5, 0:8], lf8, sc8[0:5, 24:32], ALU.add))
                step(tt(sc8[0:5, 32:40], sc8[0:5, 0:8], ig8, ALU.max))
                step(tt(sc8[0:5, 0:8], sc8[0:5, 0:8], sc8[0:5, 32:40], ALU.subtract))
                step(tt(sc8[0:5, 8:16], ig8, sc8[0:5, 32:40], ALU.subtract))
                sig(ts(sc8[0:5, 16:24], sc8[0:5, 32:40], -1.0, None, ALU.mult), "m8_rows")
                for s in range(2):
                    made(v, li, "so", s)
                    free(v.tensor_copy(R["obs"][:, s:5:2, :],
                                       bank("so", s)[0:NB, 0:64 * (3 - s)].rearrange("b (h d) -> b h d", d=64)),
                         li, "so", s)
                made(v, li, "rs")
                free(v.tensor_copy(R["e8"][:], bank("rs")[0:NB, 0:5]), li, "rs")
                made(v, li, "aw")
                free(v.tensor_copy(R["aw"][:].rearrange("p f b -> p (f b)"), bank("aw")[:, 0:48]), li, "aw")
                diag(1)
                a8, w8 = R["aw"][:, :, 0:NB], R["aw"][:, :, NB:2 * NB]
                step(tt(R["ff"][:], R["kh"][:, :, SEQ:T], w8, ALU.mult))
                step(v.tensor_copy(R["k8"][:], a8))
                step(tt(C8, C8, bc(R["k8"][:].rearrange("p f b -> p (f b)").unsqueeze(2), P, 3 * NB, 65), ALU.mult))
                outer("vc", ff)
                masked_query(R["bt"][:])
                step(tt(C8[:, :, 64], C8[:, :, 64], ff, ALU.add))
                sig(tt(C8[:, :, 0:64], C8[:, :, 0:64], tmp, ALU.add), "c8_made")
                n8, d8 = R["n8"], R["d8"]
                for s in range(2):
                    made(v, li, "co", s)
                    free(v.tensor_copy(n8[:, s:5:2, :],
                                       bank("co", s)[0:NB, 0:65 * (3 - s)].rearrange("b (h d) -> b h d", d=65)),
                         li, "co", s)
                step(stt(d8[:], n8[:, :, 64], -1.0, n8[:, :, 64], ALU.mult, ALU.max))
                step(tt(d8[:], d8[:], R["e8"][:], ALU.max))
                step(v.reciprocal(d8[:], d8[:]))
                step(tt(R["obs"][:, 5:10, :], n8[:, :, 0:64], bc(d8[:].unsqueeze(2), NB, 5, 64), ALU.mult))
                step(tt(R["sq8"][:], R["obs"][:], R["obs"][:], ALU.mult))
                sig(v.tensor_reduce(R["s10"][:], R["sq8"][:], AX, ALU.add), "obs_ms")
                v.wait_ge(S("obs_rms"), li + 1)
                sig(tt(R["obs"][:], R["obs"][:], bc(R["s10"][:].unsqueeze(2), NB, 10, 64), ALU.mult), "obs_normed")
                made(v, li, "fx")
                fx = bank("fx")[:, 0:64].rearrange("p (m b) -> p m b", b=NB)
                step(tt(R["fx"][:], fx[:, 0:5, :], bc(par(li, PR_ON, 5).unsqueeze(2), P, 5, NB), ALU.mult))
                step(tt(proj[:, TG:TG + 5, SEQ:T], proj[:, TG:TG + 5, SEQ:T], R["fx"][:], ALU.mult))
                free(v.tensor_copy(proj[:, TSQ:TSQ + 3, SEQ:T], fx[:, 5:8, :]), li, "fx")

            v.wait_ge(const_in, 64)
            for li in range(2):
                norm(2 * li)
                if li == 0:
                    p0, p1 = par(0, PR_LB, 3), par(1, PR_LB, 3)
                    step(tt(lbt[:, 2, :], p0, p1, ALU.max))
                    step(tt(lbt[:, 0, :], p0, lbt[:, 2, :], ALU.subtract))
                    sig(tt(lbt[:, 1, :], p1, lbt[:, 2, :], ALU.subtract), "lb_centred")
                    v.wait_ge(S("lb_exp"), 1)
                    step(tt(lbt[:, 3, :], lbt[:, 0, :], lbt[:, 1, :], ALU.add))
                    step(v.reciprocal(lbt[:, 3, :], lbt[:, 3, :]))
                    step(tt(lbt[:, 2, :], lbt[:, 1, :], lbt[:, 3, :], ALU.mult))
                    step(ts(lbt[:, 3, :], lbt[:, 2, :], -1.0, 1.0, ALU.mult, ALU.add))
                for n in range(3):
                    v.wait_ge(unit_done, U_IN[li] + n + 1)
                    v.tensor_copy(halves(proj[:, n, :]), part(U_IN[li] + n)).then_inc(proj_read, 1)
                with v.Fori(0, (NT - 3) // 6) as i:
                    for n in range(6):
                        u = U_IN[li] + 3 + n
                        v.wait_ge(unit_done, i * 6 + (u + 1))
                        dst = proj[:, bass.ds(i * 6 + (3 + n), 1), :].rearrange("p o (s t) -> p (o s) t", s=2)
                        v.tensor_copy(dst, part(u)).then_inc(proj_read, 1)
                window(li)
                if li:
                    split_lo(v, U_OUT[1] + 1, KD * P, lo_dve)
                hgrn(li)
                mlstm(li)
                sample(li)
                for m in range(1, KD, 2):
                    v.wait_ge(mixh_made, KD * li + m + 1)
                    tt(xnl[:, m, :], proj[:, MIXT[m], :], xnh[:, m, :].bitcast(F32), ALU.subtract).then_inc(mixl_dve, 1)
                for n in range(KD):
                    if li and n % 2 and n + 2 < KD:
                        split_lo(v, U_OUT[1] + n + 2, KD * P, lo_dve)
                    v.wait_ge(unit_done, U_OUT[li] + n + 1)
                    x = halves(xT[:, n, :])
                    tt(x, part(U_OUT[li] + n), x, ALU.add).then_inc(x_updated, 1)
                norm(2 * li + 1)
                if li == 1:
                    v.wait_ge(rt_done, 1)
                    bump(ts(halves(lg[:]), psum[0:8, 6:8, 0:H2], par(1, PR_RB, 1, 8), None, ALU.add), rt_read, v)
                    step(v.memset(rl[:], 0.0))
                    v.wait_ge(rt_done, 2)
                    step(v.tensor_copy(rl[:, 0:4, :], psum[:, 6, 0:32].rearrange("p (t e) -> p t e", e=8)))
                    step(v.tensor_copy(rl[0:8, 4, :], psum[0:8, 6, 32:40]))
                    step(v.tensor_reduce(rm[:], rl[:], AX, ALU.max))
                    sig(tt(re[:], rl[:], bc(rm[:].unsqueeze(2), P, 5, 8), ALU.subtract), "rt_centred")
                    for t in range(5):
                        other = bc(rl[:, t, :].unsqueeze(1), P, 8, 8)
                        mine = bc(rl[:, t, :].unsqueeze(2), P, 8, 8)
                        step(tt(c1[:, 8 * t:8 * t + 8, :], other, mine, ALU.is_gt))
                        step(tt(c2[:, 8 * t:8 * t + 8, :], other, mine, ALU.is_equal))
                        step(tt(c2[:, 8 * t:8 * t + 8, :], c2[:, 8 * t:8 * t + 8, :],
                                K(C_LT, 64).rearrange("p (e j) -> p e j", j=8), ALU.mult))
                    step(tt(c1[:], c1[:], c2[:], ALU.add))
                    step(v.tensor_reduce(rk[:], c1[:], AX, ALU.add))
                    step(ts(rk[:], rk[:], TOP_K - 0.5, None, ALU.is_lt))
                    bump(tt(rsel[:], rk[:].rearrange("p (t e) -> p t e", e=8), bc(K(C_VM, 5).unsqueeze(2), P, 5, 8), ALU.mult),
                         rt_read, v)
                    v.wait_ge(S("rt_exp"), 1)
                    re2 = re[:].rearrange("p t e -> p (t e)")
                    step(tt(re2, re2, rk[:], ALU.mult))
                    step(v.tensor_reduce(rm[:], re[:], AX, ALU.add))
                    step(v.reciprocal(rm[:], rm[:]))
                    step(tt(re[:], re[:], bc(rm[:].unsqueeze(2), P, 5, 8), ALU.mult))
                    g8 = ghl[:, :, 0:8, :]
                    step(ts(ghl[:, :, SPARE, :], re[:, :, 0:2], 0.0, None, ALU.mult))
                    step(v.tensor_copy(g8[:, :, :, 0], re[:]))
                    bump(tt(g8[:, :, :, 1], re[:], g8[:, :, :, 0].bitcast(F32), ALU.subtract), rt_read, v)
                    v.wait_ge(rt_done, 3)
                    step(v.memset(pos[:], 0.0))
                    step(tt(pos[:, :, 0:8], psum[:, 6, 0:40].rearrange("p (t e) -> p t e", e=8), rsel[:], ALU.mult))
                    step(ts(pos[:], pos[:], -1.0, None, ALU.add))
                    step(v.tensor_copy(tot[:], psum[:, 7, 0:8]))
                    step(v.tensor_reduce(rm[:, 0:1], tot[:], AX, ALU.max))
                    sig(ts(flag[:], rm[:, 0:1], SLOTS + 0.5, None, ALU.is_gt), "flag_made")
                else:
                    with v.Fori(0, NEX[0]) as e:
                        def hidden_lo(j):
                            v.wait_ge(hh_made, e * KF + (j + 1))
                            tt(hl[:, j, :], h32[:, j % 2, :], hh[:, j, :].bitcast(F32), ALU.subtract).then_inc(hl_made, 1)

                        for j in range(KF):
                            v.wait_ge(unit_done, e * UPE + (U_FF[0] + 2 * j + 2))
                            v.wait_ge(gate_read, e * KF + (j + 1))
                            if j >= 2:
                                v.wait_ge(hl_made, e * KF + (j - 1))
                            tt(halves(h32[:, j % 2, :]), part(U_FF[0] + 2 * j + 1), halves(sg[:, j % 2, :]), ALU.mult
                               ).then_inc(up_read, 1)
                            if j:
                                hidden_lo(j - 1)
                        hidden_lo(KF - 1)
                        v.wait_ge(hl_made, e * KF + KF)
                        for m in range(KD):
                            u = U_FF[0] + 2 * KF + m
                            v.wait_ge(unit_done, e * UPE + (u + 1))
                            x = halves(xT[:, m, :])
                            tt(x, part(u), x, ALU.add).then_inc(x_updated, 1)
                        v.wait_ge(x_updated, e * KD + (X_OUT[0] + KD))

            def select(e):
                v.tensor_copy(ge[:].unsqueeze(2), ghl[:, :, bass.ds(e, 1), :].bitcast(F32))
                tt(sel[:], bc(K(C_IOTA, WIDE).unsqueeze(1), P, 5, WIDE),
                   bc(pos[:, :, bass.ds(e, 1)], P, 5, WIDE), ALU.is_equal).then_inc(sel_made, 1)

            def weighted_lo(f, q):
                rows, st, c0, b = y_piece(q)
                v.wait_ge(yh_made, f * 4 + (q + 1))
                stt(yl[0:rows, st, c0:c0 + 512], psum[0:rows, b, :], gslot[0:rows, st:st + 1],
                    yh[0:rows, st, c0:c0 + 512].bitcast(F32), ALU.mult, ALU.subtract).then_inc(yl_made, 1)

            def add(f, m):
                v.wait_ge(scattered, f * KD + (m + 1))
                x = halves(xT[:, m, :])
                tt(x, scatter_bank(m), x, ALU.add).then_inc(x_updated, 1)

            def experts(c):
                select(0)
                for m in range(KD):
                    v.memset(yf[:, m, :], 0.0).then_inc(yf_made, 1)
                for st in range(2):
                    ts(selT[:, st, :], xT[:, st, :], 0.0, None, ALU.mult).then_inc(selT_made, 1)
                v.memset(gslot[:], 0.0).then_inc(gsl, 1)
                with v.Fori(0, 8) as e:
                    p_, f_ = c * 8 + e, c * 9 + e

                    def mine(n):
                        if n < UPE and n not in WHOLE:
                            expert_lo(v, n, p_, lo_dve, lo_cols(n)[0])

                    def hidden_lo(j):
                        v.wait_ge(hh_made, p_ * KF + (G_FF[1] + j + 1))
                        tt(ehl[:, j, SLOTS:2 * SLOTS], e32[:, j % 2, :], ehl[:, j, 0:SLOTS].bitcast(F32), ALU.subtract
                           ).then_inc(hl_made, 1)

                    def hidden(j):
                        v.wait_ge(S("silu_made"), p_ * KF + (j + 1))
                        v.wait_ge(up_read, p_ * KF + (G_FF[1] + j + 1))
                        if j >= 2:
                            v.wait_ge(hl_made, p_ * KF + (G_FF[1] + j - 1))
                        tt(e32[:, j % 2, :], u32[:, j % 2, :], esg[:, j % 2, :], ALU.mult).then_inc(S("e32_made"), 1)

                    for n in range(3):
                        mine(n)
                    for j in range(KF):
                        v.wait_ge(unit_done, p_ * UPE + (U_FF[1] + 2 * j + 1))
                        v.tensor_reduce(g32[:, j % 2, :], two(2 * j), AX, ALU.add).then_inc(gate_read, 1)
                        if j < KF - 1:
                            mine(2 * j + 3)
                        v.wait_ge(unit_done, p_ * UPE + (U_FF[1] + 2 * j + 2))
                        if j >= 2:
                            v.wait_ge(S("e32_made"), p_ * KF + (j - 1))
                        v.tensor_reduce(u32[:, j % 2, :], two(2 * j + 1), AX, ALU.add).then_inc(up_read, 1)
                        if j < KF - 1:
                            mine(2 * j + 4)
                        if 1 <= j < KF - 1:
                            hidden(j - 1)
                        if 2 <= j < KF - 1:
                            hidden_lo(j - 2)
                        if 2 <= j < 6:
                            weighted_lo(f_, j - 2)
                    add(f_, 0)
                    hidden(KF - 2)
                    add(f_, 1)
                    hidden_lo(KF - 3)
                    hidden(KF - 1)
                    add(f_, 2)
                    hidden_lo(KF - 2)
                    add(f_, 3)
                    hidden_lo(KF - 1)
                    for m in range(4, KD):
                        add(f_, m)
                    mine(2 * KF + 1)
                    for st in range(2):
                        rows = (P, SLOTS - P)[st]
                        v.wait_ge(turned_sel, p_ * 3 + (st + 1))
                        v.tensor_copy(selT[0:rows, st, 0:SEQ], psum[0:rows, (1, 6)[st], :])
                        v.tensor_copy(selT[0:rows, st, SEQ:T], psum[0:rows, (3, 7)[st], 0:NB]).then_inc(selT_made, 1)
                    v.wait_ge(turned_sel, p_ * 3 + 3)
                    v.tensor_copy(gs2[:, 0, :], psum[:, 5, 0:2])
                    v.tensor_copy(gs2[0:SLOTS - P, 1, :], psum[0:SLOTS - P, 5, 2:4]).then_inc(S("gs2_made"), 1)
                    v.wait_ge(S("gs2_made"), p_ + 1)
                    tt(gslot[:, 0:1], gs2[:, 0, 0:1], gs2[:, 0, 1:2], ALU.add)
                    tt(gslot[0:SLOTS - P, 1:2], gs2[0:SLOTS - P, 1, 0:1], gs2[0:SLOTS - P, 1, 1:2], ALU.add).then_inc(gsl, 1)
                    select(e + 1)
                    for m in range(KD):
                        n = 2 * KF + m
                        v.wait_ge(unit_done, p_ * UPE + (U_FF[1] + n + 1))
                        v.tensor_reduce(yf[:, m, :], two(n), AX, ALU.add).then_inc(yf_made, 1)
                        mine(n + 3)
                for q in range(4):
                    weighted_lo(c * 9 + 8, q)
                for m in range(KD):
                    add(c * 9 + 8, m)
                v.wait_ge(x_updated, c * 9 * KD + (X_OUT[1] + 9 * KD))

            v.wait_ge(S("flag_made"), 1)
            v.wait_ge(xt_made, 20)
            experts(0)
            with v.If(v.value_load(flag[0:1, 0:1], min_val=0, max_val=1) > 0):
                with v.Fori(0, NPASS - 1) as k:
                    ts(pos[:], pos[:], -float(SLOTS), None, ALU.add).then_inc(S("pos_moved"), 1)
                    v.wait_ge(S("pos_moved"), k + 1)
                    experts(k + 1)
            norm(4)


IN_SHAPES = {
    "x": [P, KD, T], "cst": [P, C_END], "lvm": [P, LVL + 1, P], "prm": [P, 2, PR_END], "bd": [P, 2, 2, 3, P],
    "cbuf": [P, 2, 3, CONV - 1, NB], "w_in": [2, NT, P, KD * P], "w_out": [2, KD, P, KD * P],
    "ffn_gu": [2, 2 * KF, P, KD * P], "ffn_dn": [2, KD, P, KF * P],
    "moe_gu": [8, 2 * KF, P, KD * P], "moe_dn": [8, KD, P, KF * P], "rw": [P, KD * 8],
    "ck": [2, P, 3, NB, 256], "hgrn_in": [2, P, 3 * NB * 64], "mlstm_in": [2, P, 3 * NB * 65], "m_in": [2, 5, NB],
    "cache0": [2, NB, WB[0], 2, P], "cache1": [2, NB, WB[1], 2, P], "cache2": [2, NB, WB[2], 2, P],
}
OUT_SHAPES = {
    "y": [P, KD, T], "hgrn_p": [2, P, 3, 64], "hgrn_s": [2, P, 3 * NB * 64], "mlstm_p": [2, P, 3, 65],
    "mlstm_s": [2, P, 3 * NB * 65], "m_p": [2, 5, 1], "m_s": [2, 5, NB], "mu_out": [2, P, 3, 3], "conv_s": [2, P, 3, 3, NB],
    "kv_p": [2, P, 6, SEQ], "cache0_s": [2, NB, WB[0], 2, P], "cache1_s": [2, NB, WB[1], 2, P],
    "cache2_s": [2, NB, WB[2], 2, P],
}


def constants(np):
    c = np.zeros((P, C_END), np.float32)
    n = np.arange(P)
    c[:, C_ID:C_ID + P] = np.eye(P)
    c[:, C_ONE:C_ONE + P] = 1.0
    q, k = n[:, None], n[None, :]
    c[:, C_NEGC:C_NEGC + P] = np.where(k >= q, 0.0, NEG)
    causal = np.where(k <= q, 0.0, NEG)
    c[:, C_NEG0:C_NEG0 + 256] = np.concatenate([np.full((P, P), NEG), causal], 1)
    c[:, C_NEG1:C_NEG1 + 256] = np.concatenate([np.where(k >= q, 0.0, NEG), causal], 1)
    c[:, C_NEGT:C_NEGT + P] = causal
    c[:, C_NEGR:C_NEGR + P] = np.where((q % 4 == k % 4) & (k <= q), 0.0, NEG)
    for f in range(3):
        for h in range(2):
            if 2 * f + h < 5:
                c[2 * f + h, C_HP + f * P + 64 * h:C_HP + f * P + 64 * h + 64] = 1.0
    c[:, C_DM:C_DM + 2 * NB * NB] = np.tile(np.eye(NB).reshape(1, -1), (P, 2))
    for h in range(2):
        c[h, C_S2 + 64 * h:C_S2 + 64 * h + 64] = 1.0
    c[:, C_RST:C_RST + SEQ] = (np.arange(SEQ) % CH != 0)[None, :]
    c[:, C_EPS] = EPS
    c[:, C_VM:C_VM + 5] = n[:, None] + P * np.arange(5)[None, :] < T
    c[:, C_TRI:C_TRI + P] = q <= k
    c[:, C_IOTA:C_IOTA + WIDE] = np.arange(WIDE)[None, :]
    e = np.arange(8)
    c[:, C_LT:C_LT + 64] = (e[None, :] < e[:, None]).reshape(1, -1)
    x = n[:, None] ^ n[None, :]
    m = np.zeros((P, LVL + 1, P), np.int32)
    for l in range(LVL):
        half = CH >> (l + 1)
        m[:, l, :] = (x >= half) & (x < 2 * half) & (n[:, None] < n[None, :])
    m[:, LVL, :] = x == 0
    return c, m


def kernel(**inputs):
    import numpy as np
    import concourse.bacc as bacc
    from concourse.bass_utils import run_bass_kernel_spmd

    v = {k: np.asarray(x) for k, x in inputs.items()}
    f32 = np.float32

    def fm(x):
        y = x.reshape(x.shape[:-1] + (-1, P))
        return np.moveaxis(y, -1, 0)

    def pad(x, n):
        return np.concatenate([x, np.zeros(x.shape[:-1] + (n - x.shape[-1],), f32)], -1)

    def ktile(w):
        k, m = w.shape
        return w.reshape(k // P, P, m // P, P).transpose(2, 1, 0, 3).reshape(m // P, P, k)

    d = {}
    d["cst"], d["lvm"] = constants(np)
    x = np.concatenate([v["x_prompt"][0], v["x_sample"][:, 0]], 0)
    d["x"] = x.T.reshape(KD, P, T).transpose(1, 0, 2)
    prm = np.zeros((P, 2, PR_END), f32)
    bd = np.zeros((P, 2, 2, 3, P), f32)
    w_in = np.zeros((2, NT, P, KD * P), f32)
    z64 = np.zeros((D, 64), f32)
    for li in range(2):
        prm[:, li, PR_G1:PR_G1 + KD] = fm(v["norm1_g"][li])
        prm[:, li, PR_G2:PR_G2 + KD] = fm(v["norm2_g"][li])
        prm[:, li, PR_GF:PR_GF + KD] = fm(v["final_norm_g"])
        prm[:, li, PR_ON:PR_ON + 5] = fm(np.concatenate([v["hgrn_onorm_g"][li], v["mlstm_onorm_g"][li]]))
        cw = fm(pad(v["mlstm_conv_w"][li], 384))
        prm[:, li, PR_CW:PR_CW + 12] = cw.transpose(0, 2, 1).reshape(P, 12)
        prm[:, li, PR_CB:PR_CB + 3] = fm(pad(v["mlstm_conv_b"][li], 384))
        prm[:, li, PR_LB:PR_LB + 3] = fm(pad(v["hgrn_lb_param"][li], 384))
        prm[64:69, li, PR_IB] = v["mlstm_ig_b"][li]
        prm[96:101, li, PR_FB] = v["mlstm_fg_b"][li]
        prm[0:8, li, PR_RB] = v["moe_router_b"][0]
        for s, name in enumerate(("mlstm_wq", "mlstm_wk")):
            for h in range(5):
                r = 64 * (h % 2)
                bd[r:r + 64, li, s, h // 2, r:r + 64] = v[name][li, h]
        w = v["w_in"][li]
        hq, hf, hi, hg, mu, mv, mo = (w[:, 320 * n:320 * (n + 1)] for n in range(7))
        gates = np.zeros((D, 64), f32)
        gates[:, 0:5] = w[:, 2240:2245]
        gates[:, 32:37] = w[:, 2245:2250]
        cols = np.concatenate([hq, gates, hf, hi[:, 256:320], hi[:, 0:256], hg, mo, mu, mv[:, 256:320], mv[:, 0:256],
                               w[:, 2250:3402]], 1)
        w_in[li] = ktile(cols)
    d["prm"], d["bd"], d["w_in"] = prm, bd, w_in
    cb = fm(pad(v["state_mlstm_conv"], 384))
    d["cbuf"] = cb.transpose(0, 1, 4, 3, 2)
    d["w_out"] = np.stack([ktile(v["w_out"][li]) for li in range(2)])

    def gu(wg, wu):
        g, u = ktile(wg), ktile(wu)
        return np.stack([g, u], 1).reshape(2 * KF, P, KD * P)

    d["ffn_gu"] = np.stack([gu(v["ffn_w_gate"][0][:, e * EFF:(e + 1) * EFF], v["ffn_w_up"][0][:, e * EFF:(e + 1) * EFF])
                            for e in range(2)])
    d["ffn_dn"] = np.stack([ktile(v["ffn_w_down"][0][e * EFF:(e + 1) * EFF]) for e in range(2)])
    d["moe_gu"] = np.stack([gu(v["moe_w_gate"][0, e], v["moe_w_up"][0, e]) for e in range(8)])
    d["moe_dn"] = np.stack([ktile(v["moe_w_down"][0, e]) for e in range(8)])
    d["rw"] = v["moe_router_w"][0].reshape(KD, P, 8).transpose(1, 0, 2).reshape(P, KD * 8)
    ck = np.zeros((2, P, 3, NB, 256), f32)
    for g, (name, dil) in enumerate((("cache_swa_w128", 1), ("cache_swa_w512", 4), ("cache_swa_w2048", 16))):
        c = v[name].reshape(2, NB, WB[g], 256)
        d[f"cache{g}"] = c.reshape(2, NB, WB[g], 2, P)
        ck[:, 0:ROWS_G[g], g] = c[:, :, ::dil].transpose(0, 2, 1, 3)
    d["ck"] = ck

    def heads_in(s):
        s = np.concatenate([s, np.zeros_like(s[:, :, 0:1])], 2)
        w = s.shape[-1]
        return s.reshape(2, NB, 3, 2, 64, w).transpose(0, 3, 4, 2, 1, 5).reshape(2, P, 3 * NB * w)

    d["hgrn_in"] = heads_in(v["state_hgrn"])
    d["mlstm_in"] = heads_in(np.concatenate([v["state_mlstm_C"], v["state_mlstm_n"][..., None]], -1))
    d["m_in"] = v["state_mlstm_m"].transpose(0, 2, 1)

    nc = bacc.Bacc("TRN2", target_bir_lowering=False, num_devices=1)
    arrays, args = {}, {}
    for name, shape in IN_SHAPES.items():
        arr = np.ascontiguousarray(d[name])
        assert list(arr.shape) == shape, (name, arr.shape, shape)
        arrays["in_" + name] = arr
        args[name] = nc.dram_tensor("in_" + name, arr.shape, mybir.dt.from_np(arr.dtype), kind="ExternalInput").ap()
    for name, shape in OUT_SHAPES.items():
        args[name] = nc.dram_tensor("out_" + name, tuple(shape), F32, kind="ExternalOutput").ap()
    program(nc, args)
    res = run_bass_kernel_spmd(nc, [arrays], core_ids=[0]).results[0]
    o = {name: np.asarray(res["out_" + name]) for name in OUT_SHAPES}

    y = o["y"].transpose(2, 1, 0).reshape(T, D)

    def heads_out(s, n, w):
        s = s.reshape(2, 2, 64, 3, n, w).transpose(0, 4, 3, 1, 2, 5).reshape(2, n, 6, 64, w)
        return np.ascontiguousarray(s[:, :, 0:5])

    C_p, C_s = heads_out(o["mlstm_p"], 1, 65), heads_out(o["mlstm_s"], NB, 65)
    mu = o["mu_out"].transpose(0, 3, 2, 1).reshape(2, 3, 384)[:, :, 0:320]
    conv_s = o["conv_s"].transpose(0, 4, 3, 2, 1).reshape(2, NB, 3, 384)[..., 0:320]
    kv = o["kv_p"].reshape(2, P, 2, 3, SEQ).transpose(0, 3, 4, 2, 1)
    out = [y[None, 0:SEQ], y[SEQ:, None], heads_out(o["hgrn_p"], 1, 64), heads_out(o["hgrn_s"], NB, 64),
           C_p[..., 0:64], C_s[..., 0:64], C_p[..., 64], C_s[..., 64],
           o["m_p"].transpose(0, 2, 1), o["m_s"].transpose(0, 2, 1), mu[:, None], conv_s]
    for g, w in enumerate((128, 512, 512)):
        out.append(kv[:, g, SEQ - w:].reshape(2, 1, w, 2, 2, 64))
        out.append(o[f"cache{g}_s"].reshape(2, NB, WB[g], 2, 2, 64))
    return tuple(np.ascontiguousarray(x) for x in out)
```
